# Optimizing a Trainium2 kernel written in Bass

```python
import jax, jax.numpy as jnp
from jax import lax
import numpy as np

D_MODEL = 1024
BATCH = 1
SEQ = 1024
DEPTH = 1

GRID_W = 64
CTX_LEN = 256
MLA_HEADS = 8
QK_NOPE = 64
QK_ROPE = 32
V_HEAD = 64
Q_LORA = 384
KV_LORA = 256
Q_BLOCK = 128
ROPE_THETA = 10000.0
MLA_SCALE = (QK_NOPE + QK_ROPE) ** -0.5
M_HEADS = 4
M_DQK = 64
M_DV = 128
CHUNK = 128
N_EXPERTS = 32
TOP_K = 4
D_FF = 1024
SWIGLU_LIMIT = 7.0
SWIGLU_ALPHA = 1.702
MOE_BLOCK = 128
EPS = 1e-6

MLA_WIDTH = MLA_HEADS * V_HEAD
MLSTM_WIDTH = M_HEADS * M_DV
MIX_WIDTH = MLA_WIDTH + MLSTM_WIDTH
IN_SPLITS = (Q_LORA, KV_LORA, QK_ROPE, M_HEADS * M_DQK, M_HEADS * M_DQK, MLSTM_WIDTH, MLSTM_WIDTH, 4 * M_HEADS)
IN_WIDTH = sum(IN_SPLITS)

kernel_name = "hybrid_mla_mlstm_moe_dit_block"

def rms_norm(x, g):
    xf = x.astype(jnp.float32)
    y = xf * lax.rsqrt(jnp.mean(xf * xf, axis=-1, keepdims=True) + EPS)
    return (y * g.astype(jnp.float32)).astype(x.dtype)

def modulate(h, shift, scale):
    return h * (1 + scale) + shift

def split_cols(a, sizes):
    out, start = [], 0
    for s in sizes:
        out.append(a[..., start:start + s])
        start += s
    return out

def rope_tables(n_tokens):
    rows = n_tokens // GRID_W
    row = jnp.repeat(jnp.arange(rows, dtype=jnp.float32), GRID_W)
    col = jnp.tile(jnp.arange(GRID_W, dtype=jnp.float32), rows)
    pairs = QK_ROPE // 4
    inv = ROPE_THETA ** (-jnp.arange(pairs, dtype=jnp.float32) / pairs)
    ang = jnp.concatenate([row[:, None] * inv, col[:, None] * inv], axis=-1)
    return jnp.cos(ang), jnp.sin(ang)

def apply_rope(x, cos, sin):
    half = x.shape[-1] // 2
    xf = x.astype(jnp.float32)
    x1, x2 = xf[..., :half], xf[..., half:]
    return jnp.concatenate([x1 * cos - x2 * sin, x1 * sin + x2 * cos], axis=-1).astype(x.dtype)

def mla_q(cq, q_norm_g, w_uq, cos, sin):
    B, S = cq.shape[:2]
    q = (rms_norm(cq, q_norm_g) @ w_uq).reshape(B, S, MLA_HEADS, QK_NOPE + QK_ROPE)
    q_nope, q_rope = q[..., :QK_NOPE], q[..., QK_NOPE:]
    if cos is not None:
        q_rope = apply_rope(q_rope, cos[:, None, :], sin[:, None, :])
    return q_nope, q_rope

def mla_kv(ckv, k_rope, kv_norm_g, w_ukv, cos, sin):
    B, S = ckv.shape[:2]
    kv = (rms_norm(ckv, kv_norm_g) @ w_ukv).reshape(B, S, MLA_HEADS, QK_NOPE + V_HEAD)
    k_nope, v = kv[..., :QK_NOPE], kv[..., QK_NOPE:]
    if cos is not None:
        k_rope = apply_rope(k_rope, cos, sin)
    return k_nope, k_rope, v

def attend(q_nope, q_rope, k_nope, k_rope, v):
    s = jnp.einsum('bqhd,bkhd->bhqk', q_nope, k_nope) + jnp.einsum('bqhr,bkr->bhqk', q_rope, k_rope)
    p = jax.nn.softmax(s.astype(jnp.float32) * MLA_SCALE, axis=-1).astype(v.dtype)
    return jnp.einsum('bhqk,bkhd->bqhd', p, v)

def blocked_attention(q_nope, q_rope, k_nope, k_rope, v):
    B, S, H, _ = q_nope.shape
    nb = S // Q_BLOCK
    blk = lambda a: jnp.moveaxis(a.reshape(B, nb, Q_BLOCK, *a.shape[2:]), 1, 0)
    out = lax.map(lambda qs: attend(qs[0], qs[1], k_nope, k_rope, v), (blk(q_nope), blk(q_rope)))
    return jnp.moveaxis(out, 0, 1).reshape(B, S, H * V_HEAD)

def mlstm_heads(mq, mk, mv, mg, b_gates):
    B, S = mq.shape[:2]
    to_h = lambda a, d: jnp.moveaxis(a.astype(jnp.float32).reshape(B, S, M_HEADS, d), 1, 2)
    q = to_h(mq, M_DQK) * M_DQK ** -0.5
    k = to_h(mk, M_DQK)
    v = to_h(mv, M_DV)
    g = (mg.astype(jnp.float32) + b_gates.astype(jnp.float32)).reshape(B, S, 4, M_HEADS)
    g = jnp.moveaxis(g, 1, 3)
    return q, k, v, g

def mlstm_chunked(q, k, v, log_i, log_f, state):
    B, NH, S, _ = q.shape
    nc = S // CHUNK
    chunks = lambda a: jnp.moveaxis(a.reshape(B, NH, nc, CHUNK, *a.shape[3:]), 2, 0)
    tril = jnp.tril(jnp.ones((CHUNK, CHUNK), dtype=bool))

    def step(carry, inp):
        C, n, m = carry
        qc, kc, vc, li, lf = inp
        b = jnp.cumsum(lf, axis=-1)
        d_intra = jnp.where(tril, b[..., :, None] - b[..., None, :] + li[..., None, :], -jnp.inf)
        d_inter = b + m[..., None]
        m_t = jnp.maximum(d_inter, d_intra.max(-1))
        s = jnp.einsum('bhtd,bhsd->bhts', qc, kc) * jnp.exp(d_intra - m_t[..., None])
        w_inter = jnp.exp(d_inter - m_t)
        num = jnp.einsum('bhts,bhsv->bhtv', s, vc) + w_inter[..., None] * jnp.einsum('bhvd,bhtd->bhtv', C, qc)
        den = s.sum(-1) + w_inter * jnp.einsum('bhd,bhtd->bht', n, qc)
        h = num / jnp.maximum(jnp.abs(den), jnp.exp(-m_t))[..., None]
        b_last = b[..., -1]
        w_src = b_last[..., None] - b + li
        m_new = jnp.maximum(b_last + m, w_src.max(-1))
        decay = jnp.exp(b_last + m - m_new)
        w_src = jnp.exp(w_src - m_new[..., None])
        C_new = decay[..., None, None] * C + jnp.einsum('bhs,bhsv,bhsd->bhvd', w_src, vc, kc)
        n_new = decay[..., None] * n + jnp.einsum('bhs,bhsd->bhd', w_src, kc)
        return (C_new, n_new, m_new), h

    state, h = lax.scan(step, state, (chunks(q), chunks(k), chunks(v), chunks(log_i), chunks(log_f)))
    return state, jnp.moveaxis(h, 0, 2).reshape(B, NH, S, -1)

def rev(a, d):
    return jnp.flip(a, axis=2) if d == 1 else a

def mlstm_bidirectional(lat, ctxh):
    q, k, v, g = lat
    qc, kc, vc, gc = ctxh
    B = q.shape[0]
    h_lat, h_ctx = 0.0, 0.0
    for d in range(2):
        state0 = (jnp.zeros((B, M_HEADS, M_DV, M_DQK), jnp.float32),
                  jnp.zeros((B, M_HEADS, M_DQK), jnp.float32),
                  jnp.zeros((B, M_HEADS), jnp.float32))
        i_c, f_c = gc[:, 2 * d], jax.nn.log_sigmoid(gc[:, 2 * d + 1])
        i_x, f_x = g[:, 2 * d], jax.nn.log_sigmoid(g[:, 2 * d + 1])
        state_c, hc = mlstm_chunked(rev(qc, d), rev(kc, d), rev(vc, d), rev(i_c, d), rev(f_c, d), state0)
        _, hx = mlstm_chunked(rev(q, d), rev(k, d), rev(v, d), rev(i_x, d), rev(f_x, d), state_c)
        h_lat = h_lat + rev(hx, d)
        h_ctx = h_ctx + rev(hc, d)
    return h_lat, h_ctx

def mlstm_out(h, o, m_norm_g):
    B, NH, S, DV = h.shape
    h = h * lax.rsqrt(jnp.mean(h * h, axis=-1, keepdims=True) + EPS)
    h = jnp.moveaxis(h, 1, 2).reshape(B, S, NH * DV) * m_norm_g.astype(jnp.float32)
    return (h * jax.nn.sigmoid(o.astype(jnp.float32))).astype(o.dtype)

def token_mixer(hx, hc, w_in, b_gates, q_norm_g, w_uq, kv_norm_g, w_ukv, m_norm_g, w_out, cos, sin, want_ctx):
    B, S = hx.shape[:2]
    px = split_cols(hx @ w_in, IN_SPLITS)
    pc = split_cols(hc @ w_in, IN_SPLITS)
    qn, qr = mla_q(px[0], q_norm_g, w_uq, cos, sin)
    kn, kr, v = mla_kv(px[1], px[2], kv_norm_g, w_ukv, cos, sin)
    kn_c, kr_c, v_c = mla_kv(pc[1], pc[2], kv_norm_g, w_ukv, None, None)
    attn_x = blocked_attention(qn, qr, jnp.concatenate([kn_c, kn], axis=1),
                               jnp.concatenate([kr_c, kr], axis=1), jnp.concatenate([v_c, v], axis=1))
    lat = mlstm_heads(px[3], px[4], px[5], px[7], b_gates)
    ctxh = mlstm_heads(pc[3], pc[4], pc[5], pc[7], b_gates)
    h_lat, h_ctx = mlstm_bidirectional(lat, ctxh)
    out_x = jnp.concatenate([attn_x, mlstm_out(h_lat, px[6], m_norm_g)], axis=-1) @ w_out
    out_c = None
    if want_ctx:
        qn_c, qr_c = mla_q(pc[0], q_norm_g, w_uq, None, None)
        attn_c = attend(qn_c, qr_c, kn_c, kr_c, v_c).reshape(B, hc.shape[1], MLA_WIDTH)
        out_c = jnp.concatenate([attn_c, mlstm_out(h_ctx, pc[6], m_norm_g)], axis=-1) @ w_out
    return out_x, out_c

def routed_ffn(h, router_w, router_b, w_gu, b_gu, w_down, b_down):
    shp = h.shape
    t = h.reshape(-1, shp[-1])
    T = t.shape[0]
    TK = T * TOP_K
    logits = (t @ router_w + router_b).astype(jnp.float32)
    top_logit, top_idx = lax.top_k(logits, TOP_K)
    gates = jax.nn.softmax(top_logit, axis=-1)
    flat_e = top_idx.reshape(-1)
    order = jnp.argsort(flat_e)
    sorted_e = flat_e[order]
    counts = jnp.bincount(flat_e, length=N_EXPERTS)
    padded = (counts + MOE_BLOCK - 1) // MOE_BLOCK * MOE_BLOCK
    pad_end = jnp.cumsum(padded)
    rank = jnp.arange(TK) - (jnp.cumsum(counts) - counts)[sorted_e]
    dest = ((pad_end - padded)[sorted_e] + rank).astype(jnp.int32)
    n_blocks = -(-TK // MOE_BLOCK) + N_EXPERTS
    rows_tok = jnp.zeros(n_blocks * MOE_BLOCK, jnp.int32).at[dest].set((order // TOP_K).astype(jnp.int32))
    block_e = jnp.minimum(jnp.searchsorted(pad_end, jnp.arange(n_blocks) * MOE_BLOCK, side='right'), N_EXPERTS - 1)
    x_blocks = t[rows_tok].reshape(n_blocks, MOE_BLOCK, shp[-1])

    def expert_block(args):
        xb, e = args
        gu = xb @ w_gu[e] + b_gu[e]
        glu = jnp.minimum(gu[:, :D_FF], SWIGLU_LIMIT)
        lin = jnp.clip(gu[:, D_FF:], -SWIGLU_LIMIT, SWIGLU_LIMIT)
        return (glu * jax.nn.sigmoid(SWIGLU_ALPHA * glu) * (lin + 1)) @ w_down[e] + b_down[e]

    y_rows = lax.map(expert_block, (x_blocks, block_e)).reshape(n_blocks * MOE_BLOCK, shp[-1])
    slot = jnp.zeros(TK, jnp.int32).at[order].set(dest)
    y = jnp.einsum('tkd,tk->td', y_rows[slot].reshape(T, TOP_K, shp[-1]), gates.astype(h.dtype))
    return y.reshape(shp)

def setup_inputs(seed: int = 0) -> dict:
    key = jax.random.key(seed)
    ks = jax.random.split(key, 24)
    L, D = DEPTH, D_MODEL
    nrm = lambda k, shape, scale: jax.random.normal(k, shape, jnp.float32) * scale
    gain = lambda k, shape: 1.0 + nrm(k, shape, 0.05)
    b_gates = (nrm(ks[9], (L, 4, M_HEADS), 0.3) + jnp.array([0.0, 3.0, 0.0, 3.0], jnp.float32)[None, :, None]).reshape(L, 4 * M_HEADS)
    return {
        "x": nrm(ks[0], (BATCH, SEQ, D), 1.0),
        "c": nrm(ks[1], (BATCH, D), 1.0),
        "ctx": nrm(ks[2], (BATCH, CTX_LEN, D), 1.0),
        "c_ctx": nrm(ks[3], (D,), 1.0),
        "w_mod": nrm(ks[4], (L, D, 6 * D), D ** -0.5),
        "b_mod": nrm(ks[5], (L, 6 * D), 0.01),
        "norm1_g": gain(ks[6], (L, D)),
        "w_in": nrm(ks[7], (L, D, IN_WIDTH), D ** -0.5),
        "b_gates": b_gates,
        "q_norm_g": gain(ks[8], (L, Q_LORA)),
        "w_uq": nrm(ks[10], (L, Q_LORA, MLA_HEADS * (QK_NOPE + QK_ROPE)), Q_LORA ** -0.5),
        "kv_norm_g": gain(ks[11], (L, KV_LORA)),
        "w_ukv": nrm(ks[12], (L, KV_LORA, MLA_HEADS * (QK_NOPE + V_HEAD)), KV_LORA ** -0.5),
        "m_norm_g": gain(ks[13], (L, MLSTM_WIDTH)),
        "w_out": nrm(ks[14], (L, MIX_WIDTH, D), MIX_WIDTH ** -0.5),
        "norm2_g": gain(ks[15], (L, D)),
        "router_w": nrm(ks[16], (L, D, N_EXPERTS), D ** -0.5),
        "router_b": nrm(ks[17], (L, N_EXPERTS), 0.01),
        "w_gu": nrm(ks[18], (L, N_EXPERTS, D, 2 * D_FF), D ** -0.5),
        "b_gu": nrm(ks[19], (L, N_EXPERTS, 2 * D_FF), 0.01),
        "w_down": nrm(ks[20], (L, N_EXPERTS, D_FF, D), D_FF ** -0.5),
        "b_down": nrm(ks[21], (L, N_EXPERTS, D), 0.01),
        "final_norm_g": gain(ks[22], (D,)),
    }

def reference(x, c, ctx, c_ctx, w_mod, b_mod, norm1_g, w_in, b_gates, q_norm_g, w_uq, kv_norm_g, w_ukv,
              m_norm_g, w_out, norm2_g, router_w, router_b, w_gu, b_gu, w_down, b_down, final_norm_g):
    cos, sin = rope_tables(x.shape[1])
    for l in range(DEPTH):
        want_ctx = l < DEPTH - 1
        mod_x = (jax.nn.silu(c) @ w_mod[l] + b_mod[l])[:, None, :]
        mod_c = (jax.nn.silu(c_ctx) @ w_mod[l] + b_mod[l])[None, None, :]
        sh1, sc1, g1, sh2, sc2, g2 = jnp.split(mod_x, 6, axis=-1)
        csh1, csc1, cg1, csh2, csc2, cg2 = jnp.split(mod_c, 6, axis=-1)
        hx = modulate(rms_norm(x, norm1_g[l]), sh1, sc1)
        hc = modulate(rms_norm(ctx, norm1_g[l]), csh1, csc1)
        mix_x, mix_c = token_mixer(hx, hc, w_in[l], b_gates[l], q_norm_g[l], w_uq[l], kv_norm_g[l], w_ukv[l],
                                   m_norm_g[l], w_out[l], cos, sin, want_ctx)
        x = x + g1 * mix_x
        x = x + g2 * routed_ffn(modulate(rms_norm(x, norm2_g[l]), sh2, sc2),
                                router_w[l], router_b[l], w_gu[l], b_gu[l], w_down[l], b_down[l])
        if want_ctx:
            ctx = ctx + cg1 * mix_c
            ctx = ctx + cg2 * routed_ffn(modulate(rms_norm(ctx, norm2_g[l]), csh2, csc2),
                                         router_w[l], router_b[l], w_gu[l], b_gu[l], w_down[l], b_down[l])
    return rms_norm(x, final_norm_g)


_drawn_inputs = setup_inputs


def setup_inputs(seed=0):
    import zlib

    import numpy as np

    out = dict(_drawn_inputs(seed))
    spreads = {}
    factors = {'q_norm_g': 6.347, 'router_b': 3.201, 'b_gu': 8.0, 'b_down': 8.0}
    for name, (base, spread) in spreads.items():
        noise = np.random.default_rng([zlib.crc32(name.encode()), seed]).standard_normal(out[name].shape)
        drawn = base * np.exp(spread * noise) if base else spread * noise
        out[name] = __import__('jax').numpy.asarray(drawn.astype(out[name].dtype))
    for name, factor in factors.items():
        out[name] = (out[name] * factor).astype(out[name].dtype)
    return out
```

```python
from contextlib import contextmanager

import numpy as np
import concourse.bass as bass
from concourse import mybir

F32 = mybir.dt.float32
F32R = mybir.dt.float32r
BF16 = mybir.dt.bfloat16
I32 = mybir.dt.int32
U32 = mybir.dt.uint32
ALU = mybir.AluOpType
ACT = mybir.ActivationFunctionType
AX = mybir.AxisListType

P = 128
D = 1024
KD = D // P
SEQ = 1024
CTX = 256
TX = SEQ // P
TC = CTX // P
NT = TC + TX
KEYS = SEQ + CTX
EPS = 1e-6
QL, KVL, NOPE, ROPE, VH, HEADS = 384, 256, 64, 32, 64, 8
MH, MQK, MV = 4, 64, 128
NE, TOPK, FF = 32, 4, 1024
SCALE = float(NOPE + ROPE) ** -0.5
C_Q, C_KV, C_KR = 0, QL, QL + KVL
C_MQ = C_KR + ROPE
C_MK = C_MQ + MH * MQK
C_MV = C_MK + MH * MQK
C_O = C_MV + MH * MV
C_G = C_O + MH * MV
IN_W = C_G + 4 * MH
R_SH1, R_SC1, R_G1, R_SH2, R_SC2, R_G2 = (KD * i for i in range(6))
R_CSH1, R_CSC1 = 48, 56
R_N1, R_N2, R_QN, R_KVN, R_MN = 64, 72, 80, 83, 85
N_COLS = 89


RELEASED = []


@contextmanager
def semaphores(nc, phase):
    taken = []

    def sem(name):
        taken.append(nc.alloc_semaphore(f"{phase}_{name}"))
        return taken[-1]
    yield sem
    RELEASED.extend(taken)


class Chain:

    def __init__(self, eng, sem, start=0):
        self.eng, self.sem, self.start, self.n = eng, sem, start, 0

    def done(self, ins):
        ins.then_inc(self.sem, 1)
        self.n += 1
        self.eng.wait_ge(self.sem, self.start + self.n)


class Memory:

    def __init__(self, nc):
        self.nc = nc

    def at(self, name, shape, dt, offset):
        return self.nc.alloc_sbuf_tensor_at(name, shape, dt, offset=offset)

    def run(self, offset, items):
        out = []
        for name, shape, dt in items:
            out.append(self.at(name, shape, dt, offset))
            size = int(np.prod(shape[1:])) * (2 if dt == BF16 else 4)
            offset += -(-size // 32) * 32
        return out, offset


def phase_modulation(nc, a, m, PS):
    NCH = 12
    with semaphores(nc, "modulation") as sem:
        s_rows, s_id, s_ca = sem("c_rows_in"), sem("ident_ready"), sem("mod_chain_act")
        s_cd, s_ct, s_exp = sem("mod_chain_dve"), sem("c_cols_ready"), sem("exp_ready")
        s_silu, s_w0, s_w1 = sem("silu_ready"), sem("wmod_in0"), sem("wmod_in1")
        s_b0, s_b1, s_mm = sem("bmod_in0"), sem("bmod_in1"), sem("mod_chunk_done")
        s_row, s_st0, s_st1 = sem("mod_row_ready"), sem("mod_row_stored0"), sem("mod_row_stored1")
        s_v, s_vt, s_ld = sem("vec_rows_in"), sem("cols_transposed"), sem("loads_done")
        s_w, s_b, s_st = (s_w0, s_w1), (s_b0, s_b1), (s_st0, s_st1)
        (crow, ccol, cexp, csilu), _ = m.run(m.R1 + 2 * 16384, [
            ("crow", [16, P], F32), ("ccol", [P, 16], F32), ("cexp", [P, 16], F32), ("csilu", [P, 16], F32)])
        wch = [m.at(f"wmod{i}", [P, KD, 512], F32, m.R1 + 16384 * i) for i in range(2)]
        (bch0, bch1, row0, row1, vrows), _ = m.run(m.R1 + 2 * 16384 + 1024, [
            ("bch0", [2, 512], F32), ("bch1", [2, 512], F32), ("mrow0", [2, 512], F32), ("mrow1", [2, 512], F32),
            ("vrows", [N_COLS, P], F32)])
        bch, row = (bch0, bch1), (row0, row1)
        wsrc = a["w_mod"].rearrange("l (k p) n -> p (l k) n", p=P)
        with nc.Block() as block:
            @block.sync
            def _(sp):
                sp.dma_start(crow[0:KD, :], a["c"].rearrange("a (k p) -> (a k) p", p=P)).then_inc(s_rows, 16)
                sp.dma_start(crow[KD:2 * KD, :], a["c_ctx"].rearrange("(k p) -> k p", p=P)).then_inc(s_rows, 16)
                def load(j, i):
                    sp.dma_start(wch[i][:, :, :], wsrc[:, :, bass.ds(j * 512, 512)]).then_inc(s_w[i], 16)
                    sp.dma_start(bch[i][0:1, :], a["b_mod"][:, bass.ds(j * 512, 512)]).then_inc(s_b[i], 16)
                    sp.dma_start(bch[i][1:2, :], a["b_mod"][:, bass.ds(j * 512, 512)]).then_inc(s_b[i], 16)
                load(0, 0)
                load(1, 1)
                with sp.Fori(1, NCH // 2) as h:
                    for i in range(2):
                        sp.wait_ge(s_row, 2 * h + i - 1)
                        load(2 * h + i, i)
                sp.dma_start(m.w_in[:, :, :], a["w_in"].rearrange("l (k p) n -> p (l k) n", p=P)).then_inc(s_ld, 16)
                sp.dma_start(m.bgates[:, :], a["b_gates"].to_broadcast([P, 16])).then_inc(s_ld, 16)
                sp.dma_start(m.cs_tab[:, :, :], a["cs_tab"].rearrange("(t p) n -> p t n", p=P)).then_inc(s_ld, 16)
                sp.dma_start(m.sn_tab[:, :, :], a["sn_tab"].rearrange("(t p) n -> p t n", p=P)).then_inc(s_ld, 16)
                sp.wait_ge(s_row, NCH)
                sp.wait_ge(s_st0, 8 * NCH)
                sp.wait_ge(s_st1, 8 * NCH)
                md = a["mod"]
                sp.dma_start(vrows[0:48, :], md[0:1, :].rearrange("a (r p) -> (a r) p", p=P)).then_inc(s_v, 16)
                sp.dma_start(vrows[48:64, :], md[1:2, 0:2 * D].rearrange("a (r p) -> (a r) p", p=P)).then_inc(s_v, 16)
                for name, r in (("norm1_g", R_N1), ("norm2_g", R_N2), ("q_norm_g", R_QN), ("kv_norm_g", R_KVN), ("m_norm_g", R_MN)):
                    src = a[name].rearrange("l (r p) -> (l r) p", p=P)
                    sp.dma_start(vrows[r:r + src.shape[0], :], src).then_inc(s_v, 16)
                sp.wait_ge(s_ld, 64)

            @block.gpsimd
            def _(pool):
                pool.memset(m.ident[:, :], 0.0).then_inc(s_id, 1)
                pool.wait_ge(s_id, 1)
                pool.affine_select(out=m.ident[:, :], in_=m.ident[:, :], compare_op=ALU.not_equal, fill=1.0,
                                   base=0, pattern=[[-1, P]], channel_multiplier=1).then_inc(s_id, 1)

            @block.vector
            def _(dve):
                chain = Chain(dve, s_cd)
                dve.memset(m.eps[:, :], EPS).then_inc(s_cd, 1)
                chain.n = 1
                dve.wait_ge(s_ct, 1)
                chain.done(dve.tensor_copy(ccol[:, :], PS[:, 2, 0:16]))
                dve.sem_inc(s_silu, 1)
                dve.wait_ge(s_exp, 1)
                chain.done(dve.tensor_scalar(cexp[:, :], cexp[:, :], 1.0, None, ALU.add))
                chain.done(dve.reciprocal(cexp[:, :], cexp[:, :]))
                dve.tensor_tensor(csilu[:, :], ccol[:, :], cexp[:, :], ALU.mult).then_inc(s_silu, 1)

                def finish(j, i, first):
                    dve.wait_ge(s_mm, j + 1)
                    dve.wait_ge(s_b[i], 32 * (j // 2 + 1) if first else 32 * j2 + 32)
                    if not first:
                        dve.wait_ge(s_st[i], 16 * j2)
                    dve.tensor_tensor(row[i][:, :], PS[0:2, i, :], bch[i][:, :], ALU.add).then_inc(s_row, 1)
                for i in range(2):
                    finish(i, i, True)
                with dve.Fori(1, NCH // 2) as j2:
                    for i in range(2):
                        finish(2 * j2 + i, i, False)
                dve.wait_ge(s_vt, 1)
                chain.done(dve.tensor_copy(m.cols[:, :], PS[:, 3, 0:N_COLS]))
                for dst, g, sc in ((m.s1x, R_N1, R_SC1), (m.s1c, R_N1, R_CSC1), (m.s2, R_N2, R_SC2)):
                    chain.done(dve.scalar_tensor_tensor(out=dst[:, :], in0=m.cols[:, sc:sc + KD], scalar=1.0,
                                                        in1=m.cols[:, g:g + KD], op0=ALU.add, op1=ALU.mult))

            @block.tensor
            def _(pe):
                pe.wait_ge(s_id, 2)
                pe.wait_ge(s_rows, 32)
                pe.transpose(PS[:, 2, 0:16], crow[:, :], m.ident[0:16, 0:16]).then_inc(s_ct, 1)
                pe.wait_ge(s_silu, 2)

                def chunk(j, i, first):
                    pe.wait_ge(s_w[i], 16 if first else 16 * j2 + 16)
                    if not first:
                        pe.wait_ge(s_row, j - 1)
                    for k in range(KD):
                        mm = pe.matmul(PS[0:2, i, :], csilu[:, k:16:KD], wch[i][:, k, :], start=(k == 0), stop=(k == KD - 1))
                    mm.then_inc(s_mm, 1)
                for i in range(2):
                    chunk(i, i, True)
                with pe.Fori(1, NCH // 2) as j2:
                    for i in range(2):
                        chunk(2 * j2 + i, i, False)
                pe.wait_ge(s_v, 7 * 16)
                pe.transpose(PS[:, 3, 0:N_COLS], vrows[:, :], m.ident[0:N_COLS, 0:N_COLS]).then_inc(s_vt, 1)

            @block.scalar
            def _(act):
                act.wait_ge(s_silu, 1)
                act.activation(cexp[:, :], PS[:, 2, 0:16], ACT.Exp, scale=-1.0).then_inc(s_exp, 1)

                def store(j, i):
                    act.wait_ge(s_row, j + 1)
                    act.dma_start(a["mod"][:, bass.ds(j * 512, 512)], row[i][:, :]).then_inc(s_st[i], 16)
                with act.Fori(0, NCH // 2) as j2:
                    for i in range(2):
                        store(2 * j2 + i, i)


def phase_projection(nc, a, m, PS):
    with semaphores(nc, "projection") as sem:
        s_x = [sem("xtile_in0"), sem("xtile_in1")]
        s_ca, s_cd = sem("proj_chain_act"), sem("proj_chain_dve")
        s_rstd, s_xn, s_xT = sem("x_rstd_ready"), sem("xn_ready"), sem("xT_in_psum")
        s_hxa, s_hxd = sem("hxT_lo_chunks_ready"), sem("hxT_hi_chunks_ready")
        s_g0, s_g1, s_mq = sem("cq_done"), sem("ckv_done"), sem("mq_done")
        s_g2, s_g3, s_g4 = sem("k_v_done"), sem("v_o_done"), sem("o_gate_done")
        s_qr, s_kr = sem("cq_rstd_ready"), sem("ckv_rstd_ready")
        s_ctn, s_cT = sem("latents_normed"), sem("latentsT_in_psum")
        s_cTa, s_cTd = sem("cqT_kept"), sem("ckvT_kept")
        s_emq = sem("mq_bank_free")
        s_e2, s_e3, s_e4 = sem("k_v_taken"), sem("v_o_taken"), sem("o_gate_taken")
        s_one = sem("ones_set")

        (x0, x1, xn, hx0, hx1, cqn, ckvn, krn, krt, junk, st), _ = m.run(m.R1, [
            ("x0", [P, D], F32), ("x1", [P, D], F32), ("xn", [P, D], F32), ("hx0", [P, KD, P], F32),
            ("hx1", [P, KD, P], F32), ("cqn", [P, QL], F32), ("ckvn", [P, KVL], F32), ("krn", [P, ROPE], F32),
            ("krt", [P, ROPE], F32), ("junk", [P, D], F32), ("stats", [P, 16], F32)])
        xt, hx = (x0, x1), (hx0, hx1)
        T = PS[:, 6:8, :].rearrange("p b n -> p (b n)")
        xsrc = a["x"].rearrange("b (t p) d -> (b t) p d", p=P)
        csrc = a["ctx"].rearrange("b (t p) d -> (b t) p d", p=P)
        QK_, KVK = QL // P, KVL // P
        LAST = 9

        def tiles(eng, body):
            for t in range(TC):
                body(t, t % 2, t)
            with eng.Fori(TC // 2, NT // 2 - 1) as i:
                for j in range(2):
                    body(2 * i + j, j, 2)
            body(NT - 2, 0, 2)
            body(NT - 1, 1, LAST)

        def after(kind):
            return min(kind + 1, 2)

        with nc.Block() as block:
            @block.sync
            def _(sp):
                def tile(t, j, kind):
                    if kind >= 2:
                        sp.wait_ge(s_xn, t - 1)
                        sp.dma_start(xt[j][:, :], xsrc[t - TC]).then_inc(s_x[j], 16)
                    else:
                        sp.dma_start(xt[j][:, :], csrc[t]).then_inc(s_x[j], 16)
                tiles(sp, tile)

            @block.scalar
            def _(act):
                def rstd(chain, ssq, out, n, signal):
                    chain.done(act.activation(st[:, 3:4], ssq, ACT.Ln, bias=m.eps[:, 0:1], scale=1.0 / n))
                    act.activation(out, st[:, 3:4], ACT.Exp, scale=-0.5).then_inc(signal, 1)

                def x_stats(chain, t, j, kind):
                    act.wait_ge(s_x[j], (t - j) * 8 + 16)
                    if kind >= 1:
                        act.wait_ge(s_xn, t)
                    chain.done(act.activation(junk[:, :], xt[j][:, :], ACT.Square, accum_out=st[:, 0:1]))
                    rstd(chain, st[:, 0:1], st[:, 4:5], D, s_rstd)

                def hx_copy(t, j, kind):
                    act.wait_ge(s_xT, t + 1)
                    if kind >= 2:
                        act.wait_ge(s_g4, t - 1)
                    sc, sh = (m.s1c, R_CSH1) if kind < TC else (m.s1x, R_SH1)
                    for k in range(KD // 2):
                        ins = act.activation(hx[j][:, k, :], T[:, k * P:(k + 1) * P], ACT.Identity,
                                             scale=sc[:, k:k + 1], bias=m.cols[:, sh + k:sh + k + 1])
                    ins.then_inc(s_hxa, 1)

                x_stats(Chain(act, s_ca), 0, 0, 0)
                hx_copy(0, 0, 0)

                def tile(t, j, kind):
                    x = kind >= TC
                    base = Chain(act, s_ca, 2 + (4 * t if kind < TC else 4 * TC + (t - TC) * 6))
                    if kind != LAST:
                        x_stats(base, t + 1, 1 - j, after(kind))
                    if x:
                        act.wait_ge(s_g0, t - TC + 1)
                        act.wait_ge(s_ctn, t)
                        base.done(act.activation(junk[:, 0:QL], PS[:, 0, 0:QL], ACT.Square, accum_out=st[:, 1:2]))
                        rstd(base, st[:, 1:2], st[:, 5:6], QL, s_qr)
                    act.wait_ge(s_g1, t + 1)
                    if kind >= 1:
                        act.wait_ge(s_ctn, t)
                    base.done(act.activation(junk[:, 0:KVL], PS[:, 1, 0:KVL], ACT.Square, accum_out=st[:, 2:3]))
                    rstd(base, st[:, 2:3], st[:, 6:7], KVL, s_kr)
                    if x:
                        act.wait_ge(s_mq, t - TC + 1)
                        act.activation(m.mqT[:, :, bass.ds((t - TC) * P, P)], PS[:, 5, 0:2 * P].rearrange("p (c n) -> p c n", c=2),
                                       ACT.Copy, scale=MQK ** -0.5).then_inc(s_emq, 1)
                    if kind != LAST:
                        hx_copy(t + 1, 1 - j, after(kind))
                    act.wait_ge(s_g3, t + 1)
                    ins = act.activation(m.vaug[:, t, 2:4, 0:MV], PS[:, 3, 0:256].rearrange("p (h n) -> p h n", h=2), ACT.Copy)
                    if x:
                        ins = act.activation(m.og[:, t - TC, 0:256], PS[:, 3, 256:512], ACT.Exp, scale=-1.0)
                    ins.then_inc(s_e3, 1)
                    act.wait_ge(s_g4, t + 1)
                    if x:
                        act.activation(m.og[:, t - TC, 256:512], PS[:, 4, 0:256], ACT.Exp, scale=-1.0)
                    act.activation(m.g16[:, t, :], PS[:, 4, 256:272], ACT.Copy).then_inc(s_e4, 1)
                    if x:
                        act.wait_ge(s_cT, t + 1)
                        for k in range(QK_):
                            ins = act.activation(m.cqT[:, k, bass.ds((t - TC) * P, P)], T[:, k * P:(k + 1) * P], ACT.Copy,
                                                 scale=m.cols[:, R_QN + k:R_QN + k + 1])
                        ins.then_inc(s_cTa, 1)
                tiles(act, tile)

            @block.vector
            def _(dve):
                dve.memset(m.vaug[:, :, :, MV:MV + 1], 1.0).then_inc(s_one, 1)

                def x_norm(t, j, kind):
                    dve.wait_ge(s_rstd, t + 1)
                    if kind >= 1:
                        dve.wait_ge(s_xT, t)
                    dve.tensor_scalar(xn[:, :], xt[j][:, :], st[:, 4:5], None, ALU.mult).then_inc(s_xn, 1)

                def hx_copy(t, j, kind):
                    dve.wait_ge(s_xT, t + 1)
                    if kind >= 2:
                        dve.wait_ge(s_g4, t - 1)
                    sc, sh = (m.s1c, R_CSH1) if kind < TC else (m.s1x, R_SH1)
                    for k in range(KD // 2, KD):
                        ins = dve.tensor_scalar(hx[j][:, k, :], T[:, k * P:(k + 1) * P], sc[:, k:k + 1],
                                                m.cols[:, sh + k:sh + k + 1], ALU.mult, ALU.add)
                    ins.then_inc(s_hxd, 1)

                x_norm(0, 0, 0)
                hx_copy(0, 0, 0)

                def tile(t, j, kind):
                    x = kind >= TC
                    chain = Chain(dve, s_cd, t * 2)
                    if kind != LAST:
                        x_norm(t + 1, 1 - j, after(kind))
                    if kind >= 1:
                        dve.wait_ge(s_cT, t)
                    if x:
                        dve.wait_ge(s_qr, t - TC + 1)
                        dve.tensor_scalar(cqn[:, :], PS[:, 0, 0:QL], st[:, 5:6], None, ALU.mult)
                    dve.wait_ge(s_kr, t + 1)
                    dve.tensor_scalar(ckvn[:, :], PS[:, 1, 0:KVL], st[:, 6:7], None, ALU.mult)
                    kr = PS[:, 1, KVL:KVL + ROPE]
                    chain.done(dve.tensor_tensor(krn[:, :], kr, m.cs_tab[:, t, :], ALU.mult))
                    swapped = kr.rearrange("p (s n) -> p s n", s=2)[:, ::-1, :]
                    chain.done(dve.tensor_tensor(krt[:, :].rearrange("p (s n) -> p s n", s=2), swapped,
                                                 m.sn_tab[:, t, :].rearrange("p (s n) -> p s n", s=2), ALU.mult))
                    dve.tensor_tensor(krn[:, :], krn[:, :], krt[:, :], ALU.add).then_inc(s_ctn, 1)
                    if kind != LAST:
                        hx_copy(t + 1, 1 - j, after(kind))
                    dve.wait_ge(s_g2, t + 1)
                    dve.tensor_copy(m.mk[:, t, :], PS[:, 2, 0:256])
                    dve.tensor_copy(m.vaug[:, t, 0:2, 0:MV], PS[:, 2, 256:512].rearrange("p (h n) -> p h n", h=2)).then_inc(s_e2, 1)
                    dve.wait_ge(s_cT, t + 1)
                    for k in range(KVK):
                        dve.tensor_scalar(m.ckvT[:, k, bass.ds(t * P, P)], T[:, (4 + k) * P:(5 + k) * P],
                                          m.cols[:, R_KVN + k:R_KVN + k + 1], None, ALU.mult)
                    for kT in m.kT:
                        ins = dve.tensor_copy(kT[NOPE:NOPE + ROPE, bass.ds(t * P, P)], T[0:ROPE, 6 * P:7 * P])
                    ins.then_inc(s_cTd, 1)
                tiles(dve, tile)

            @block.tensor
            def _(pe):
                def x_transposes(t, j, kind):
                    pe.wait_ge(s_xn, t + 1)
                    if kind >= 2:
                        pe.wait_ge(s_cTa, t - 1)
                        pe.wait_ge(s_cTd, t - 1)
                    for k in range(KD):
                        tr = pe.transpose(T[:, k * P:(k + 1) * P], xn[:, k * P:(k + 1) * P], m.ident[:, :])
                    tr.then_inc(s_xT, 1)
                pe.sem_inc(s_cTa, TC)
                pe.sem_inc(s_emq, 1)
                x_transposes(0, 0, 0)

                def group(j, bank, lo, hi, signal, start=0):
                    for k in range(KD):
                        mm = pe.matmul(PS[:, bank, start:start + hi - lo], hx[j][:, k, :], m.w_in[:, k, lo:hi],
                                       start=(k == 0), stop=(k == KD - 1))
                    if signal is not None:
                        mm.then_inc(signal, 1)

                def tile(t, j, kind):
                    x = kind >= TC
                    pe.wait_ge(s_hxa, t + 1)
                    pe.wait_ge(s_hxd, t + 1)
                    if x:
                        pe.wait_ge(s_ctn, t)
                        group(j, 0, C_Q, C_KV, s_g0)
                    elif kind == 1:
                        pe.wait_ge(s_ctn, t)
                    group(j, 1, C_KV, C_MQ, s_g1)
                    if x:
                        pe.wait_ge(s_emq, t - TC + 1)
                        for c in range(2):
                            for k in range(KD):
                                mm = pe.matmul(PS[:, 5, c * P:(c + 1) * P], m.w_in[:, k, C_MQ + c * P:C_MQ + (c + 1) * P],
                                               hx[j][:, k, :], start=(k == 0), stop=(k == KD - 1))
                        mm.then_inc(s_mq, 1)
                    if kind >= 1:
                        pe.wait_ge(s_e2, t)
                    group(j, 2, C_MK, C_MK + 512, s_g2)
                    if kind != LAST:
                        x_transposes(t + 1, 1 - j, after(kind))
                    if kind >= 1:
                        pe.wait_ge(s_e3, t)
                        pe.wait_ge(s_e4, t)
                    if x:
                        group(j, 3, C_MK + 512, C_MK + 1024, s_g3)
                        group(j, 4, C_MK + 1024, IN_W, s_g4)
                    else:
                        group(j, 3, C_MK + 512, C_O, s_g3)
                        group(j, 4, C_G, IN_W, s_g4, start=256)
                    pe.wait_ge(s_ctn, t + 1)
                    if kind != LAST:
                        pe.wait_ge(s_hxa, t + 2)
                        pe.wait_ge(s_hxd, t + 2)
                    if x:
                        for k in range(QK_):
                            pe.transpose(T[:, k * P:(k + 1) * P], cqn[:, k * P:(k + 1) * P], m.ident[:, :])
                    for k in range(KVK):
                        pe.transpose(T[:, (4 + k) * P:(5 + k) * P], ckvn[:, k * P:(k + 1) * P], m.ident[:, :])
                    pe.transpose(T[0:ROPE, 6 * P:7 * P], krn[:, :], m.ident[:, :]).then_inc(s_cT, 1)
                tiles(pe, tile)


def phase_mlstm(nc, a, m, PS):
    ROWS = 64
    with semaphores(nc, "mlstm") as sem:
        s_cst = sem("mlstm_constants")
        s_pad, s_gT, s_rows = sem("gates_padded"), sem("gatesT_in_psum"), sem("gate_rows_ready")
        s_cd, s_ca = sem("mlstm_chain_dve"), sem("mlstm_chain_act")
        s_fa, s_fl = sem("abs_f_ready"), sem("log1p_ready")
        s_ex, s_exd = sem("exponents_ready"), sem("exponentials_ready")
        s_qc, s_qcd, s_dec, s_decd = sem("columns_in_psum"), sem("columns_kept"), sem("decay_in_psum"), sem("decay_kept")
        s_ktp, s_mb, s_st, s_u, s_num = sem("kT_in_psum"), sem("row_broadcasts_done"), sem("scores_done"), sem("kv_products_done"), sem("numerators_done")
        s_qz, s_kt, s_kw = sem("q_chunk_ready"), sem("kT_chunk_ready"), sem("weighted_k_ready")
        s_e, s_qw, s_pt = sem("weights_ready"), sem("scaled_q_ready"), sem("weighted_scores_ready")
        s_mkc = sem("k_chunk_copied")
        s_c, s_h = sem("state_updated"), sem("h_written")

        items, end = m.run(m.W, [
            ("hsum", [P, TX, MH * MV], F32),
            ("gi", [P, NT, ROWS], F32), ("gf", [P, NT, ROWS], F32), ("gab", [P, NT, 8], F32), ("gln", [P, NT, 8], F32),
            ("ri", [ROWS, KEYS], F32), ("rf", [ROWS, KEYS], F32), ("rb", [ROWS, KEYS], F32), ("ra", [ROWS, KEYS], F32),
            ("rm", [ROWS, KEYS], F32), ("rwi", [ROWS, KEYS], F32), ("rem", [ROWS, KEYS], F32)])
        hsum, gi, gf, gab, gln, ri, rf, rb, ra, rm, rwi, rem = items
        assert end <= m.R1
        items, end = m.run(m.R1, [
            ("rws", [ROWS, KEYS], F32), ("mprev", [ROWS, NT + 1], F32), ("rdec", [ROWS, NT], F32),
            ("qcol", [P, 4, NT, 8], F32), ("dcol", [P, 4, NT], F32),
            ("sel", [ROWS, 8, P], F32), ("selp", [ROWS, 4, P], F32), ("identb", [P, P], BF16), ("maskb", [P, 2, P], BF16),
            ("kwt0", [P, MH, P], F32), ("kwt1", [P, MH, P], F32), ("ktc", [P, 2, P], F32), ("ewt", [P, MH, P], F32),
            ("small", [P, 3, MH], F32)])
        rws, mprev, rdec, qcol, dcol, sel, selp, identb, maskb, kwt0, kwt1, ktc, ewt, small = items
        assert end <= m.R1 + 32768
        items, end = m.run(m.R1 + 32768 + 8 * KEYS, [
            ("ptt0", [P, MH, P], F32), ("ptt1", [P, MH, P], F32), ("cst0", [P, 2, MV + 1], F32), ("cst1", [P, 2, MV + 1], F32), ("other", [P, MH, P], F32),
            ("mkc0", [P, MH * MQK], F32), ("mkc1", [P, MH * MQK], F32)])
        ptt0, ptt1, cst0, cst1, other, mkc0, mkc1 = items
        mkc = (mkc0, mkc1)
        assert end <= 229344
        (qz0, qz1), end = m.run(m.W + 4 * TX * MH * MV, [("qz0", [P, MH, P], F32), ("qz1", [P, MH, P], F32)])
        (qw0, qw1), _ = m.run(end, [("qw0", [P, MH, P], F32), ("qw1", [P, MH, P], F32)])
        kwt, ptt, cst, qz, qw = (kwt0, kwt1), (ptt0, ptt1), (cst0, cst1), (qz0, qz1), (qw0, qw1)
        m.hsum = hsum
        DIRS = ((0, 1), (32, -1))
        ORDER = (list(range(NT)), list(range(TC - 1, -1, -1)) + list(range(NT - 1, TC - 1, -1)))
        QA, QWI, QEM, QWS = range(4)

        def fb(tile):
            return tile.rearrange("p t (d r) -> p t d r", d=2)[:, :, :, 0:MH]

        NUM = PS[:, 5:7, :].rearrange("p b (h n) -> p (b h) n", h=2)
        with nc.Block() as block:
            @block.gpsimd
            def _(pool):
                pool.memset(sel[:, :, :], 0.0)
                pool.memset(selp[:, :, :], 0.0)
                pool.memset(identb[:, :], 0.0)
                pool.memset(maskb[:, :, :], 0.0)
                pool.memset(gi[:, :, :], 0.0)
                pool.memset(gf[:, :, :], 0.0).then_inc(s_cst, 1)
                pool.wait_ge(s_cst, 1)
                v = sel[:, :, :].rearrange("r (d h) n -> r d h n", d=2)
                pool.affine_select(out=v, in_=v, compare_op=ALU.not_equal, fill=1.0, base=0,
                                   pattern=[[-32, 2], [-1, MH], [0, P]], channel_multiplier=1)
                v = selp[:, :, :].rearrange("r (d c) (e n) -> r d (c e) n", d=2, e=2)
                for d in range(2):
                    pool.affine_select(out=v[:, d], in_=v[:, d], compare_op=ALU.not_equal, fill=1.0, base=-32 * d,
                                       pattern=[[-1, 4], [0, MQK]], channel_multiplier=1)
                pool.affine_select(out=identb[:, :], in_=identb[:, :], compare_op=ALU.not_equal, fill=1.0,
                                   base=0, pattern=[[-1, P]], channel_multiplier=1)
                for d, step in enumerate((1, -1)):
                    ins = pool.affine_select(out=maskb[:, d, :], in_=maskb[:, d, :], compare_op=ALU.is_ge, fill=1e30,
                                             base=0, pattern=[[step, P]], channel_multiplier=-step)
                ins.then_inc(s_cst, 1)

            @block.scalar
            def _(act):
                act.preload_act_table_set("natural_log_exp_and_others")
                chain = Chain(act, s_ca)
                act.wait_ge(s_fa, 1)
                chain.done(act.activation(gln[:, :, :], gab[:, :, :], ACT.Exp, scale=-1.0))
                act.activation(gln[:, :, :], gln[:, :, :], ACT.Ln, bias=1.0).then_inc(s_fl, 1)
                for n, (r, scale) in enumerate(((rwi, -1.0), (rem, -1.0), (rws, 1.0))):
                    act.wait_ge(s_ex, n + 1)
                    act.activation(r[:, :], r[:, :], ACT.Exp, scale=scale).then_inc(s_exd, 1)
                act.wait_ge(s_ex, 4)
                act.activation(rdec[:, :], rdec[:, :], ACT.Exp).then_inc(s_exd, 1)
                act.wait_ge(s_qcd, 1)

                def k_copy(x, t, d):
                    act.wait_ge(s_num, x)
                    act.activation(mkc[d][:, :], m.mk[:, t, :], ACT.Copy).then_inc(s_mkc, 1)

                def weights(n, t, d):
                    act.wait_ge(s_mb, n)
                    act.wait_ge(s_pt, n)
                    for h in range(MH):
                        ins = act.activation(ewt[:, h, :], PS[:, 1, h * P:(h + 1) * P], ACT.Exp, scale=-1.0,
                                             bias=qcol[:, QA, t, 4 * d + h:4 * d + h + 1])
                    ins.then_inc(s_e, 1)
                for lo in (TC, TC + TX // 2):
                    with act.Fori(lo, lo + TX // 2) as i:
                        for d in range(2):
                            x, t = 2 * (i - TC) + d + 1, i if d == 0 else i * -1 + (NT + 1)
                            k_copy(x, t, d)
                            weights(x, t, d)

            @block.vector
            def _(dve):
                chain = Chain(dve, s_cd)
                dve.wait_ge(s_cst, 1)
                for d in range(2):
                    chain.done(dve.memset(cst[d][:, :, :], 0.0))
                    chain.done(dve.memset(kwt[d][:, :, :], 0.0))
                chain.done(dve.memset(mprev[:, :], 0.0))
                bias = m.bgates[:, :].rearrange("p (a n) -> p a n", a=1).to_broadcast([P, NT, 16])
                chain.done(dve.tensor_tensor(m.g16[:, :, :], m.g16[:, :, :], bias, ALU.add))
                g4 = m.g16[:, :, :].rearrange("p t (d q h) -> p t d q h", d=2, q=2)
                f4 = gab[:, :, :].rearrange("p t (d h) -> p t d h", d=2)
                l4 = gln[:, :, :].rearrange("p t (d h) -> p t d h", d=2)
                for d in range(2):
                    dve.tensor_copy(fb(gi[:, :, :])[:, :, d, :], g4[:, :, d, 0, :])
                    chain.done(dve.tensor_scalar(fb(gf[:, :, :])[:, :, d, :], g4[:, :, d, 1, :], 0.0, None, ALU.min))
                    chain.done(dve.scalar_tensor_tensor(out=f4[:, :, d, :], in0=g4[:, :, d, 1, :], scalar=-1.0, in1=g4[:, :, d, 1, :],
                                                        op0=ALU.mult, op1=ALU.max))
                dve.sem_inc(s_fa, 1)
                dve.wait_ge(s_fl, 1)
                for d in range(2):
                    ins = dve.tensor_tensor(fb(gf[:, :, :])[:, :, d, :], fb(gf[:, :, :])[:, :, d, :], l4[:, :, d, :], ALU.subtract)
                ins.then_inc(s_pad, 1)
                dve.wait_ge(s_gT, 1)
                dve.tensor_copy(ri[:, :], PS[0:ROWS, 0:3, :].rearrange("p b n -> p (b n)")[:, 0:KEYS])
                chain.done(dve.tensor_copy(rf[:, :], PS[0:ROWS, 3:6, :].rearrange("p b n -> p (b n)")[:, 0:KEYS]))

                def chunk(r, d, t):
                    p0, step = DIRS[d]
                    return r[p0:p0 + MH, t * P:(t + 1) * P][:, ::step]

                def last(r, d, t):
                    p0, step = DIRS[d]
                    e = t * P + (P - 1 if step == 1 else 0)
                    return r[p0:p0 + MH, e:e + 1]
                dve.memset(rb[:, :], 0.0)
                chain.done(dve.memset(rm[:, :], 0.0))
                for t in range(NT):
                    for d in range(2):
                        ins = dve.tensor_tensor_scan(chunk(rb, d, t), chunk(rf, d, t), chunk(rf, d, t), 0.0, ALU.add, ALU.bypass)
                chain.done(ins)
                chain.done(dve.tensor_tensor(ra[:, :], ri[:, :], rb[:, :], ALU.subtract))
                for i in range(NT):
                    for d in range(2):
                        t, p0 = ORDER[d][i], DIRS[d][0]
                        ins = dve.tensor_tensor_scan(chunk(rm, d, t), chunk(ra, d, t), chunk(ra, d, t),
                                                     mprev[p0:p0 + MH, t:t + 1], ALU.max, ALU.max)
                    chain.done(ins)
                    for d in range(2):
                        t, p0 = ORDER[d][i], DIRS[d][0]
                        nxt = ORDER[d][i + 1] if i + 1 < NT else NT
                        ins = dve.tensor_tensor(mprev[p0:p0 + MH, nxt:nxt + 1], last(rb, d, t), last(rm, d, t), ALU.add)
                    chain.done(ins)
                mp = mprev[:, 0:NT].rearrange("p (t o) -> p t o", o=1)

                def c3(r):
                    return r[:, :].rearrange("p (t n) -> p t n", n=P)
                dve.tensor_tensor(c3(rwi), c3(rm), mp.to_broadcast([ROWS, NT, P]), ALU.subtract).then_inc(s_ex, 1)
                dve.tensor_tensor(rem[:, :], rm[:, :], rb[:, :], ALU.add).then_inc(s_ex, 1)
                for half, e in ((0, P - 1), (32, 0)):
                    ml = c3(rm)[half:half + 32, :, e:e + 1]
                    ins = dve.tensor_tensor(c3(rws)[half:half + 32], c3(ra)[half:half + 32], ml.to_broadcast([32, NT, P]), ALU.subtract)
                ins.then_inc(s_ex, 1)
                for half, e in ((0, P - 1), (32, 0)):
                    ml = c3(rm)[half:half + 32, :, e:e + 1]
                    ins = dve.tensor_tensor(rdec[half:half + 32, :], mprev[half:half + 32, 0:NT], ml.rearrange("p t o -> p (t o)"), ALU.subtract)
                ins.then_inc(s_ex, 1)
                dve.wait_ge(s_qc, 1)
                for q in range(4):
                    src = PS[:, 0:5, :].rearrange("p b (x d r) -> p (b x) d r", d=2, r=32)[:, q * NT:(q + 1) * NT, :, 0:MH]
                    for d in range(2):
                        ins = dve.tensor_copy(qcol[:, q, :, 4 * d:4 * d + 4], src[:, :, d, :])
                dve.wait_ge(s_dec, 1)
                chain.done(dve.tensor_copy(dcol[:, :, :], PS[:, 7, 0:4 * NT].rearrange("p (c t) -> p c t", c=4)))
                for d in range(2):
                    chain.done(dve.memset(qz[d][:, :, :], 0.0))
                dve.sem_inc(s_qcd, 2)
                base = chain.n

                def weigh_k(n, t, d):
                    dve.wait_ge(s_u, n - 2) if not isinstance(n, int) or n > 2 else None
                    w = qcol[:, QWS, t, 4 * d:4 * d + 4].rearrange("p (h o) -> p h o", o=1)
                    k = m.mk[:, t, :].rearrange("p (h n) -> p h n", h=MH)
                    for e in range(2):
                        ins = dve.tensor_tensor(kwt[d][:, e:MH:2, 64 * e:64 * e + MQK], k[:, e:MH:2, :],
                                                w[:, e:MH:2, :].to_broadcast([P, 2, MQK]), ALU.mult)
                    ins.then_inc(s_kw, 1)

                def update(n, t, d):
                    dve.wait_ge(s_u, n)
                    for c in range(2):
                        ins = dve.scalar_tensor_tensor(out=cst[d][:, c, :], in0=cst[d][:, c, :], scalar=dcol[:, 2 * d + c, bass.ds(t, 1)],
                                                       in1=PS[:, 4, c * 256:c * 256 + MV + 1], op0=ALU.mult, op1=ALU.add)
                    ins.then_inc(s_c, 1)

                for i in range(TC):
                    for d in range(2):
                        weigh_k(2 * i + d + 1, ORDER[d][i], d)
                        update(2 * i + d + 1, ORDER[d][i], d)

                def latent(i, d, first):
                    t = i if d == 0 else i * -1 + (NT + 1)
                    n, x = 2 * i + d + 1, 2 * (i - TC) + d + 1
                    dve.wait_ge(s_num, x)
                    for e in range(2):
                        ins = dve.tensor_copy(qz[d][64 * e:64 * e + 64, e:MH:2, :], m.mqT[64 * e:64 * e + 64, :, bass.ds((t - TC) * P, P)])
                    ins.then_inc(s_qz, 1)
                    weigh_k(n, t, d)
                    dve.wait_ge(s_ktp, x)
                    dve.tensor_copy(ktc[:, :, :], PS[:, 3, 0:2 * P].rearrange("p (c n) -> p c n", c=2)).then_inc(s_kt, 1)
                    dve.wait_ge(s_mb, x)
                    dve.wait_ge(s_qz, x)
                    dve.tensor_tensor(qw[d][:, :, :], qz[d][:, :, :], PS[:, 2, :].rearrange("p (h n) -> p h n", h=MH), ALU.mult).then_inc(s_qw, 1)
                    dve.wait_ge(s_st, x)
                    dve.wait_ge(s_e, x + 1)
                    dve.tensor_tensor(ptt[d][:, :, :], ewt[:, :, :], PS[:, 0, :].rearrange("p (h n) -> p h n", h=MH), ALU.mult).then_inc(s_pt, 1)
                    dve.wait_ge(s_num, x + 2)
                    c = Chain(dve, s_cd, base + (x - 1) * 3)
                    c.done(dve.scalar_tensor_tensor(out=small[:, 0, :], in0=NUM[:, :, MV], scalar=-1.0,
                                                    in1=qcol[:, QEM, t, 4 * d:4 * d + 4], op0=ALU.mult, op1=ALU.max))
                    c.done(dve.tensor_tensor(small[:, 1, :], NUM[:, :, MV], small[:, 0, :], ALU.max))
                    c.done(dve.reciprocal(small[:, 2, :], small[:, 1, :]))
                    r = small[:, 2, :].rearrange("p (h o) -> p h o", o=1).to_broadcast([P, MH, MV])
                    dst = hsum[:, t - TC, :].rearrange("p (h n) -> p h n", h=MH)
                    if first:
                        dve.tensor_tensor(dst, NUM[:, :, 0:MV], r, ALU.mult).then_inc(s_h, 1)
                    else:
                        dve.tensor_tensor(other[:, :, :], NUM[:, :, 0:MV], r, ALU.mult).then_inc(s_h, 1)
                        dve.wait_ge(s_h, x + 1)
                        dve.tensor_tensor(dst, dst, other[:, :, :], ALU.add)
                    update(n, t, d)
                for lo in (TC, TC + TX // 2):
                    with dve.Fori(lo, lo + TX // 2) as i:
                        for d in range(2):
                            latent(i, d, lo == TC)

            @block.tensor
            def _(pe):
                pe.sem_inc(s_num, 2)
                pe.sem_inc(s_pt, 1)
                pe.sem_inc(s_h, 1)
                pe.sem_inc(s_kt, 1)
                pe.sem_inc(s_e, 1)
                pe.sem_inc(s_qw, 1)
                pe.wait_ge(s_cst, 2)
                pe.wait_ge(s_pad, 1)
                for g, bank in ((gi, 0), (gf, 3)):
                    for t in range(NT):
                        tr = pe.transpose(PS[0:ROWS, bank + t // 4, (t % 4) * P:(t % 4 + 1) * P], g[:, t, :], m.ident[:, :])
                tr.then_inc(s_gT, 1)
                pe.wait_ge(s_exd, 4)
                for q, r in enumerate((ra, rwi, rem, rws)):
                    for t in range(NT):
                        x = q * NT + t
                        tr = pe.transpose(PS[:, x // 8, (x % 8) * ROWS:(x % 8 + 1) * ROWS], r[:, t * P:(t + 1) * P], m.ident[0:ROWS, 0:ROWS])
                tr.then_inc(s_qc, 1)
                for c in range(4):
                    mm = pe.matmul(PS[:, 7, c * NT:(c + 1) * NT], selp[:, c, :], rdec[:, :], start=True, stop=True)
                mm.then_inc(s_dec, 1)
                pe.wait_ge(s_qcd, 1)

                def products(n, t, d):
                    pe.wait_ge(s_kw, n)
                    if not isinstance(n, int) or n > 1:
                        pe.wait_ge(s_c, n - 1)
                    for h in range(MH):
                        mm = pe.matmul(PS[:, 4, (h // 2) * 256:(h // 2) * 256 + MV + 1], kwt[d][:, h, :], m.vaug[:, t, h, :],
                                       start=(h % 2 == 0), stop=(h % 2 == 1), skip_group_check=True)
                    mm.then_inc(s_u, 1)
                for i in range(TC):
                    for d in range(2):
                        products(2 * i + d + 1, ORDER[d][i], d)

                def latent(i, d):
                    t = i if d == 0 else i * -1 + (NT + 1)
                    n, x = 2 * i + d + 1, 2 * (i - TC) + d + 1
                    pe.wait_ge(s_kt, x)
                    pe.wait_ge(s_mkc, x)
                    for c in range(2):
                        tr = pe.transpose(PS[:, 3, c * P:(c + 1) * P], mkc[d][:, c * P:(c + 1) * P], m.ident[:, :])
                    tr.then_inc(s_ktp, 1)
                    pe.wait_ge(s_e, x)
                    pe.wait_ge(s_qw, x)
                    for h in range(MH):
                        pe.matmul(PS[:, 1, h * P:(h + 1) * P], sel[:, 4 * d + h, :], rm[:, bass.ds(t * P, P)],
                                  start=(h == 0), stop=False, skip_group_check=True)
                    pe.matmul(PS[:, 1, :].rearrange("p (h n) -> p h n", h=MH), identb[:, :],
                              maskb[:, d, :].rearrange("p (o n) -> p o n", o=1).to_broadcast([P, MH, P]),
                              start=False, stop=True, skip_group_check=True)
                    for h in range(MH):
                        mm = pe.matmul(PS[:, 2, h * P:(h + 1) * P], sel[:, 4 * d + h, :], rwi[:, bass.ds(t * P, P)], start=True, stop=True)
                    mm.then_inc(s_mb, 1)
                    products(n, t, d)
                    pe.wait_ge(s_kt, x + 1)
                    pe.wait_ge(s_qz, x)
                    pe.wait_ge(s_pt, x)
                    for h in range(MH):
                        mm = pe.matmul(PS[:, 0, h * P:(h + 1) * P], ktc[:, h // 2, :], qz[d][:, h, :], start=True, stop=True)
                    mm.then_inc(s_st, 1)
                    pe.wait_ge(s_qw, x + 1)
                    pe.wait_ge(s_pt, x + 1)
                    pe.wait_ge(s_h, x)
                    for h in range(MH):
                        pe.matmul(NUM[:, h, 0:MV + 1], qw[d][:, h, :], cst[d][:, h // 2, :], start=True, stop=False, skip_group_check=True)
                        mm = pe.matmul(NUM[:, h, 0:MV + 1], ptt[d][:, h, :], m.vaug[:, t, h, :], start=False, stop=True, skip_group_check=True)
                    mm.then_inc(s_num, 1)
                for lo in (TC, TC + TX // 2):
                    with pe.Fori(lo, lo + TX // 2) as i:
                        for d in range(2):
                            latent(i, d)


def phase_attention(nc, a, m, PS):
    DQ = NOPE + ROPE
    with semaphores(nc, "attention") as sem:
        s_w = [sem("head_weights_in0"), sem("head_weights_in1")]
        s_tab = sem("rope_tables_in")
        s_rot = sem("rotated_weights_ready")
        s_kp, s_qp = sem("k_projected"), sem("q_v_projected")
        s_kd, s_qd, s_vd, s_qc = sem("kT_kept"), sem("qT_kept"), sem("v_kept"), sem("rope_chain")
        s_s, s_mx, s_p = sem("scores_done"), sem("max_ready"), sem("probs_ready")
        s_a, s_b, s_c = sem("transposed_0_3"), sem("transposed_4_7"), sem("transposed_8_9")
        s_pa, s_pb, s_pc = sem("probsT_0_3_kept"), sem("probsT_4_7_kept"), sem("probsT_8_9_kept")
        s_pv, s_rc, s_o = sem("pv_done"), sem("sum_inverted"), sem("attention_written")
        base = m.W + 4 * TX * MH * MV
        items, end = m.run(base, [
            ("attn", [P, TX, HEADS * VH], F32), ("qT0", [DQ, SEQ], F32), ("qT1", [DQ, SEQ], F32),
            ("v0", [P, NT, VH], F32), ("v1", [P, NT, VH], F32),
            ("wqh0", [P, QL // P, P], F32), ("wqh1", [P, QL // P, P], F32),
            ("wkvh0", [P, KVL // P, P], F32), ("wkvh1", [P, KVL // P, P], F32),
            ("prob0", [P, KEYS], F32), ("prob1", [P, KEYS], F32)])
        m.attn, qT0, qT1, v0, v1, wq0, wq1, wkv0, wkv1, p0, p1 = items
        assert end <= m.R1
        (probT, cst, rtmp, negmax, rsum, rinv), end = m.run(m.R1, [
            ("probT", [P, KEYS], F32), ("cst", [P, SEQ], F32), ("rtmp", [P, SEQ], F32),
            ("negmax", [P, 2], F32), ("rsum", [P, 4], F32), ("rinv", [P, 2], F32)])
        assert end <= m.R1 + 32768
        qT, v, wqh, wkvh, prob = (qT0, qT1), (v0, v1), (wq0, wq1), (wkv0, wkv1), (p0, p1)
        uq = a["w_uq"].rearrange("l (k p) (h n) -> p (l k) h n", p=P, n=DQ)
        ukv = a["w_ukv"].rearrange("l (k p) (h n) -> p (l k) h n", p=P, n=NOPE + VH)
        CH = ((0, 512), (512, 512), (1024, 256))

        def steps(last):
            out = []
            for hh in range(2):
                for u in range(8):
                    if u == 6 and not (last and hh == 1):
                        out += [("K", hh + 1), ("Q", hh + 1)]
                    out.append(("U", 8 * hh + u))
            return out

        def pairs(eng, body):
            body(0, True, False)
            with eng.Fori(1, HEADS // 2 - 1) as i:
                body(i, False, False)
            body(HEADS // 2 - 1, False, True)

        def walk(first, last, step, flush):
            todo = steps(last)
            pend = [] if first else [-2, -1]
            full = [("K", 0), ("Q", 0)] if first else [("U", -2), ("U", -1)]
            full += todo
            for n, this in enumerate(todo):
                done = None
                if this[0] == "U" and len(pend) == 2:
                    done = pend.pop(0)
                step(n, this, full[n], full[n + 1], done)
                if this[0] == "U":
                    pend.append(this[1])
            if last:
                flush(pend, todo[-1])

        with nc.Block() as block:
            @block.sync
            def _(sp):
                sp.dma_start(cst[NOPE:DQ, :], a["cs_tabT"]).then_inc(s_tab, 16)
                sp.dma_start(cst[96:128, :], a["sn_tabT"]).then_inc(s_tab, 16)

                def load(h, j):
                    sp.dma_start(wqh[j][:, :, 0:DQ], uq[:, :, h, :]).then_inc(s_w[j], 16)
                    sp.dma_start(wkvh[j][:, :, :], ukv[:, :, h, :]).then_inc(s_w[j], 16)
                load(0, 0)
                load(1, 1)
                with sp.Fori(1, HEADS // 2) as i:
                    for j in range(2):
                        sp.wait_ge(s_qp, 2 * i + j - 1)
                        load(2 * i + j, j)

            @block.scalar
            def _(act):
                act.preload_act_table_set("natural_log_exp_and_others")

                def post(what, n, i):
                    g = 3 * ((n - 1) % 2)
                    if what[0] == "K":
                        h, j = 2 * i + what[1], what[1] % 2
                        act.wait_ge(s_kp, h + 1)
                        for c, (lo, w) in enumerate(CH):
                            act.activation(m.kT[j][0:NOPE, lo:lo + w], PS[0:NOPE, g + c, 0:w], ACT.Copy)
                        act.activation(v[j][:, 8:10, :], PS[:, g + 2, 256:384].rearrange("p (t n) -> p t n", t=2), ACT.Copy).then_inc(s_kd, 1)
                    elif what[0] == "Q":
                        h, j = 2 * i + what[1], what[1] % 2
                        act.wait_ge(s_qp, h + 1)
                        act.activation(v[j][:, 0:8, :], PS[:, g + 2, :].rearrange("p (t n) -> p t n", t=8), ACT.Copy).then_inc(s_vd, 1)
                    else:
                        U = 16 * i + what[1]
                        act.wait_ge(s_mx, U + 1)
                        if not isinstance(U, int) or U > 1:
                            act.wait_ge(s_c, U - 1)
                            act.wait_ge(s_rc, U - 1)
                        act.activation(prob[what[1] % 2][:, :], PS[:, g:g + 3, :].rearrange("p b n -> p (b n)")[:, 0:KEYS], ACT.Exp,
                                       bias=negmax[:, what[1] % 2:what[1] % 2 + 1],
                                       accum_out=rsum[:, what[1] % 2:what[1] % 2 + 1]).then_inc(s_p, 1)

                def finish(r, i):
                    act.wait_ge(s_a, 16 * i + r + 1)
                    act.activation(probT[:, 0:512], PS[:, 6, :], ACT.Copy).then_inc(s_pa, 1)

                def body(i, first, last):
                    def step(n, this, before2, before1, done):
                        if done is not None:
                            finish(done, i)
                        post(before1, n, i)

                    def flush(pend, lastone):
                        finish(pend[0], i)
                        post(lastone, len(steps(True)), i)
                        finish(pend[1], i)
                    walk(first, last, step, flush)
                post(("K", 0), 1, 0)
                pairs(act, body)

            @block.vector
            def _(dve):
                def swap(h, j, first):
                    dve.wait_ge(s_w[j], 16 * (h - j) + 32)
                    dve.tensor_copy(wqh[j][:, :, DQ:DQ + 16], wqh[j][:, :, DQ - 16:DQ])
                    dve.tensor_copy(wqh[j][:, :, DQ + 16:P], wqh[j][:, :, NOPE:NOPE + 16]).then_inc(s_rot, 1)

                def project_q(h, j, n):
                    g = 3 * (n % 2)
                    dve.wait_ge(s_qp, h + 1)
                    for c in range(2):
                        cols = slice(512 * c, 512 * c + 512)
                        dve.tensor_scalar(qT[j][0:NOPE, cols], PS[0:NOPE, g + c, :], SCALE, None, ALU.mult)
                        dve.tensor_tensor(qT[j][NOPE:DQ, cols], PS[NOPE:DQ, g + c, :], cst[NOPE:DQ, cols], ALU.mult)
                        dve.tensor_tensor(rtmp[NOPE:DQ, cols], PS[96:128, g + c, :], cst[96:128, cols], ALU.mult).then_inc(s_qc, 1)
                        dve.wait_ge(s_qc, 2 * h + c + 1)
                        ins = dve.tensor_tensor(qT[j][NOPE:DQ, cols], qT[j][NOPE:DQ, cols], rtmp[NOPE:DQ, cols], ALU.add)
                    ins.then_inc(s_qd, 1)

                def finish_t(r, i):
                    U = 16 * i + r
                    dve.wait_ge(s_b, U + 1)
                    dve.tensor_copy(probT[:, 512:1024], PS[:, 7, :]).then_inc(s_pb, 1)
                    dve.wait_ge(s_p, U + 1)
                    dve.reciprocal(rinv[:, r % 2:r % 2 + 1], rsum[:, r % 2:r % 2 + 1]).then_inc(s_rc, 1)
                    dve.wait_ge(s_c, U + 1)
                    dve.tensor_copy(probT[:, 1024:KEYS], PS[:, 6, 0:256]).then_inc(s_pc, 1)

                def finish_o(r, i):
                    U = 16 * i + r
                    h = 2 * i + (1 if r >= 8 else 0) if r >= 0 else 2 * i - 1
                    dve.wait_ge(s_pv, U + 1)
                    dve.wait_ge(s_rc, U + 1)
                    dve.tensor_scalar(m.attn[:, r % 8, bass.ds(h * VH, VH)], PS[:, 7, 0:VH], rinv[:, r % 2:r % 2 + 1], None, ALU.mult).then_inc(s_o, 1)

                def body(i, first, last):
                    def step(n, this, before2, before1, done):
                        if done is not None:
                            finish_t(done, i)
                        if this[0] == "U":
                            U = 16 * i + this[1]
                            g = 3 * (n % 2)
                            dve.wait_ge(s_s, U + 1)
                            dve.tensor_reduce(negmax[:, this[1] % 2:this[1] % 2 + 1], PS[:, g:g + 3, :].rearrange("p b n -> p (b n)")[:, 0:KEYS],
                                              AX.X, ALU.max, negate=True).then_inc(s_mx, 1)
                        elif this[0] == "K":
                            swap(2 * i + this[1], this[1] % 2, False)
                        else:
                            project_q(2 * i + this[1], this[1] % 2, n)
                        if done is not None:
                            finish_o(done, i)

                    def flush(pend, lastone):
                        for r in pend:
                            finish_t(r, i)
                            finish_o(r, i)
                    walk(first, last, step, flush)
                dve.wait_ge(s_tab, 32)
                swap(0, 0, True)
                project_q(0, 0, 1)
                pairs(dve, body)

            @block.tensor
            def _(pe):
                def free(what, i):
                    if what[0] == "K":
                        pe.wait_ge(s_kd, 2 * i + what[1] + 1)
                    elif what[0] == "Q":
                        pe.wait_ge(s_qd, 2 * i + what[1] + 1)
                        pe.wait_ge(s_vd, 2 * i + what[1] + 1)
                    else:
                        pe.wait_ge(s_p, 16 * i + what[1] + 1)

                def project_v(j, t, bank, col):
                    for k in range(KVL // P):
                        mm = pe.matmul(PS[:, bank, col:col + VH], m.ckvT[:, k, t * P:(t + 1) * P], wkvh[j][:, k, NOPE:NOPE + VH],
                                       start=(k == 0), stop=(k == KVL // P - 1))
                    return mm

                def project_k(h, j, n):
                    g = 3 * (n % 2)
                    pe.wait_ge(s_rot, h + 1)
                    for c, (lo, w) in enumerate(CH):
                        for k in range(KVL // P):
                            pe.matmul(PS[0:NOPE, g + c, 0:w], wkvh[j][:, k, 0:NOPE], m.ckvT[:, k, lo:lo + w],
                                      start=(k == 0), stop=(k == KVL // P - 1))
                    for t in (8, 9):
                        mm = project_v(j, t, g + 2, 256 + (t - 8) * VH)
                    mm.then_inc(s_kp, 1)

                def project_q(j, n):
                    g = 3 * (n % 2)
                    for c in range(2):
                        for k in range(QL // P):
                            pe.matmul(PS[:, g + c, :], wqh[j][:, k, :], m.cqT[:, k, 512 * c:512 * c + 512],
                                      start=(k == 0), stop=(k == QL // P - 1))
                    for t in range(8):
                        mm = project_v(j, t, g + 2, t * VH)
                    mm.then_inc(s_qp, 1)

                def scores(r, n, c):
                    lo, w = CH[c]
                    return pe.matmul(PS[:, 3 * (n % 2) + c, 0:w], qT[r // 8][:, (r % 8) * P:(r % 8 + 1) * P], m.kT[r // 8][:, lo:lo + w],
                                     start=True, stop=True)

                def transposes(r, bank, lo, hi, signal):
                    for t in range(lo, hi):
                        tr = pe.transpose(PS[:, bank, (t - lo) * P:(t - lo + 1) * P], prob[r % 2][:, t * P:(t + 1) * P], m.ident[:, :])
                    tr.then_inc(signal, 1)

                def finish_ab(r, i):
                    U = 16 * i + r
                    static = isinstance(U, int)
                    pe.wait_ge(s_p, U + 1)
                    if not static or U > 0:
                        pe.wait_ge(s_pc, U)
                    transposes(r, 6, 0, 4, s_a)
                    if not static or U > 0:
                        pe.wait_ge(s_o, U)
                    transposes(r, 7, 4, 8, s_b)

                def finish_c(r, i):
                    pe.wait_ge(s_pa, 16 * i + r + 1)
                    transposes(r, 6, 8, 10, s_c)

                def finish_pv(r, i):
                    U = 16 * i + r
                    pe.wait_ge(s_pb, U + 1)
                    pe.wait_ge(s_pc, U + 1)
                    for t in range(NT):
                        mm = pe.matmul(PS[:, 7, 0:VH], probT[:, t * P:(t + 1) * P], v[(r // 8) % 2][:, t, :], start=(t == 0), stop=(t == NT - 1))
                    mm.then_inc(s_pv, 1)

                def body(i, first, last):
                    def step(n, this, before2, before1, done):
                        if done is not None:
                            finish_ab(done, i)
                        free(before2, i)
                        if this[0] == "K":
                            project_k(2 * i + this[1], this[1] % 2, n)
                        elif this[0] == "Q":
                            project_q(this[1] % 2, n)
                        else:
                            r = this[1]
                            if r % 8 == 0:
                                h = 2 * i + r // 8
                                pe.wait_ge(s_kd, h + 1)
                                pe.wait_ge(s_qd, h + 1)
                                pe.wait_ge(s_vd, h + 1)
                            scores(r, n, 0)
                            if done is not None:
                                finish_c(done, i)
                            scores(r, n, 1)
                            scores(r, n, 2).then_inc(s_s, 1)
                        if done is not None:
                            finish_pv(done, i)

                    def flush(pend, lastone):
                        for r in pend:
                            finish_ab(r, i)
                            finish_c(r, i)
                            finish_pv(r, i)
                    walk(first, last, step, flush)
                project_k(0, 0, 0)
                project_q(0, 1)
                pairs(pe, body)


def phase_output(nc, a, m, PS):
    with semaphores(nc, "output") as sem:
        s_wo, s_bc, s_pad = sem("w_out_in"), sem("row_vectors_in"), sem("padding_rows_stored")
        s_bi, s_rw = sem("expert_biases_in"), sem("router_weights_in")
        s_x = [sem("x_in0"), sem("x_in1")]
        s_cd, s_ca = sem("out_chain_dve"), sem("out_chain_act")
        s_s2 = sem("gain_rows_ready")
        s_mv, s_mr = sem("mlstm_mean_square"), sem("mlstm_rstd_raw")
        s_at, s_cat = sem("attention_copied"), sem("mixed_tile_ready")
        s_tc, s_tca, s_tcd = sem("catT_in_psum"), sem("catT_lo_kept"), sem("catT_hi_kept")
        s_mm, s_x2 = sem("mixed_projected"), sem("residual_ready")
        s_ssq, s_xv, s_xr = sem("x2_square_sum"), sem("x2_variance"), sem("x2_rstd_raw")
        s_h2, s_th, s_tha, s_thd = sem("h2_ready"), sem("h2T_in_psum"), sem("h2T_lo_kept"), sem("h2T_hi_kept")
        s_lg, s_lgd = sem("logits_in_psum"), sem("logits_kept")
        s_sx, s_sh = [sem("x2_stored0"), sem("x2_stored1")], [sem("h2_stored0"), sem("h2_stored1")]
        s_z, s_ln = sem("zero_rows_set"), sem("x2_log_ready")

        p_at = SB0 + 4608 + 4 * TX * MH * MV
        items, end = m.run(p_at, [
            ("w_out", [P, KD, D], F32), ("g1bc", [P, D], F32), ("s2bc", [P, D], F32), ("sh2bc", [P, D], F32), ("n2bc", [P, D], F32),
            ("rw", [P, KD, NE], F32)])
        w_out, g1bc, s2bc, sh2bc, n2bc, rw = items
        assert end <= m.W
        items, end = m.run(m.W + 8 * TX * MH * MV, [
            ("cat0", [P, D], F32), ("cat1", [P, D], F32), ("catT0", [P, KD, P], F32), ("catT1", [P, KD, P], F32),
            ("ox0", [P, D], F32), ("ox1", [P, D], F32), ("x20", [P, D], F32), ("x21", [P, D], F32),
            ("h20", [P, D], F32), ("h21", [P, D], F32), ("h2T", [P, KD, P], F32), ("junk2", [P, D], F32),
            ("sq", [P, 512], F32), ("msv", [P, 4, 4], F32), ("xst", [P, 8], F32), ("sg", [P, 512], F32), ("msln", [P, 4], F32)])
        cat0, cat1, catT0, catT1, x0, x1, x20, x21, h20, h21, h2T, junk, sq, msv, xst, sg, msln = items
        cat, catT, xt, x2, h2 = (cat0, cat1), (catT0, catT1), (x0, x1), (x20, x21), (h20, h21)
        (bias_f, m.bias3, m.logits, m.rbbc, bhi), end = m.run(end, [
            ("bias_f", [96, 2 * FF + D], F32), ("bias3", [96, 2 * FF + D], BF16), ("logits", [P, TX, NE], F32), ("rbbc", [P, NE], F32),
            ("bhi", [96, 2 * FF + D], BF16)])
        assert end <= 229344, end
        xsrc = a["x"].rearrange("b (t p) d -> (b t) p d", p=P)
        acc = a["acc"].rearrange("(t p) d -> t p d", p=P)
        h2d = a["h2"].rearrange("(t p) d -> t p d", p=P)

        def tiles(eng, body):
            body(0, 0, True, False)
            with eng.Fori(0, TX // 2 - 1) as i:
                for j in range(2):
                    body(2 * i + 1 + j, (1 + j) % 2, False, False)
            body(TX - 1, 1, False, True)

        with nc.Block() as block:
            @block.sync
            def _(sp):
                sp.dma_start(xt[0][:, :], xsrc[0]).then_inc(s_x[0], 16)
                sp.dma_start(w_out[:, :, :], a["w_out"].rearrange("l (k p) n -> p (l k) n", p=P)).then_inc(s_wo, 16)
                for dst, row in ((g1bc, R_G1), (s2bc, R_SC2), (sh2bc, R_SH2)):
                    sp.dma_start(dst[:, :], a["mod"][0:1, row * P:row * P + D].to_broadcast([P, D])).then_inc(s_bc, 16)
                sp.dma_start(n2bc[:, :], a["norm2_g"].to_broadcast([P, D])).then_inc(s_bc, 16)
                sp.dma_start(m.rbbc[:, :], a["router_b"].to_broadcast([P, NE])).then_inc(s_bc, 16)
                sp.dma_start(rw[:, :, :], a["router_w"].rearrange("l (k p) n -> p (l k) n", p=P)).then_inc(s_rw, 16)
                sp.dma_start(xt[1][:, :], xsrc[1]).then_inc(s_x[1], 16)
                for g in range(3):
                    sp.dma_start(bias_f[32 * g:32 * g + 32, 0:2 * FF], a["b_gu"].rearrange("l e n -> (l e) n")).then_inc(s_bi, 16)
                    sp.dma_start(bias_f[32 * g:32 * g + 32, 2 * FF:], a["b_down"].rearrange("l e n -> (l e) n")).then_inc(s_bi, 16)
                sp.wait_ge(s_z, 1)
                sp.dma_start(acc[TX], junk[:, :]).then_inc(s_pad, 16)
                sp.dma_start(h2d[TX], junk[:, :]).then_inc(s_pad, 16)

                def tile(t, j, first, last):
                    sp.wait_ge(s_x2, t + 1)
                    sp.dma_start(acc[t], x2[j][:, :]).then_inc(s_sx[j], 16)
                    sp.wait_ge(s_h2, t + 1)
                    sp.dma_start(h2d[t], h2[j][:, :]).then_inc(s_sh[j], 16)
                tile(0, 0, True, False)
                with sp.Fori(0, TX // 2 - 1) as i:
                    for j in range(2):
                        t = 2 * i + 1 + j
                        sp.wait_ge(s_x2, t)
                        sp.dma_start(xt[j][:, :], xsrc[t + 1]).then_inc(s_x[j], 16)
                        tile(t, (1 + j) % 2, False, False)
                tile(TX - 1, 1, False, True)
                for j in range(2):
                    sp.wait_ge(s_sx[j], 16 * TX // 2)
                    sp.wait_ge(s_sh[j], 16 * TX // 2)

            @block.scalar
            def _(act):
                act.preload_act_table_set("natural_log_exp_and_others")

                def pre(t, j, first):
                    if not first:
                        act.wait_ge(s_tc, t)
                    act.activation(cat[j][:, 0:512], m.attn[:, t, :], ACT.Copy).then_inc(s_at, 1)
                    act.wait_ge(s_mv, t + 1)
                    act.activation(msln[:, :], msv[:, 0, :], ACT.Ln).then_inc(s_ca, 1)
                    act.wait_ge(s_ca, t + 1)
                    act.activation(msv[:, 1, :], msln[:, :], ACT.Exp, scale=-0.5).then_inc(s_mr, 1)

                def keep(t, j, first):
                    act.wait_ge(s_tc, t + 1)
                    act.activation(catT[j][:, 0:4, :], PS[:, 6, :].rearrange("p (k n) -> p k n", k=4), ACT.Copy).then_inc(s_tca, 1)

                def h2t(t):
                    act.wait_ge(s_th, t + 1)
                    act.activation(h2T[:, 0:4, :], PS[:, 4, :].rearrange("p (k n) -> p k n", k=4), ACT.Copy).then_inc(s_tha, 1)
                pre(0, 0, True)
                keep(0, 0, True)

                def tile(t, j, first, last):
                    if not last:
                        pre(t + 1, 1 - j, False)
                        keep(t + 1, 1 - j, False)
                    if not first:
                        h2t(t - 1)
                    act.wait_ge(s_x2, t + 1)
                    act.activation(junk[:, :], x2[j][:, :], ACT.Square, accum_out=xst[:, 0:1]).then_inc(s_ssq, 1)
                    act.wait_ge(s_xv, t + 1)
                    act.activation(xst[:, 3:4], xst[:, 1:2], ACT.Ln).then_inc(s_ln, 1)
                    act.wait_ge(s_ln, t + 1)
                    act.activation(xst[:, 2:3], xst[:, 3:4], ACT.Exp, scale=-0.5).then_inc(s_xr, 1)
                act.wait_ge(s_pad, 32)
                tiles(act, tile)
                h2t(TX - 1)

            @block.vector
            def _(dve):
                dve.memset(junk[:, :], 0.0).then_inc(s_z, 1)
                chain = Chain(dve, s_cd)
                dve.wait_ge(s_bc, 80)
                chain.done(dve.scalar_tensor_tensor(out=s2bc[:, :], in0=s2bc[:, :], scalar=1.0, in1=n2bc[:, :], op0=ALU.add, op1=ALU.mult))
                dve.wait_ge(s_bi, 96)
                chain.done(dve.tensor_copy(bhi[:, :], bias_f[:, :]))
                chain.done(dve.tensor_copy(m.bias3[0:32, :], bhi[0:32, :]))
                chain.done(dve.tensor_tensor(bias_f[:, :], bias_f[:, :], bhi[:, :], ALU.subtract))
                chain.done(dve.tensor_copy(bhi[:, :], bias_f[:, :]))
                chain.done(dve.tensor_copy(m.bias3[32:64, :], bhi[32:64, :]))
                chain.done(dve.tensor_tensor(bias_f[:, :], bias_f[:, :], bhi[:, :], ALU.subtract))
                chain.done(dve.tensor_copy(m.bias3[64:96, :], bias_f[64:96, :]))
                base = chain.n
                A, B = 9, 6

                def newton(c, v, r, tmp):
                    c.done(dve.tensor_tensor(tmp, r, r, ALU.mult))
                    c.done(dve.tensor_tensor(tmp, tmp, v, ALU.mult))
                    c.done(dve.tensor_scalar(tmp, tmp, -0.5, 1.5, ALU.mult, ALU.add))
                    c.done(dve.tensor_tensor(r, r, tmp, ALU.mult))

                def pre(c, t, j, first):
                    h = m.hsum[:, t, :]
                    h3 = h.rearrange("p (h n) -> p h n", h=MH)
                    c.done(dve.tensor_tensor(sq[:, :], h, h, ALU.mult))
                    c.done(dve.tensor_reduce(msv[:, 2, :], sq[:, :].rearrange("p (h n) -> p h n", h=MH), AX.X, ALU.add))
                    dve.tensor_scalar(msv[:, 0, :], msv[:, 2, :], 1.0 / MV, EPS, ALU.mult, ALU.add).then_inc(s_mv, 1)
                    c.done(dve.tensor_scalar(sg[:, :], m.og[:, t, :], 1.0, None, ALU.add))
                    c.done(dve.reciprocal(sg[:, :], sg[:, :]))
                    dve.wait_ge(s_mr, t + 1)
                    newton(c, msv[:, 0, :], msv[:, 1, :], msv[:, 3, :])
                    r = msv[:, 1, :].rearrange("p (h o) -> p h o", o=1).to_broadcast([P, MH, MV])
                    c.done(dve.tensor_tensor(sq[:, :].rearrange("p (h n) -> p h n", h=MH), h3, r, ALU.mult))
                    if not first:
                        dve.wait_ge(s_tc, t)
                    dve.tensor_tensor(cat[j][:, 512:1024], sq[:, :], sg[:, :], ALU.mult).then_inc(s_cat, 1)
                    dve.wait_ge(s_tc, t + 1)
                    for k in range(4, KD):
                        ins = dve.tensor_scalar(catT[j][:, k, :], PS[:, 7, (k - 4) * P:(k - 3) * P], m.cols[:, R_MN + k - 4:R_MN + k - 3], None, ALU.mult)
                    ins.then_inc(s_tcd, 1)

                def h2t(t):
                    dve.wait_ge(s_th, t + 1)
                    dve.tensor_copy(h2T[:, 4:8, :], PS[:, 5, :].rearrange("p (k n) -> p k n", k=4)).then_inc(s_thd, 1)
                    dve.wait_ge(s_lg, t + 1)
                    dve.tensor_tensor(m.logits[:, t, :], PS[:, 6, 0:NE], m.rbbc[:, :], ALU.add).then_inc(s_lgd, 1)

                def residual(c, t, j, first):
                    dve.wait_ge(s_mm, t + 1)
                    dve.wait_ge(s_x[j], 8 * (t - j) + 16)
                    if not first:
                        dve.wait_ge(s_sx[j], 8 * (t - j))
                        dve.wait_ge(s_sh[j], 8 * (t - j))
                    ps = PS[:, 2 * j:2 * j + 2, :].rearrange("p b n -> p (b n)")
                    c.done(dve.tensor_tensor(x2[j][:, :], ps, g1bc[:, :], ALU.mult))
                    dve.tensor_tensor(x2[j][:, :], x2[j][:, :], xt[j][:, :], ALU.add).then_inc(s_x2, 1)
                    dve.wait_ge(s_ssq, t + 1)
                    dve.tensor_scalar(xst[:, 1:2], xst[:, 0:1], 1.0 / D, EPS, ALU.mult, ALU.add).then_inc(s_xv, 1)
                    dve.wait_ge(s_xr, t + 1)
                    newton(c, xst[:, 1:2], xst[:, 2:3], xst[:, 4:5])
                    c.done(dve.scalar_tensor_tensor(out=h2[j][:, :], in0=x2[j][:, :], scalar=xst[:, 2:3], in1=s2bc[:, :], op0=ALU.mult, op1=ALU.mult))
                    dve.tensor_tensor(h2[j][:, :], h2[j][:, :], sh2bc[:, :], ALU.add).then_inc(s_h2, 1)
                pre(Chain(dve, s_cd, base), 0, 0, True)

                def tile(t, j, first, last):
                    c = Chain(dve, s_cd, base + A + t * (A + B))
                    if not last:
                        pre(c, t + 1, 1 - j, False)
                    if not first:
                        h2t(t - 1)
                    residual(c, t, j, first)
                    assert c.n == (B if last else A + B), c.n
                tiles(dve, tile)
                h2t(TX - 1)

            @block.tensor
            def _(pe):
                def cat_transposes(t, j, first):
                    pe.wait_ge(s_at, t + 1)
                    pe.wait_ge(s_cat, t + 1)
                    if not first:
                        pe.wait_ge(s_lgd, t - 1)
                        pe.wait_ge(s_tcd, t)
                        pe.wait_ge(s_tca, t)
                    for k in range(KD):
                        tr = pe.transpose(PS[:, 6 + k // 4, (k % 4) * P:(k % 4 + 1) * P], cat[j][:, k * P:(k + 1) * P], m.ident[:, :])
                    tr.then_inc(s_tc, 1)

                def project(t, j, n):
                    for k in range(KD):
                        mm = pe.matmul(PS[:, 2 * j + n, :], catT[j][:, k, :], w_out[:, k, 512 * n:512 * n + 512], start=(k == 0), stop=(k == KD - 1))
                    return mm

                def route(t, j, first, last):
                    pe.wait_ge(s_h2, t + 1)
                    for k in range(KD):
                        tr = pe.transpose(PS[:, 4 + k // 4, (k % 4) * P:(k % 4 + 1) * P], h2[j][:, k * P:(k + 1) * P], m.ident[:, :])
                    tr.then_inc(s_th, 1)
                    pe.wait_ge(s_tha, t + 1)
                    pe.wait_ge(s_thd, t + 1)
                    if not last:
                        pe.wait_ge(s_tca, t + 3)
                    for k in range(KD):
                        mm = pe.matmul(PS[:, 6, 0:NE], h2T[:, k, :], rw[:, k, :], start=(k == 0), stop=(k == KD - 1))
                    mm.then_inc(s_lg, 1)
                pe.sem_inc(s_lgd, 1)
                cat_transposes(0, 0, True)
                pe.wait_ge(s_wo, 16)
                pe.wait_ge(s_rw, 16)

                def tile(t, j, first, last):
                    pe.wait_ge(s_tca, t + 1)
                    pe.wait_ge(s_tcd, t + 1)
                    if not first:
                        pe.wait_ge(s_x2, t)
                    project(t, j, 0)
                    if not last:
                        cat_transposes(t + 1, 1 - j, False)
                    project(t, j, 1).then_inc(s_mm, 1)
                    if not first:
                        route(t - 1, 1 - j, False, last)
                tiles(pe, tile)
                route(TX - 1, 1, False, True)


NW = 12
NBLK = 64
GRID_W = 256


def phase_route(nc, a, m, PS):
    TK = TX * TOPK
    with semaphores(nc, "route") as sem:
        s_grid, s_cd = sem("index_constants_in"), sem("route_chain_dve")
        s_top, s_exp = sem("top_logits_ready"), sem("gate_exps_ready")
        s_mask, s_cum = sem("mask_ready"), sem("ranks_in_psum")
        s_pair, s_tab = sem("pair_codes_ready"), sem("tables_in_psum")
        items, end = m.run(SB0 + 4608, [
            ("grid", [P, GRID_W], F32), ("ones", [P, P], F32), ("upper", [P, P], F32),
            ("mx", [P, TX, 8], F32), ("ix", [P, TX, 8], U32), ("gt", [P, TX, TOPK], F32), ("gsum", [P, TX], F32),
            ("ixf", [P, TX, TOPK], F32), ("oh", [P, TK, NE], F32), ("ohc", [P, TK, NE], F32),
            ("mask", [P, TX, NE], F32), ("rank", [P, TX, NE], F32), ("tot", [P, TX + 1, NE], F32),
            ("nb", [P, NE], F32), ("b1", [P, NE], F32), ("b0", [P, NE], F32), ("code", [P, TK], F32),
            ("codei", [P, TK], I32), ("coli", [P, TK], I32), ("lanei", [P, TK], I32),
            ("colf", [P, TK], F32), ("lanef", [P, TK], F32),
            ("rowsel", [P, TK, P], F32), ("colsel", [P, TK, NBLK], F32), ("pairs", [P, TK, 2, NBLK], F32),
            ("cmp", [P, NBLK, NE], F32), ("blk", [P, NBLK], F32), ("tokf", [P, NBLK], F32), ("empty", [P, NBLK], F32),
            ("zeros", [P, NE], F32), ("used", [P, NE], F32)])
        (grid, ones, upper, mx, ix, gt, gsum, ixf, oh, ohc, mask, rank, tot, nb, b1, b0, code, codei, coli, lanei,
         colf, lanef, rowsel, colsel, pairs, cmp, blk, tokf, empty, zeros, used) = items
        assert end <= 198176
        (m.tokens, m.gates, m.table, m.esel), m.free = m.run(205472, [
            ("tokens", [P, NBLK], I32), ("gates", [P, NBLK], F32), ("table", [P, NBLK + NE + 1], I32), ("esel", [96, NBLK], BF16)])
        iota = grid[:, 0:P]
        tok1, pmod, pad1, lane = grid[:, P:P + TX], grid[:, 136:137], grid[:, 137:138], grid[:, 138:139]

        with nc.Block() as block:
            @block.sync
            def _(sp):
                sp.dma_start(grid[:, :], a["grid"]).then_inc(s_grid, 16)
                sp.wait_ge(s_grid, 16)

            @block.scalar
            def _(act):
                act.wait_ge(s_top, 1)
                act.activation(gt[:, :, :], gt[:, :, :], ACT.Exp).then_inc(s_exp, 1)

            @block.tensor
            def _(pe):
                pe.wait_ge(s_mask, 1)
                pe.matmul(PS[:, 0, 0:TX * NE], upper[:, :], mask[:, :, :], start=True, stop=True)
                pe.matmul(PS[:, 1, 0:TX * NE], ones[:, :], mask[:, :, :], start=True, stop=True).then_inc(s_cum, 1)
                pe.wait_ge(s_pair, 1)
                for j in range(TK):
                    mm = pe.matmul(PS[:, 2, 0:2 * NBLK], rowsel[:, j, :], pairs[:, j, :, :], start=(j == 0), stop=(j == TK - 1))
                mm.then_inc(s_tab, 1)

            @block.vector
            def _(dve):
                chain = Chain(dve, s_cd)

                def bc(ap, shape):
                    return ap.to_broadcast(shape)
                for t in range(TX):
                    ins = dve.max(out=mx[:, t, :], in_=m.logits[:, t, :])
                chain.done(ins)
                for t in range(TX):
                    ins = dve.max_index(out=ix[:, t, :], in_max=mx[:, t, :], in_values=m.logits[:, t, :])
                chain.done(ins)
                dve.tensor_tensor(gt[:, :, :], mx[:, :, 0:TOPK], bc(mx[:, :, 0:1], [P, TX, TOPK]), ALU.subtract).then_inc(s_top, 1)
                chain.done(dve.tensor_copy(ixf[:, :, :], ix[:, :, 0:TOPK]))
                dve.wait_ge(s_grid, 16)
                dve.memset(ones[:, :], 1.0)
                dve.tensor_scalar(upper[:, :], iota, lane, None, ALU.is_gt)
                chain.done(dve.tensor_tensor(oh[:, :, :], bc(grid[:, 0:NE].unsqueeze(1), [P, TK, NE]),
                                             bc(ixf.rearrange("p t k -> p (t k)").unsqueeze(2), [P, TK, NE]), ALU.is_equal))
                dve.tensor_reduce(mask[:, :, :], oh.rearrange("p (t k) e -> p t e k", k=TOPK), AX.X, ALU.add).then_inc(s_mask, 1)
                dve.wait_ge(s_exp, 1)
                chain.done(dve.tensor_reduce(gsum[:, :], gt[:, :, :], AX.X, ALU.add))
                chain.done(dve.reciprocal(gsum[:, :], gsum[:, :]))
                chain.done(dve.tensor_tensor(gt[:, :, :], gt[:, :, :], bc(gsum[:, :].unsqueeze(2), [P, TX, TOPK]), ALU.mult))
                dve.wait_ge(s_cum, 1)
                dve.memset(zeros[:, :], 0.0)
                chain.done(dve.memset(tot[:, 0, :], 0.0))
                for t in range(TX):
                    chain.done(dve.tensor_tensor(tot[:, t + 1, :], tot[:, t, :], PS[:, 1, t * NE:(t + 1) * NE], ALU.add))
                chain.done(dve.memset(nb[:, :], 1.0))
                for j in range(1, SEQ // P):
                    chain.done(dve.scalar_tensor_tensor(out=nb[:, :], in0=tot[:, TX, :], scalar=float(P * j), in1=nb[:, :],
                                                        op0=ALU.is_gt, op1=ALU.add))
                chain.done(dve.tensor_tensor_scan(b1[:, :], nb[:, :], zeros[:, :], 0.0, ALU.add, ALU.add))
                chain.done(dve.tensor_tensor(b0[:, :], b1[:, :], nb[:, :], ALU.subtract))
                chain.done(dve.tensor_tensor(rank[:, :, :], PS[:, 0, 0:TX * NE].rearrange("p (t e) -> p t e", e=NE),
                                             tot[:, 0:TX, :], ALU.add))
                for t in range(TX):
                    ins = dve.scalar_tensor_tensor(out=rank[:, t, :], in0=b0[:, :], scalar=float(P), in1=rank[:, t, :],
                                                   op0=ALU.mult, op1=ALU.add)
                chain.done(ins)
                for t in range(TX):
                    ins = dve.tensor_tensor(ohc[:, TOPK * t:TOPK * t + TOPK, :], oh[:, TOPK * t:TOPK * t + TOPK, :],
                                            bc(rank[:, t:t + 1, :], [P, TOPK, NE]), ALU.mult)
                chain.done(ins)
                chain.done(dve.tensor_reduce(code[:, :], ohc[:, :, :], AX.X, ALU.add))
                chain.done(dve.tensor_copy(codei[:, :], code[:, :]))
                dve.tensor_scalar(coli[:, :], codei[:, :], 7, None, ALU.arith_shift_right)
                chain.done(dve.tensor_scalar(lanei[:, :], codei[:, :], P - 1, None, ALU.bitwise_and))
                dve.tensor_copy(colf[:, :], coli[:, :])
                chain.done(dve.tensor_copy(lanef[:, :], lanei[:, :]))
                dve.tensor_tensor(rowsel[:, :, :], bc(iota.unsqueeze(1), [P, TK, P]), bc(lanef[:, :].unsqueeze(2), [P, TK, P]), ALU.is_equal)
                chain.done(dve.tensor_tensor(colsel[:, :, :], bc(grid[:, 0:NBLK].unsqueeze(1), [P, TK, NBLK]),
                                             bc(colf[:, :].unsqueeze(2), [P, TK, NBLK]), ALU.is_equal))
                for t in range(TX):
                    dve.tensor_scalar(pairs[:, TOPK * t:TOPK * t + TOPK, 0, :], colsel[:, TOPK * t:TOPK * t + TOPK, :],
                                      tok1[:, t:t + 1], None, ALU.mult)
                chain.done(dve.tensor_tensor(pairs[:, :, 1, :], colsel[:, :, :],
                                             bc(gt.rearrange("p t k -> p (t k)").unsqueeze(2), [P, TK, NBLK]), ALU.mult))
                dve.sem_inc(s_pair, 1)
                chain.done(dve.tensor_tensor(cmp[:, :, :], bc(grid[:, 0:NBLK].unsqueeze(2), [P, NBLK, NE]),
                                             bc(b1[:, :].unsqueeze(1), [P, NBLK, NE]), ALU.is_ge))
                chain.done(dve.tensor_reduce(blk[:, :], cmp[:, :, :], AX.X, ALU.add))
                chain.done(dve.tensor_scalar(blk[:, :], blk[:, :], float(NE - 1), None, ALU.min))
                chain.done(dve.tensor_scalar(used[:, :], b0[:, :], float(NW), float(-NW), ALU.mult, ALU.add))
                chain.done(dve.tensor_scalar(used[:, :], used[:, :], 0.0, None, ALU.max))
                dve.tensor_copy(m.table[:, 0:NBLK], blk[:, :])
                dve.tensor_copy(m.table[:, NBLK:NBLK + NE], used[:, :])
                dve.tensor_copy(m.table[:, NBLK + NE:NBLK + NE + 1], b1[:, NE - 1:NE])
                dve.tensor_scalar(m.esel[:, :], blk[0:96, :], pmod[0:96, :], None, ALU.is_equal)
                dve.wait_ge(s_tab, 1)
                dve.tensor_copy(m.gates[:, :], PS[:, 2, NBLK:2 * NBLK])
                chain.done(dve.tensor_scalar(empty[:, :], PS[:, 2, 0:NBLK], 0.0, None, ALU.is_equal))
                chain.done(dve.scalar_tensor_tensor(out=tokf[:, :], in0=empty[:, :], scalar=pad1, in1=PS[:, 2, 0:NBLK],
                                                    op0=ALU.mult, op1=ALU.add))
                chain.done(dve.tensor_scalar(m.tokens[:, :], tokf[:, :], -1.0, None, ALU.add))


def phase_experts(nc, a, m, PS):
    H = FF // 2
    SLOTS = 4
    ALPHA = 1.702
    G0, DN, TR = 0, 4, 6
    nc.clear_and_free_semaphores(RELEASED)
    nc.all_engine_barrier()
    RELEASED.clear()
    with semaphores(nc, "experts") as sem:
        s_w = [sem(f"weights_in{c}") for c in range(NW)]
        s_hi, s_lo, s_used, s_gb = sem("chunk_hi_ready"), sem("chunk_lo_ready"), sem("chunks_used"), sem("g2_rows_in")
        s_xg, s_sc = sem("rows_gathered"), sem("rows_added")
        s_step, s_yf, s_pc, s_cd = sem("indirect_dma_may_start"), sem("y_free"), sem("index_copied"), sem("expert_chain_dve")
        s_sel, s_g, s_sg = sem("selector_ready"), sem("gate_clamped"), sem("silu_ready")
        s_h, s_tp, s_eh, s_el = sem("hidden_ready"), sem("transposed"), sem("transpose_hi_kept"), sem("transpose_lo_kept")
        s_bias, s_y = sem("selector_used"), sem("y_ready")
        items, end = m.run(SB0 + 4608, [(f"w{c}", [P, 2048], F32) for c in range(NW)]
                           + [(f"wh{c}", [P, 2048], F32R) for c in range(SLOTS)] + [(f"wl{c}", [P, 2048], F32R) for c in range(SLOTS)]
                           + [("xTh", [P, KD, P], F32R), ("xTl", [P, KD, P], F32R), ("hTh", [P, FF // P, P], F32R),
                              ("idxg", [P, 1], I32), ("idxs", [P, 1], I32), ("gcol", [P, 1], F32), ("sel", [96, P], BF16)])
        w, wh, wl = items[:NW], items[NW:NW + SLOTS], items[NW + SLOTS:NW + 2 * SLOTS]
        xTh, xTl, hTh, idxg, idxs, gcol, sel = items[NW + 2 * SLOTS:]
        assert end <= 198176
        (hTl, xg, hid, gc, sgm, g2bc), end = m.run(m.free, [
            ("hTl", [P, FF // P, P], F32R), ("xg", [P, D], F32), ("hid", [P, FF], F32), ("gc", [P, H], F32), ("sgm", [P, H], F32),
            ("g2bc", [P, D], F32)])
        assert end <= 229344
        y = hid
        xT, hT = (xTh, xTl), (hTh, hTl)
        wv = [w[c].rearrange("p (k g n) -> p k g n", k=2, g=2) for c in range(NW)]
        whv, wlv = ([s.rearrange("p (k g n) -> p k g n", k=2, g=2) for s in ws] for ws in (wh, wl))
        gu_src = a["w_gu"].rearrange("l e (k p) (g j n) -> (l e) j p k g n", p=P, g=2, j=2)
        dn_src = a["w_down"].rearrange("l e (k p) (g n) -> (l e) p k g n", p=P, g=2)
        T_E, T_B, T_N = 0, NBLK, NBLK + NE

        def count(eng):
            return eng.value_load(m.table[0:1, T_N:T_N + 1], min_val=NE, max_val=NBLK - 1)

        def expert(eng, i):
            return eng.value_load(m.table[0:1, bass.ds(i, 1)], min_val=0, max_val=NE - 1)

        def bank4(half):
            return PS[:, TR + half, :].rearrange("p (q n) -> p q n", q=4)

        with nc.Block() as block:
            @block.sync
            def _(sp):
                def load(e, c):
                    for g in range(2):
                        if c < 8:
                            src = gu_src[e, c // 4][:, 2 * (c % 4):2 * (c % 4) + 2, g, :]
                        else:
                            src = dn_src[e][:, 2 * (c - 8):2 * (c - 8) + 2, g, :]
                        sp.dma_start(wv[c][:, :, g, :], src).then_inc(s_w[c], 16)
                sp.dma_start(g2bc[:, :], a["mod"][0:1, R_G2 * P:R_G2 * P + D].to_broadcast([P, D])).then_inc(s_gb, 16)
                for c in range(NW):
                    load(0, c)
                with sp.Fori(1, NE) as e:
                    used = sp.value_load(m.table[0:1, bass.ds(e + T_B, 1)], min_val=0, max_val=NW * (NBLK - 2))
                    for c in range(NW):
                        sp.wait_ge(s_lo, used + (c + 1))
                        load(e, c)
                sp.wait_ge(s_gb, 16)

            @block.gpsimd
            def _(pool):
                n = count(pool)

                def gather():
                    pool.indirect_dma_start(out=xg[:, :], out_offset=None, in_=a["h2"],
                                            in_offset=bass.IndirectOffsetOnAxis(ap=idxg[:, 0:1], axis=0)).then_inc(s_xg, 16)
                pool.sem_inc(s_yf, 1)
                pool.tensor_copy(idxg[:, :], m.tokens[:, 0:1]).then_inc(s_pc, 1)
                pool.wait_ge(s_pc, 1)
                gather()
                with pool.Fori(0, n) as i:
                    pool.wait_ge(s_tp, 4 * i + 2)
                    pool.tensor_copy(idxg[:, :], m.tokens[:, bass.ds(i + 1, 1)]).then_inc(s_pc, 1)
                    pool.tensor_copy(idxs[:, :], m.tokens[:, bass.ds(i, 1)]).then_inc(s_pc, 1)
                    pool.wait_ge(s_pc, 2 * i + 3)
                    pool.sem_inc(s_step, 1)
                    gather()
                    pool.wait_ge(s_y, i + 2)
                    pool.sem_inc(s_step, 1)
                    pool.indirect_dma_start(out=a["acc"], out_offset=bass.IndirectOffsetOnAxis(ap=idxs[:, 0:1], axis=0),
                                            in_=y[:, :], in_offset=None, compute_op=ALU.add).then_inc(s_sc, 16)
                    pool.wait_ge(s_sc, 16 * i + 16)
                    pool.sem_inc(s_yf, 1)
                pool.wait_ge(s_xg, n * 16 + 16)

            @block.tensor
            def _(pe):
                n = count(pe)

                def transposes(src, half):
                    for q in range(4):
                        k = 4 * half + q
                        ins = pe.transpose(PS[:, TR + half, q * P:(q + 1) * P], src[:, k * P:(k + 1) * P], m.ident[:, :])
                    ins.then_inc(s_tp, 1)

                def product(bank, xs, k, slot, kk, last):
                    for op, ws in ((xs[0], whv), (xs[0], wlv), (xs[1], whv)):
                        for g in range(2):
                            mm = pe.matmul(PS[:, bank + g, :], op[:, k, :], ws[slot][:, kk, g, :], start=False,
                                           stop=(last and op is xs[1]))
                    return mm
                pe.wait_ge(s_xg, 16)
                transposes(xg, 0)
                transposes(xg, 1)
                with pe.Fori(0, n) as i:
                    pe.wait_ge(s_sel, i + 1)

                    def bias(bank, col):
                        return pe.matmul(PS[:, bank, :], sel[:, :], m.bias3[:, col:col + 512], start=True, stop=False)

                    def step(c, kk):
                        if kk == 0:
                            pe.wait_ge(s_lo, i * NW + (c + 1))
                        if c < 8:
                            mm = product(G0 + 2 * (c // 4), xT, 2 * (c % 4) + kk, c % SLOTS, kk, c % 4 == 3 and kk == 1)
                        else:
                            mm = product(DN, hT, 2 * (c - 8) + kk, c % SLOTS, kk, c == NW - 1 and kk == 1)
                        if kk == 1:
                            mm.then_inc(s_used, 1)

                    def chunk(c):
                        step(c, 0)
                        step(c, 1)
                    bias(G0, 0)
                    bias(G0 + 1, FF)
                    pe.wait_ge(s_el, 4 * i + 1)
                    chunk(0)
                    chunk(1)
                    pe.wait_ge(s_el, 4 * i + 2)
                    chunk(2)
                    chunk(3)
                    bias(G0 + 2, H)
                    bias(G0 + 3, FF + H)
                    chunk(4)
                    chunk(5)
                    chunk(6)
                    pe.wait_ge(s_h, 2 * i + 1)
                    transposes(hid, 0)
                    chunk(7)
                    pe.wait_ge(s_y, i + 1)
                    bias(DN, 2 * FF)
                    bias(DN + 1, 2 * FF + 512).then_inc(s_bias, 1)
                    pe.wait_ge(s_el, 4 * i + 3)
                    chunk(8)
                    step(9, 0)
                    pe.wait_ge(s_h, 2 * i + 2)
                    transposes(hid, 1)
                    step(9, 1)
                    pe.wait_ge(s_xg, 16 * i + 32)
                    transposes(xg, 0)
                    pe.wait_ge(s_el, 4 * i + 4)
                    chunk(10)
                    transposes(xg, 1)
                    chunk(11)

            @block.scalar
            def _(act):
                n = count(act)
                act.preload_act_table_set("silu_and_others")

                def keep(dst, half, which, scale=1.0):
                    act.wait_ge(s_tp, which)
                    act.activation(dst[0][:, 4 * half:4 * half + 4, :], bank4(half), ACT.Copy, scale=scale).then_inc(s_eh, 1)

                def split(c, e, used):
                    act.wait_ge(s_w[c], e * 32 + 32)
                    if used is not None:
                        act.wait_ge(s_used, used)
                    act.activation(wh[c % SLOTS][:, :], w[c][:, :], ACT.Copy).then_inc(s_hi, 1)
                keep(xT, 0, 1)
                keep(xT, 1, 2)
                for c in range(SLOTS):
                    split(c, 0, None)
                with act.Fori(0, n) as i:
                    e = expert(act, i)
                    e1 = expert(act, i + 1)

                    def this(*cs):
                        for c in cs:
                            split(c, e, i * NW + (c + 1 - SLOTS))

                    def following(c):
                        split(c, e1, i * NW + (c + 1 + NW - SLOTS))

                    def silu(j):
                        act.wait_ge(s_g, 2 * i + (j + 1))
                        act.activation(sgm[:, :], gc[:, :], ACT.Silu).then_inc(s_sg, 1)
                    this(4, 5, 6)
                    silu(0)
                    this(7, 8, 9)
                    keep(hT, 0, 4 * i + 3, 1.0 / ALPHA)
                    this(10)
                    silu(1)
                    this(11)
                    keep(hT, 1, 4 * i + 4, 1.0 / ALPHA)
                    following(0)
                    keep(xT, 0, 4 * i + 5)
                    following(1)
                    keep(xT, 1, 4 * i + 6)
                    following(2)
                    following(3)

            @block.vector
            def _(dve):
                n = count(dve)

                def keep(dst, half, which, scale=1.0):
                    dve.wait_ge(s_eh, which)
                    dve.scalar_tensor_tensor(out=dst[1][:, 4 * half:4 * half + 4, :], in0=bank4(half), scalar=scale,
                                             in1=dst[0][:, 4 * half:4 * half + 4, :].bitcast(F32), op0=ALU.mult,
                                             op1=ALU.subtract).then_inc(s_el, 1)

                def split(c, done):
                    dve.wait_ge(s_hi, done)
                    dve.tensor_tensor(wl[c % SLOTS][:, :], w[c % NW][:, :], wh[c % SLOTS][:, :].bitcast(F32), ALU.subtract).then_inc(s_lo, 1)
                dve.sem_inc(s_y, 1)
                dve.tensor_copy(sel[:, :], m.esel[:, 0:1].to_broadcast([96, P])).then_inc(s_sel, 1)
                keep(xT, 0, 1)
                keep(xT, 1, 2)
                for c in range(SLOTS):
                    split(c, c + 1)
                dve.wait_ge(s_gb, 16)
                with dve.Fori(0, n) as i:
                    chain = Chain(dve, s_cd, 3 * i)

                    def this(*cs):
                        for c in cs:
                            split(c, i * NW + (c + 1))

                    def hidden(j):
                        dve.wait_ge(s_used, i * NW + (4 * j + 4))
                        dve.tensor_scalar(gc[:, :], PS[:, G0 + 2 * j, :], 7.0, ALPHA, ALU.min, ALU.mult).then_inc(s_g, 1)
                        hj = hid[:, j * H:(j + 1) * H]
                        if j == 0:
                            dve.wait_ge(s_yf, i + 1)
                        chain.done(dve.tensor_scalar(hj, PS[:, G0 + 2 * j + 1, :], 7.0, -7.0, ALU.min, ALU.max))
                        dve.wait_ge(s_sg, 2 * i + (j + 1))
                        dve.scalar_tensor_tensor(out=hj, in0=hj, scalar=1.0, in1=sgm[:, :], op0=ALU.add, op1=ALU.mult).then_inc(s_h, 1)
                    this(4, 5, 6)
                    hidden(0)
                    this(7, 8, 9)
                    keep(hT, 0, 4 * i + 3, 1.0 / ALPHA)
                    this(10)
                    hidden(1)
                    dve.wait_ge(s_bias, i + 1)
                    dve.tensor_copy(sel[:, :], m.esel[:, bass.ds(i + 1, 1)].to_broadcast([96, P])).then_inc(s_sel, 1)
                    chain.done(dve.tensor_copy(gcol[:, :], m.gates[:, bass.ds(i, 1)]))
                    this(11)
                    keep(hT, 1, 4 * i + 4, 1.0 / ALPHA)
                    this(NW)
                    keep(xT, 0, 4 * i + 5)
                    this(NW + 1)
                    keep(xT, 1, 4 * i + 6)
                    this(NW + 2, NW + 3)
                    dve.wait_ge(s_used, i * NW + NW)
                    dve.scalar_tensor_tensor(out=y.rearrange("p (g n) -> p g n", g=2), in0=PS[:, DN:DN + 2, :], scalar=gcol[:, :],
                                             in1=g2bc.rearrange("p (g n) -> p g n", g=2), op0=ALU.mult, op1=ALU.mult).then_inc(s_y, 1)


def phase_final(nc, a, m, PS):
    with semaphores(nc, "final") as sem:
        s_in, s_g, s_out = sem("rows_in"), sem("final_gain_in"), [sem(f"out_stored{j}") for j in range(4)]
        s_ss, s_v, s_r, s_cd, s_o = sem("square_sum"), sem("variance"), sem("rstd_raw"), sem("final_chain"), sem("out_ready")
        s_ln = sem("log_ready")
        items, end = m.run(SB0 + 4608, [
            ("rows", [P, TX, D], F32), ("outs", [P, TX, D], F32), ("fgain", [P, D], F32), ("sqj", [P, D], F32),
            ("ss", [P, TX], F32), ("var", [P, TX], F32), ("rs", [P, TX], F32), ("rt", [P, TX], F32), ("lg", [P, TX], F32)])
        rows, outs, fgain, sqj, ss, var, rs, rt, lg = items
        with nc.Block() as block:
            @block.sync
            def _(sp):
                sp.dma_start(fgain[:, :], a["final_norm_g"].unsqueeze(0).to_broadcast([P, D])).then_inc(s_g, 16)
                sp.dma_start(rows[:, :, :], a["acc"][0:SEQ, :].rearrange("(t p) d -> p t d", p=P)).then_inc(s_in, 16)
                for t in range(TX):
                    sp.wait_ge(s_o, t + 1)
                    sp.dma_start(a["out"][0, t * P:(t + 1) * P, :], outs[:, t, :]).then_inc(s_out[t % 4], 16)
                for j in range(4):
                    sp.wait_ge(s_out[j], 16 * TX // 4)

            @block.scalar
            def _(act):
                act.wait_ge(s_in, 16)
                for t in range(TX):
                    act.activation(sqj[:, :], rows[:, t, :], ACT.Square, accum_out=ss[:, t:t + 1]).then_inc(s_ss, 1)
                    act.wait_ge(s_ss, t + 1)
                act.wait_ge(s_v, 1)
                act.activation(lg[:, :], var[:, :], ACT.Ln).then_inc(s_ln, 1)
                act.wait_ge(s_ln, 1)
                act.activation(rs[:, :], lg[:, :], ACT.Exp, scale=-0.5).then_inc(s_r, 1)

            @block.vector
            def _(dve):
                chain = Chain(dve, s_cd)
                dve.wait_ge(s_ss, TX)
                dve.tensor_scalar(var[:, :], ss[:, :], 1.0 / D, EPS, ALU.mult, ALU.add).then_inc(s_v, 1)
                dve.wait_ge(s_r, 1)
                chain.done(dve.tensor_tensor(rt[:, :], rs[:, :], rs[:, :], ALU.mult))
                chain.done(dve.tensor_tensor(rt[:, :], rt[:, :], var[:, :], ALU.mult))
                chain.done(dve.tensor_scalar(rt[:, :], rt[:, :], -0.5, 1.5, ALU.mult, ALU.add))
                chain.done(dve.tensor_tensor(rs[:, :], rs[:, :], rt[:, :], ALU.mult))
                dve.wait_ge(s_g, 16)
                for t in range(TX):
                    dve.scalar_tensor_tensor(out=outs[:, t, :], in0=rows[:, t, :], scalar=rs[:, t:t + 1], in1=fgain[:, :],
                                             op0=ALU.mult, op1=ALU.mult).then_inc(s_o, 1)


SB0 = 16512


def build_program(nc, a, last=9):
    m = Memory(nc)
    RELEASED.clear()
    a["mod"] = nc.dram_tensor("mod_dram", (2, 6 * D), F32).ap()
    a["acc"] = nc.dram_tensor("acc_dram", (SEQ + P, D), F32).ap()
    a["h2"] = nc.dram_tensor("h2_dram", (SEQ + P, D), F32).ap()
    (m.ident, m.cols, m.s1x, m.s1c, m.s2, m.eps, m.bgates, m.cs_tab, m.sn_tab), end = m.run(SB0, [
        ("ident", [P, P], F32), ("cols", [P, N_COLS], F32), ("s1x", [P, KD], F32), ("s1c", [P, KD], F32),
        ("s2", [P, KD], F32), ("eps", [P, 1], F32), ("bgates", [P, 16], F32),
        ("cs_tab", [P, NT, ROPE], F32), ("sn_tab", [P, NT, ROPE], F32)])
    (m.og, m.vaug, m.mk, m.mqT, m.cqT, m.ckvT, m.g16), end = m.run(SB0 + 4608, [
        ("og", [P, TX, MH * MV], F32), ("vaug", [P, NT, MH, MV + 1], F32), ("mk", [P, NT, MH * MQK], F32),
        ("mqT", [P, 2, SEQ], F32), ("cqT", [P, QL // P, SEQ], F32), ("ckvT", [P, KVL // P, KEYS], F32),
        ("g16", [P, NT, 4 * MH], F32)])
    m.W = end
    (m.w_in,), m.R1 = m.run(end, [("w_in", [P, KD, IN_W], F32)])
    m.kT = [m.at(f"kT{i}", [NOPE + ROPE, KEYS], F32, m.R1 + 32768 + i * 4 * KEYS) for i in range(2)]
    m.kT0 = m.kT[0]
    with nc.psum_tensor("PS", [P, 8, 512], F32) as PS:
        for n, phase in enumerate(PHASES):
            if n < last:
                phase(nc, a, m, PS)
    return m
PHASES = [phase_modulation, phase_projection, phase_mlstm, phase_attention, phase_output, phase_route, phase_experts, phase_final]


def rope_tables():
    t = np.arange(SEQ)
    row, col = (t // 64).astype(np.float32), (t % 64).astype(np.float32)
    pairs = ROPE // 4
    inv = (np.float32(10000.0) ** (-np.arange(pairs, dtype=np.float32) / np.float32(pairs))).astype(np.float32)
    ang = np.concatenate([row[:, None] * inv, col[:, None] * inv], axis=-1)
    cos, sin = np.cos(ang).astype(np.float32), np.sin(ang).astype(np.float32)
    cs = np.concatenate([np.ones((CTX, ROPE), np.float32), np.concatenate([cos, cos], 1)])
    sn = np.concatenate([np.zeros((CTX, ROPE), np.float32), np.concatenate([-sin, sin], 1)])
    csT = np.ascontiguousarray(np.concatenate([cos, cos], 1).T * np.float32(SCALE))
    snT = np.ascontiguousarray(np.concatenate([-sin, sin], 1).T * np.float32(SCALE))
    return cs, sn, csT, snT


def index_constants():
    grid = np.zeros((P, GRID_W), np.float32)
    lane = np.arange(P, dtype=np.float32)
    grid[:, 0:P] = lane[None, :]
    grid[:, P:P + TX] = 1 + lane[:, None] + P * np.arange(TX, dtype=np.float32)[None, :]
    grid[:, P + TX], grid[:, P + TX + 1], grid[:, P + TX + 2] = lane % NE, SEQ + 1 + lane, lane
    return grid


_INS = ["x", "c", "ctx", "c_ctx", "w_mod", "b_mod", "norm1_g", "w_in", "b_gates", "q_norm_g", "w_uq", "kv_norm_g",
        "w_ukv", "m_norm_g", "w_out", "norm2_g", "router_w", "router_b", "w_gu", "b_gu", "w_down", "b_down",
        "final_norm_g"]


def kernel(**inputs):
    import numpy as _np
    import concourse.bacc as _bacc
    from concourse import mybir as _mybir
    from concourse.bass_utils import run_bass_kernel_spmd as _run

    nc = _bacc.Bacc("TRN2", target_bir_lowering=False, num_devices=1)
    arrays, aps = {}, {}
    given = {n: _np.ascontiguousarray(inputs[n]) for n in _INS}
    given.update(zip(("cs_tab", "sn_tab", "cs_tabT", "sn_tabT"), rope_tables()))
    given["grid"] = index_constants()
    for name, v in given.items():
        arrays[f"in_{name}_dram"] = v
        aps[name] = nc.dram_tensor(f"in_{name}_dram", v.shape, _mybir.dt.from_np(v.dtype), kind="ExternalInput").ap()
    aps["out"] = nc.dram_tensor("out_0_dram", (1, SEQ, D), F32, kind="ExternalOutput").ap()
    build_program(nc, aps)
    r = _run(nc, [arrays], core_ids=[0])
    return r.results[0]["out_0_dram"]
```

```python
from contextlib import contextmanager

import numpy as np
import concourse.bass as bass
from concourse import mybir

F32 = mybir.dt.float32
F32R = mybir.dt.float32r
BF16 = mybir.dt.bfloat16
I32 = mybir.dt.int32
U32 = mybir.dt.uint32
ALU = mybir.AluOpType
ACT = mybir.ActivationFunctionType
AX = mybir.AxisListType

P = 128
D = 1024
KD = D // P
SEQ = 1024
CTX = 256
TX = SEQ // P
TC = CTX // P
NT = TC + TX
KEYS = SEQ + CTX
EPS = 1e-6
QL, KVL, NOPE, ROPE, VH, HEADS = 384, 256, 64, 32, 64, 8
MH, MQK, MV = 4, 64, 128
NE, TOPK, FF = 32, 4, 1024
SCALE = float(NOPE + ROPE) ** -0.5
C_Q, C_KV, C_KR = 0, QL, QL + KVL
C_MQ = C_KR + ROPE
C_MK = C_MQ + MH * MQK
C_MV = C_MK + MH * MQK
C_O = C_MV + MH * MV
C_G = C_O + MH * MV
IN_W = C_G + 4 * MH
R_SH1, R_SC1, R_G1, R_SH2, R_SC2, R_G2 = (KD * i for i in range(6))
R_CSH1, R_CSC1 = 48, 56
R_N1, R_N2, R_QN, R_KVN, R_MN = 64, 72, 80, 83, 85
N_COLS = 89


RELEASED = []


@contextmanager
def semaphores(nc, phase):
    taken = []

    def sem(name):
        taken.append(nc.alloc_semaphore(f"{phase}_{name}"))
        return taken[-1]
    yield sem
    RELEASED.extend(taken)


class Chain:

    def __init__(self, eng, sem, start=0):
        self.eng, self.sem, self.start, self.n = eng, sem, start, 0

    def done(self, ins):
        ins.then_inc(self.sem, 1)
        self.n += 1
        self.eng.wait_ge(self.sem, self.start + self.n)


class Memory:

    def __init__(self, nc):
        self.nc = nc

    def at(self, name, shape, dt, offset):
        return self.nc.alloc_sbuf_tensor_at(name, shape, dt, offset=offset)

    def run(self, offset, items):
        out = []
        for name, shape, dt in items:
            out.append(self.at(name, shape, dt, offset))
            size = int(np.prod(shape[1:])) * (2 if dt == BF16 else 4)
            offset += -(-size // 32) * 32
        return out, offset


def phase_modulation(nc, a, m, PS):
    NCH = 12
    with semaphores(nc, "modulation") as sem:
        s_rows, s_id = sem("c_rows_in"), sem("ident_ready")
        s_cd, s_ct, s_exp = sem("mod_chain_dve"), sem("c_cols_ready"), sem("exp_ready")
        s_silu, s_w0, s_w1 = sem("silu_ready"), sem("wmod_in0"), sem("wmod_in1")
        s_b0, s_b1, s_mm = sem("bmod_in0"), sem("bmod_in1"), sem("mod_chunk_done")
        s_row, s_st0, s_st1 = sem("mod_row_ready"), sem("mod_row_stored0"), sem("mod_row_stored1")
        s_v, s_vt, s_ld = sem("vec_rows_in"), sem("cols_transposed"), sem("loads_done")
        s_w, s_b, s_st = (s_w0, s_w1), (s_b0, s_b1), (s_st0, s_st1)
        (crow, ccol, cexp, csilu), _ = m.run(m.R1 + 2 * 16384, [
            ("crow", [16, P], F32), ("ccol", [P, 16], F32), ("cexp", [P, 16], F32), ("csilu", [P, 16], F32)])
        wch = [m.at(f"wmod{i}", [P, KD, 512], F32, m.R1 + 16384 * i) for i in range(2)]
        (bch0, bch1, row0, row1, vrows), _ = m.run(m.R1 + 2 * 16384 + 1024, [
            ("bch0", [2, 512], F32), ("bch1", [2, 512], F32), ("mrow0", [2, 512], F32), ("mrow1", [2, 512], F32),
            ("vrows", [N_COLS, P], F32)])
        bch, row = (bch0, bch1), (row0, row1)
        wsrc = a["w_mod"].rearrange("l (k p) n -> p (l k) n", p=P)
        with nc.Block() as block:
            @block.sync
            def _(sp):
                sp.dma_start(crow[0:KD, :], a["c"].rearrange("a (k p) -> (a k) p", p=P)).then_inc(s_rows, 16)
                sp.dma_start(crow[KD:2 * KD, :], a["c_ctx"].rearrange("(k p) -> k p", p=P)).then_inc(s_rows, 16)
                def load(j, i):
                    sp.dma_start(wch[i][:, :, :], wsrc[:, :, bass.ds(j * 512, 512)]).then_inc(s_w[i], 16)
                    sp.dma_start(bch[i][0:1, :], a["b_mod"][:, bass.ds(j * 512, 512)]).then_inc(s_b[i], 16)
                    sp.dma_start(bch[i][1:2, :], a["b_mod"][:, bass.ds(j * 512, 512)]).then_inc(s_b[i], 16)
                load(0, 0)
                load(1, 1)
                def refill(h, i):
                    sp.wait_ge(s_row, 2 * h + i - 1)
                    load(2 * h + i, i)
                w_in_src = a["w_in"].rearrange("l (k p) n -> (l k) p n", p=P)
                with sp.Fori(1, 1 + KD // 2) as h:
                    for i in range(2):
                        refill(h, i)
                        sp.dma_start(m.w_in[:, bass.ds(2 * h + (i - 2), 1), :], w_in_src[2 * h + (i - 2)].unsqueeze(1)).then_inc(s_ld, 16)
                for h in range(1 + KD // 2, NCH // 2):
                    for i in range(2):
                        refill(h, i)
                sp.dma_start(m.bgates[:, :], a["b_gates"].to_broadcast([P, 16])).then_inc(s_ld, 16)
                sp.dma_start(m.cs_tab[:, :, :], a["cs_tab"].rearrange("(t p) n -> p t n", p=P)).then_inc(s_ld, 16)
                sp.dma_start(m.sn_tab[:, :, :], a["sn_tab"].rearrange("(t p) n -> p t n", p=P)).then_inc(s_ld, 16)
                sp.wait_ge(s_row, NCH)
                sp.wait_ge(s_st0, 8 * NCH)
                sp.wait_ge(s_st1, 8 * NCH)
                md = a["mod"]
                sp.dma_start(vrows[0:48, :], md[0:1, :].rearrange("a (r p) -> (a r) p", p=P)).then_inc(s_v, 16)
                sp.dma_start(vrows[48:64, :], md[1:2, 0:2 * D].rearrange("a (r p) -> (a r) p", p=P)).then_inc(s_v, 16)
                for name, r in (("norm1_g", R_N1), ("norm2_g", R_N2), ("q_norm_g", R_QN), ("kv_norm_g", R_KVN), ("m_norm_g", R_MN)):
                    src = a[name].rearrange("l (r p) -> (l r) p", p=P)
                    sp.dma_start(vrows[r:r + src.shape[0], :], src).then_inc(s_v, 16)
                sp.wait_ge(s_ld, 16 * (KD + 3))

            @block.gpsimd
            def _(pool):
                pool.memset(m.ident[:, :], 0.0).then_inc(s_id, 1)
                pool.wait_ge(s_id, 1)
                pool.affine_select(out=m.ident[:, :], in_=m.ident[:, :], compare_op=ALU.not_equal, fill=1.0,
                                   base=0, pattern=[[-1, P]], channel_multiplier=1).then_inc(s_id, 1)

            @block.vector
            def _(dve):
                chain = Chain(dve, s_cd)
                dve.memset(m.eps[:, :], EPS).then_inc(s_cd, 1)
                chain.n = 1
                dve.wait_ge(s_ct, 1)
                chain.done(dve.tensor_copy(ccol[:, :], PS[:, 2, 0:16]))
                dve.sem_inc(s_silu, 1)
                dve.wait_ge(s_exp, 1)
                chain.done(dve.tensor_scalar(cexp[:, :], cexp[:, :], 1.0, None, ALU.add))
                chain.done(dve.reciprocal(cexp[:, :], cexp[:, :]))
                dve.tensor_tensor(csilu[:, :], ccol[:, :], cexp[:, :], ALU.mult).then_inc(s_silu, 1)

                def finish(j, i, first):
                    dve.wait_ge(s_mm, j + 1)
                    dve.wait_ge(s_b[i], 32 * (j // 2 + 1) if first else 32 * j2 + 32)
                    if not first:
                        dve.wait_ge(s_st[i], 16 * j2)
                    dve.tensor_tensor(row[i][:, :], PS[0:2, i, :], bch[i][:, :], ALU.add).then_inc(s_row, 1)
                for i in range(2):
                    finish(i, i, True)
                with dve.Fori(1, NCH // 2) as j2:
                    for i in range(2):
                        finish(2 * j2 + i, i, False)
                dve.wait_ge(s_vt, 1)
                chain.done(dve.tensor_copy(m.cols[:, :], PS[:, 3, 0:N_COLS]))
                for dst, g, sc in ((m.s1x, R_N1, R_SC1), (m.s1c, R_N1, R_CSC1), (m.s2, R_N2, R_SC2)):
                    chain.done(dve.scalar_tensor_tensor(out=dst[:, :], in0=m.cols[:, sc:sc + KD], scalar=1.0,
                                                        in1=m.cols[:, g:g + KD], op0=ALU.add, op1=ALU.mult))

            @block.tensor
            def _(pe):
                pe.wait_ge(s_id, 2)
                pe.wait_ge(s_rows, 32)
                pe.transpose(PS[:, 2, 0:16], crow[:, :], m.ident[0:16, 0:16]).then_inc(s_ct, 1)
                pe.wait_ge(s_silu, 2)

                def chunk(j, i, first):
                    pe.wait_ge(s_w[i], 16 if first else 16 * j2 + 16)
                    if not first:
                        pe.wait_ge(s_row, j - 1)
                    for k in range(KD):
                        mm = pe.matmul(PS[0:2, i, :], csilu[:, k:16:KD], wch[i][:, k, :], start=(k == 0), stop=(k == KD - 1))
                    mm.then_inc(s_mm, 1)
                for i in range(2):
                    chunk(i, i, True)
                with pe.Fori(1, NCH // 2) as j2:
                    for i in range(2):
                        chunk(2 * j2 + i, i, False)
                pe.wait_ge(s_v, 7 * 16)
                pe.transpose(PS[:, 3, 0:N_COLS], vrows[:, :], m.ident[0:N_COLS, 0:N_COLS]).then_inc(s_vt, 1)

            @block.scalar
            def _(act):
                act.wait_ge(s_silu, 1)
                act.activation(cexp[:, :], PS[:, 2, 0:16], ACT.Exp, scale=-1.0).then_inc(s_exp, 1)

                def store(j, i):
                    act.wait_ge(s_row, j + 1)
                    act.dma_start(a["mod"][:, bass.ds(j * 512, 512)], row[i][:, :]).then_inc(s_st[i], 16)
                with act.Fori(0, NCH // 2) as j2:
                    for i in range(2):
                        store(2 * j2 + i, i)


def phase_projection(nc, a, m, PS):
    with semaphores(nc, "projection") as sem:
        s_x = [sem("xtile_in0"), sem("xtile_in1")]
        s_ca, s_cd = sem("proj_chain_act"), sem("proj_chain_dve")
        s_rstd, s_xn, s_xT = sem("x_rstd_ready"), sem("xn_ready"), sem("xT_in_psum")
        s_hxa, s_hxd = sem("hxT_lo_chunks_ready"), sem("hxT_hi_chunks_ready")
        s_g0, s_g1, s_mq = sem("cq_done"), sem("ckv_done"), sem("mq_done")
        s_g2, s_g3, s_g4 = sem("k_v_done"), sem("v_o_done"), sem("o_gate_done")
        s_qr, s_kr = sem("cq_rstd_ready"), sem("ckv_rstd_ready")
        s_ctn, s_cT = sem("latents_normed"), sem("latentsT_in_psum")
        s_cTa, s_cTd = sem("cqT_kept"), sem("ckvT_kept")
        s_emq = sem("mq_bank_free")
        s_e2, s_e3, s_e4 = sem("k_v_taken"), sem("v_o_taken"), sem("o_gate_taken")
        s_one = sem("ones_set")

        (x0, x1, xn, hx0, hx1, cqn, ckvn, krn, krt, junk, st), _ = m.run(m.R1, [
            ("x0", [P, D], F32), ("x1", [P, D], F32), ("xn", [P, D], F32), ("hx0", [P, KD, P], F32),
            ("hx1", [P, KD, P], F32), ("cqn", [P, QL], F32), ("ckvn", [P, KVL], F32), ("krn", [P, ROPE], F32),
            ("krt", [P, ROPE], F32), ("junk", [P, D], F32), ("stats", [P, 16], F32)])
        xt, hx = (x0, x1), (hx0, hx1)
        T = PS[:, 6:8, :].rearrange("p b n -> p (b n)")
        xsrc = a["x"].rearrange("b (t p) d -> (b t) p d", p=P)
        csrc = a["ctx"].rearrange("b (t p) d -> (b t) p d", p=P)
        QK_, KVK = QL // P, KVL // P
        LAST = 9

        def tiles(eng, body):
            for t in range(TC):
                body(t, t % 2, t)
            with eng.Fori(TC // 2, NT // 2 - 1) as i:
                for j in range(2):
                    body(2 * i + j, j, 2)
            body(NT - 2, 0, 2)
            body(NT - 1, 1, LAST)

        def after(kind):
            return min(kind + 1, 2)

        with nc.Block() as block:
            @block.sync
            def _(sp):
                def tile(t, j, kind):
                    if kind >= 2:
                        sp.wait_ge(s_xn, t - 1)
                        sp.dma_start(xt[j][:, :], xsrc[t - TC]).then_inc(s_x[j], 16)
                    else:
                        sp.dma_start(xt[j][:, :], csrc[t]).then_inc(s_x[j], 16)
                tiles(sp, tile)

            @block.scalar
            def _(act):
                def rstd(chain, ssq, out, n, signal):
                    chain.done(act.activation(st[:, 3:4], ssq, ACT.Ln, bias=m.eps[:, 0:1], scale=1.0 / n))
                    act.activation(out, st[:, 3:4], ACT.Exp, scale=-0.5).then_inc(signal, 1)

                def x_stats(chain, t, j, kind):
                    act.wait_ge(s_x[j], (t - j) * 8 + 16)
                    if kind >= 1:
                        act.wait_ge(s_xn, t)
                    chain.done(act.activation(junk[:, :], xt[j][:, :], ACT.Square, accum_out=st[:, 0:1]))
                    rstd(chain, st[:, 0:1], st[:, 4:5], D, s_rstd)

                def hx_copy(t, j, kind):
                    act.wait_ge(s_xT, t + 1)
                    if kind >= 2:
                        act.wait_ge(s_g4, t - 1)
                    sc, sh = (m.s1c, R_CSH1) if kind < TC else (m.s1x, R_SH1)
                    for k in range(KD // 2):
                        ins = act.activation(hx[j][:, k, :], T[:, k * P:(k + 1) * P], ACT.Identity,
                                             scale=sc[:, k:k + 1], bias=m.cols[:, sh + k:sh + k + 1])
                    ins.then_inc(s_hxa, 1)

                act.preload_act_table_set("natural_log_exp_and_others")
                x_stats(Chain(act, s_ca), 0, 0, 0)
                hx_copy(0, 0, 0)

                def tile(t, j, kind):
                    x = kind >= TC
                    base = Chain(act, s_ca, 2 + (4 * t if kind < TC else 4 * TC + (t - TC) * 6))
                    if kind != LAST:
                        x_stats(base, t + 1, 1 - j, after(kind))
                    if x:
                        act.wait_ge(s_g0, t - TC + 1)
                        act.wait_ge(s_ctn, t)
                        base.done(act.activation(junk[:, 0:QL], PS[:, 0, 0:QL], ACT.Square, accum_out=st[:, 1:2]))
                        rstd(base, st[:, 1:2], st[:, 5:6], QL, s_qr)
                    act.wait_ge(s_g1, t + 1)
                    if kind >= 1:
                        act.wait_ge(s_ctn, t)
                    base.done(act.activation(junk[:, 0:KVL], PS[:, 1, 0:KVL], ACT.Square, accum_out=st[:, 2:3]))
                    rstd(base, st[:, 2:3], st[:, 6:7], KVL, s_kr)
                    if x:
                        act.wait_ge(s_mq, t - TC + 1)
                        act.activation(m.mqT[:, :, bass.ds((t - TC) * P, P)], PS[:, 5, 0:2 * P].rearrange("p (c n) -> p c n", c=2),
                                       ACT.Copy, scale=MQK ** -0.5).then_inc(s_emq, 1)
                    if kind != LAST:
                        hx_copy(t + 1, 1 - j, after(kind))
                    act.wait_ge(s_g3, t + 1)
                    ins = act.activation(m.vaug[:, t, 2:4, 0:MV], PS[:, 3, 0:256].rearrange("p (h n) -> p h n", h=2), ACT.Copy)
                    if x:
                        ins = act.activation(m.og[:, t - TC, 0:256], PS[:, 3, 256:512], ACT.Exp, scale=-1.0)
                    ins.then_inc(s_e3, 1)
                    act.wait_ge(s_g4, t + 1)
                    if x:
                        act.activation(m.og[:, t - TC, 256:512], PS[:, 4, 0:256], ACT.Exp, scale=-1.0)
                    act.activation(m.g16[:, t, :], PS[:, 4, 256:272], ACT.Copy).then_inc(s_e4, 1)
                    if x:
                        act.wait_ge(s_cT, t + 1)
                        for k in range(QK_):
                            ins = act.activation(m.cqT[:, k, bass.ds((t - TC) * P, P)], T[:, k * P:(k + 1) * P], ACT.Copy,
                                                 scale=m.cols[:, R_QN + k:R_QN + k + 1])
                        ins.then_inc(s_cTa, 1)
                tiles(act, tile)

            @block.vector
            def _(dve):
                dve.memset(m.vaug[:, :, :, MV:MV + 1], 1.0).then_inc(s_one, 1)

                def x_norm(t, j, kind):
                    dve.wait_ge(s_rstd, t + 1)
                    if kind >= 1:
                        dve.wait_ge(s_xT, t)
                    dve.tensor_scalar(xn[:, :], xt[j][:, :], st[:, 4:5], None, ALU.mult).then_inc(s_xn, 1)

                def hx_copy(t, j, kind):
                    dve.wait_ge(s_xT, t + 1)
                    if kind >= 2:
                        dve.wait_ge(s_g4, t - 1)
                    sc, sh = (m.s1c, R_CSH1) if kind < TC else (m.s1x, R_SH1)
                    for k in range(KD // 2, KD):
                        ins = dve.tensor_scalar(hx[j][:, k, :], T[:, k * P:(k + 1) * P], sc[:, k:k + 1],
                                                m.cols[:, sh + k:sh + k + 1], ALU.mult, ALU.add)
                    ins.then_inc(s_hxd, 1)

                x_norm(0, 0, 0)
                hx_copy(0, 0, 0)

                def tile(t, j, kind):
                    x = kind >= TC
                    chain = Chain(dve, s_cd, t * 2)
                    if kind != LAST:
                        x_norm(t + 1, 1 - j, after(kind))
                    if kind >= 1:
                        dve.wait_ge(s_cT, t)
                    if x:
                        dve.wait_ge(s_qr, t - TC + 1)
                        dve.tensor_scalar(cqn[:, :], PS[:, 0, 0:QL], st[:, 5:6], None, ALU.mult)
                    dve.wait_ge(s_kr, t + 1)
                    dve.tensor_scalar(ckvn[:, :], PS[:, 1, 0:KVL], st[:, 6:7], None, ALU.mult)
                    kr = PS[:, 1, KVL:KVL + ROPE]
                    chain.done(dve.tensor_tensor(krn[:, :], kr, m.cs_tab[:, t, :], ALU.mult))
                    swapped = kr.rearrange("p (s n) -> p s n", s=2)[:, ::-1, :]
                    chain.done(dve.tensor_tensor(krt[:, :].rearrange("p (s n) -> p s n", s=2), swapped,
                                                 m.sn_tab[:, t, :].rearrange("p (s n) -> p s n", s=2), ALU.mult))
                    dve.tensor_tensor(krn[:, :], krn[:, :], krt[:, :], ALU.add).then_inc(s_ctn, 1)
                    if kind != LAST:
                        hx_copy(t + 1, 1 - j, after(kind))
                    dve.wait_ge(s_g2, t + 1)
                    dve.tensor_copy(m.mk[:, t, :], PS[:, 2, 0:256])
                    dve.tensor_copy(m.vaug[:, t, 0:2, 0:MV], PS[:, 2, 256:512].rearrange("p (h n) -> p h n", h=2)).then_inc(s_e2, 1)
                    dve.wait_ge(s_cT, t + 1)
                    for k in range(KVK):
                        dve.tensor_scalar(m.ckvT[:, k, bass.ds(t * P, P)], T[:, (4 + k) * P:(5 + k) * P],
                                          m.cols[:, R_KVN + k:R_KVN + k + 1], None, ALU.mult)
                    ins = dve.tensor_copy(m.kT0[NOPE:NOPE + ROPE, bass.ds(t * P, P)], T[0:ROPE, 6 * P:7 * P])
                    ins.then_inc(s_cTd, 1)
                tiles(dve, tile)

            @block.tensor
            def _(pe):
                def x_transposes(t, j, kind):
                    pe.wait_ge(s_xn, t + 1)
                    if kind >= 2:
                        pe.wait_ge(s_cTa, t - 1)
                        pe.wait_ge(s_cTd, t - 1)
                    for k in range(KD):
                        tr = pe.transpose(T[:, k * P:(k + 1) * P], xn[:, k * P:(k + 1) * P], m.ident[:, :])
                    tr.then_inc(s_xT, 1)
                pe.sem_inc(s_cTa, TC)
                pe.sem_inc(s_emq, 1)
                x_transposes(0, 0, 0)

                def group(j, bank, lo, hi, signal, start=0):
                    for k in range(KD):
                        mm = pe.matmul(PS[:, bank, start:start + hi - lo], hx[j][:, k, :], m.w_in[:, k, lo:hi],
                                       start=(k == 0), stop=(k == KD - 1))
                    if signal is not None:
                        mm.then_inc(signal, 1)

                def tile(t, j, kind):
                    x = kind >= TC
                    pe.wait_ge(s_hxa, t + 1)
                    pe.wait_ge(s_hxd, t + 1)
                    if x:
                        pe.wait_ge(s_ctn, t)
                        group(j, 0, C_Q, C_KV, s_g0)
                    elif kind == 1:
                        pe.wait_ge(s_ctn, t)
                    group(j, 1, C_KV, C_MQ, s_g1)
                    if x:
                        pe.wait_ge(s_emq, t - TC + 1)
                        for c in range(2):
                            for k in range(KD):
                                mm = pe.matmul(PS[:, 5, c * P:(c + 1) * P], m.w_in[:, k, C_MQ + c * P:C_MQ + (c + 1) * P],
                                               hx[j][:, k, :], start=(k == 0), stop=(k == KD - 1))
                        mm.then_inc(s_mq, 1)
                    if kind >= 1:
                        pe.wait_ge(s_e2, t)
                    group(j, 2, C_MK, C_MK + 512, s_g2)
                    if kind != LAST:
                        x_transposes(t + 1, 1 - j, after(kind))
                    if kind >= 1:
                        pe.wait_ge(s_e3, t)
                        pe.wait_ge(s_e4, t)
                    if x:
                        group(j, 3, C_MK + 512, C_MK + 1024, s_g3)
                        group(j, 4, C_MK + 1024, IN_W, s_g4)
                    else:
                        group(j, 3, C_MK + 512, C_O, s_g3)
                        group(j, 4, C_G, IN_W, s_g4, start=256)
                    pe.wait_ge(s_ctn, t + 1)
                    if kind != LAST:
                        pe.wait_ge(s_hxa, t + 2)
                        pe.wait_ge(s_hxd, t + 2)
                    if x:
                        for k in range(QK_):
                            pe.transpose(T[:, k * P:(k + 1) * P], cqn[:, k * P:(k + 1) * P], m.ident[:, :])
                    for k in range(KVK):
                        pe.transpose(T[:, (4 + k) * P:(5 + k) * P], ckvn[:, k * P:(k + 1) * P], m.ident[:, :])
                    pe.transpose(T[0:ROPE, 6 * P:7 * P], krn[:, :], m.ident[:, :]).then_inc(s_cT, 1)
                tiles(pe, tile)


def phase_mlstm(nc, a, m, PS):
    ROWS = 64
    with semaphores(nc, "mlstm") as sem:
        s_cst = sem("mlstm_constants")
        s_pad, s_gT = sem("gates_padded"), sem("gatesT_in_psum")
        s_cd, s_ca = sem("mlstm_chain_dve"), sem("mlstm_chain_act")
        s_fa, s_fl = sem("abs_f_ready"), sem("log1p_ready")
        s_ex, s_exd = sem("exponents_ready"), sem("exponentials_ready")
        s_qc, s_qcd, s_dec = sem("columns_in_psum"), sem("columns_kept"), sem("decay_in_psum")
        s_ktp, s_mb, s_st, s_u, s_num = sem("kT_in_psum"), sem("row_broadcasts_done"), sem("scores_done"), sem("kv_products_done"), sem("numerators_done")
        s_qz, s_kt, s_kw = sem("q_chunk_ready"), sem("kT_chunk_ready"), sem("weighted_k_ready")
        s_e, s_qw, s_pt = sem("weights_ready"), sem("scaled_q_ready"), sem("weighted_scores_ready")
        s_mkc = sem("k_chunk_copied")
        s_c, s_h = sem("state_updated"), sem("h_written")

        items, end = m.run(m.W, [
            ("hsum", [P, TX, MH * MV], F32),
            ("gi", [P, NT, ROWS], F32), ("gf", [P, NT, ROWS], F32), ("gab", [P, NT, 8], F32), ("gln", [P, NT, 8], F32),
            ("ri", [ROWS, KEYS], F32), ("rf", [ROWS, KEYS], F32), ("rb", [ROWS, KEYS], F32), ("ra", [ROWS, KEYS], F32),
            ("rm", [ROWS, KEYS], F32), ("rwi", [ROWS, KEYS], F32), ("rem", [ROWS, KEYS], F32)])
        hsum, gi, gf, gab, gln, ri, rf, rb, ra, rm, rwi, rem = items
        assert end <= m.R1
        items, end = m.run(m.R1, [
            ("rws", [ROWS, KEYS], F32), ("mprev", [ROWS, NT + 1], F32), ("rdec", [ROWS, NT], F32),
            ("qcol", [P, 4, NT, 8], F32), ("dcol", [P, 4, NT], F32),
            ("sel", [ROWS, 8, P], F32), ("selp", [ROWS, 4, P], F32), ("identb", [P, P], BF16), ("maskb", [P, 2, P], BF16),
            ("kwt0", [P, MH, P], F32), ("kwt1", [P, MH, P], F32), ("ktc", [P, 2, P], F32), ("ewt", [P, MH, P], F32),
            ("small", [P, 3, MH], F32)])
        rws, mprev, rdec, qcol, dcol, sel, selp, identb, maskb, kwt0, kwt1, ktc, ewt, small = items
        assert end <= m.R1 + 32768
        items, end = m.run(m.R1 + 32768 + 8 * KEYS, [
            ("ptt0", [P, MH, P], F32), ("ptt1", [P, MH, P], F32), ("cst0", [P, 2, MV + 1], F32), ("cst1", [P, 2, MV + 1], F32), ("other", [P, MH, P], F32),
            ("mkc0", [P, MH * MQK], F32), ("mkc1", [P, MH * MQK], F32)])
        ptt0, ptt1, cst0, cst1, other, mkc0, mkc1 = items
        mkc = (mkc0, mkc1)
        assert end <= 229344
        (qz0, qz1), end = m.run(m.W + 4 * TX * MH * MV, [("qz0", [P, MH, P], F32), ("qz1", [P, MH, P], F32)])
        (qw0, qw1), _ = m.run(end, [("qw0", [P, MH, P], F32), ("qw1", [P, MH, P], F32)])
        kwt, ptt, cst, qz, qw = (kwt0, kwt1), (ptt0, ptt1), (cst0, cst1), (qz0, qz1), (qw0, qw1)
        m.hsum = hsum
        DIRS = ((0, 1), (32, -1))
        ORDER = (list(range(NT)), list(range(TC - 1, -1, -1)) + list(range(NT - 1, TC - 1, -1)))
        QA, QWI, QEM, QWS = range(4)

        def fb(tile):
            return tile.rearrange("p t (d r) -> p t d r", d=2)[:, :, :, 0:MH]

        NUM = PS[:, 5:7, :].rearrange("p b (h n) -> p (b h) n", h=2)
        with nc.Block() as block:
            @block.gpsimd
            def _(pool):
                pool.memset(sel[:, :, :], 0.0)
                pool.memset(selp[:, :, :], 0.0)
                pool.memset(identb[:, :], 0.0)
                pool.memset(maskb[:, :, :], 0.0)
                pool.memset(gi[:, :, :], 0.0)
                pool.memset(gf[:, :, :], 0.0).then_inc(s_cst, 1)
                pool.wait_ge(s_cst, 1)
                v = sel[:, :, :].rearrange("r (d h) n -> r d h n", d=2)
                pool.affine_select(out=v, in_=v, compare_op=ALU.not_equal, fill=1.0, base=0,
                                   pattern=[[-32, 2], [-1, MH], [0, P]], channel_multiplier=1)
                v = selp[:, :, :].rearrange("r (d c) (e n) -> r d (c e) n", d=2, e=2)
                for d in range(2):
                    pool.affine_select(out=v[:, d], in_=v[:, d], compare_op=ALU.not_equal, fill=1.0, base=-32 * d,
                                       pattern=[[-1, 4], [0, MQK]], channel_multiplier=1)
                pool.affine_select(out=identb[:, :], in_=identb[:, :], compare_op=ALU.not_equal, fill=1.0,
                                   base=0, pattern=[[-1, P]], channel_multiplier=1)
                for d, step in enumerate((1, -1)):
                    ins = pool.affine_select(out=maskb[:, d, :], in_=maskb[:, d, :], compare_op=ALU.is_ge, fill=1e30,
                                             base=0, pattern=[[step, P]], channel_multiplier=-step)
                ins.then_inc(s_cst, 1)

            @block.scalar
            def _(act):
                act.preload_act_table_set("natural_log_exp_and_others")
                chain = Chain(act, s_ca)
                act.wait_ge(s_fa, 1)
                chain.done(act.activation(gln[:, :, :], gab[:, :, :], ACT.Exp, scale=-1.0))
                act.activation(gln[:, :, :], gln[:, :, :], ACT.Ln, bias=1.0).then_inc(s_fl, 1)
                for n, (r, scale) in enumerate(((rwi, -1.0), (rem, -1.0), (rws, 1.0))):
                    act.wait_ge(s_ex, n + 1)
                    act.activation(r[:, :], r[:, :], ACT.Exp, scale=scale).then_inc(s_exd, 1)
                act.wait_ge(s_ex, 4)
                act.activation(rdec[:, :], rdec[:, :], ACT.Exp).then_inc(s_exd, 1)
                act.wait_ge(s_qcd, 1)

                def k_copy(x, t, d):
                    act.wait_ge(s_num, x)
                    act.activation(mkc[d][:, :], m.mk[:, t, :], ACT.Copy).then_inc(s_mkc, 1)

                def weights(n, t, d):
                    act.wait_ge(s_mb, n)
                    act.wait_ge(s_pt, n)
                    for h in range(MH):
                        ins = act.activation(ewt[:, h, :], PS[:, 1, h * P:(h + 1) * P], ACT.Exp, scale=-1.0,
                                             bias=qcol[:, QA, t, 4 * d + h:4 * d + h + 1])
                    ins.then_inc(s_e, 1)
                for lo in (TC, TC + TX // 2):
                    with act.Fori(lo, lo + TX // 2) as i:
                        for d in range(2):
                            x, t = 2 * (i - TC) + d + 1, i if d == 0 else i * -1 + (NT + 1)
                            k_copy(x, t, d)
                            weights(x, t, d)

            @block.vector
            def _(dve):
                chain = Chain(dve, s_cd)
                dve.wait_ge(s_cst, 1)
                for d in range(2):
                    chain.done(dve.memset(cst[d][:, :, :], 0.0))
                    chain.done(dve.memset(kwt[d][:, :, :], 0.0))
                chain.done(dve.memset(mprev[:, :], 0.0))
                bias = m.bgates[:, :].rearrange("p (a n) -> p a n", a=1).to_broadcast([P, NT, 16])
                chain.done(dve.tensor_tensor(m.g16[:, :, :], m.g16[:, :, :], bias, ALU.add))
                g4 = m.g16[:, :, :].rearrange("p t (d q h) -> p t d q h", d=2, q=2)
                f4 = gab[:, :, :].rearrange("p t (d h) -> p t d h", d=2)
                l4 = gln[:, :, :].rearrange("p t (d h) -> p t d h", d=2)
                for d in range(2):
                    dve.tensor_copy(fb(gi[:, :, :])[:, :, d, :], g4[:, :, d, 0, :])
                    chain.done(dve.tensor_scalar(fb(gf[:, :, :])[:, :, d, :], g4[:, :, d, 1, :], 0.0, None, ALU.min))
                    chain.done(dve.scalar_tensor_tensor(out=f4[:, :, d, :], in0=g4[:, :, d, 1, :], scalar=-1.0, in1=g4[:, :, d, 1, :],
                                                        op0=ALU.mult, op1=ALU.max))
                dve.sem_inc(s_fa, 1)
                dve.wait_ge(s_fl, 1)
                for d in range(2):
                    ins = dve.tensor_tensor(fb(gf[:, :, :])[:, :, d, :], fb(gf[:, :, :])[:, :, d, :], l4[:, :, d, :], ALU.subtract)
                ins.then_inc(s_pad, 1)
                dve.memset(rb[:, :], 0.0)
                chain.done(dve.memset(rm[:, :], 0.0))
                dve.wait_ge(s_gT, 1)
                dve.tensor_copy(ri[:, :], PS[0:ROWS, 0:3, :].rearrange("p b n -> p (b n)")[:, 0:KEYS])
                chain.done(dve.tensor_copy(rf[:, :], PS[0:ROWS, 3:6, :].rearrange("p b n -> p (b n)")[:, 0:KEYS]))

                def chunk(r, d, t):
                    p0, step = DIRS[d]
                    return r[p0:p0 + MH, t * P:(t + 1) * P][:, ::step]

                def last(r, d, t):
                    p0, step = DIRS[d]
                    e = t * P + (P - 1 if step == 1 else 0)
                    return r[p0:p0 + MH, e:e + 1]
                for t in range(NT):
                    for d in range(2):
                        ins = dve.tensor_tensor_scan(chunk(rb, d, t), chunk(rf, d, t), chunk(rf, d, t), 0.0, ALU.add, ALU.bypass)
                chain.done(ins)
                chain.done(dve.tensor_tensor(ra[:, :], ri[:, :], rb[:, :], ALU.subtract))
                for i in range(NT):
                    for d in range(2):
                        t, p0 = ORDER[d][i], DIRS[d][0]
                        ins = dve.tensor_tensor_scan(chunk(rm, d, t), chunk(ra, d, t), chunk(ra, d, t),
                                                     mprev[p0:p0 + MH, t:t + 1], ALU.max, ALU.max)
                    chain.done(ins)
                    for d in range(2):
                        t, p0 = ORDER[d][i], DIRS[d][0]
                        nxt = ORDER[d][i + 1] if i + 1 < NT else NT
                        ins = dve.tensor_tensor(mprev[p0:p0 + MH, nxt:nxt + 1], last(rb, d, t), last(rm, d, t), ALU.add)
                    chain.done(ins)
                mp = mprev[:, 0:NT].rearrange("p (t o) -> p t o", o=1)

                def c3(r):
                    return r[:, :].rearrange("p (t n) -> p t n", n=P)
                dve.tensor_tensor(c3(rwi), c3(rm), mp.to_broadcast([ROWS, NT, P]), ALU.subtract).then_inc(s_ex, 1)
                dve.tensor_tensor(rem[:, :], rm[:, :], rb[:, :], ALU.add).then_inc(s_ex, 1)
                for half, e in ((0, P - 1), (32, 0)):
                    ml = c3(rm)[half:half + 32, :, e:e + 1]
                    ins = dve.tensor_tensor(c3(rws)[half:half + 32], c3(ra)[half:half + 32], ml.to_broadcast([32, NT, P]), ALU.subtract)
                ins.then_inc(s_ex, 1)
                for half, e in ((0, P - 1), (32, 0)):
                    ml = c3(rm)[half:half + 32, :, e:e + 1]
                    ins = dve.tensor_tensor(rdec[half:half + 32, :], mprev[half:half + 32, 0:NT], ml.rearrange("p t o -> p (t o)"), ALU.subtract)
                ins.then_inc(s_ex, 1)
                dve.wait_ge(s_qc, 1)
                for q in range(4):
                    src = PS[:, 0:5, :].rearrange("p b (x d r) -> p (b x) d r", d=2, r=32)[:, q * NT:(q + 1) * NT, :, 0:MH]
                    for d in range(2):
                        ins = dve.tensor_copy(qcol[:, q, :, 4 * d:4 * d + 4], src[:, :, d, :])
                dve.wait_ge(s_dec, 1)
                chain.done(dve.tensor_copy(dcol[:, :, :], PS[:, 7, 0:4 * NT].rearrange("p (c t) -> p c t", c=4)))
                for d in range(2):
                    chain.done(dve.memset(qz[d][:, :, :], 0.0))
                dve.sem_inc(s_qcd, 2)
                base = chain.n

                def weigh_k(n, t, d):
                    if not isinstance(n, int) or n > 2:
                        dve.wait_ge(s_u, n - 2)
                    w = qcol[:, QWS, t, 4 * d:4 * d + 4].rearrange("p (h o) -> p h o", o=1)
                    k = m.mk[:, t, :].rearrange("p (h n) -> p h n", h=MH)
                    for e in range(2):
                        ins = dve.tensor_tensor(kwt[d][:, e:MH:2, 64 * e:64 * e + MQK], k[:, e:MH:2, :],
                                                w[:, e:MH:2, :].to_broadcast([P, 2, MQK]), ALU.mult)
                    ins.then_inc(s_kw, 1)

                def update(n, t, d):
                    dve.wait_ge(s_u, n)
                    for c in range(2):
                        ins = dve.scalar_tensor_tensor(out=cst[d][:, c, :], in0=cst[d][:, c, :], scalar=dcol[:, 2 * d + c, bass.ds(t, 1)],
                                                       in1=PS[:, 4, c * 256:c * 256 + MV + 1], op0=ALU.mult, op1=ALU.add)
                    ins.then_inc(s_c, 1)

                for i in range(TC):
                    for d in range(2):
                        weigh_k(2 * i + d + 1, ORDER[d][i], d)
                        update(2 * i + d + 1, ORDER[d][i], d)

                def prepare(i, d):
                    t = i if d == 0 else i * -1 + (NT + 1)
                    n, x = 2 * i + d + 1, 2 * (i - TC) + d + 1
                    dve.wait_ge(s_num, x)
                    for e in range(2):
                        ins = dve.tensor_copy(qz[d][64 * e:64 * e + 64, e:MH:2, :], m.mqT[64 * e:64 * e + 64, :, bass.ds((t - TC) * P, P)])
                    ins.then_inc(s_qz, 1)
                    weigh_k(n, t, d)
                    dve.wait_ge(s_ktp, x)
                    dve.tensor_copy(ktc[:, :, :], PS[:, 3, 0:2 * P].rearrange("p (c n) -> p c n", c=2)).then_inc(s_kt, 1)
                    dve.wait_ge(s_mb, x)
                    dve.wait_ge(s_qz, x)
                    dve.tensor_tensor(qw[d][:, :, :], qz[d][:, :, :], PS[:, 2, :].rearrange("p (h n) -> p h n", h=MH), ALU.mult).then_inc(s_qw, 1)

                def latent(i, d, first, more=True):
                    t = i if d == 0 else i * -1 + (NT + 1)
                    n, x = 2 * i + d + 1, 2 * (i - TC) + d + 1
                    dve.wait_ge(s_st, x)
                    dve.wait_ge(s_e, x + 1)
                    dve.tensor_tensor(ptt[d][:, :, :], ewt[:, :, :], PS[:, 0, :].rearrange("p (h n) -> p h n", h=MH), ALU.mult).then_inc(s_pt, 1)
                    if more:
                        prepare(i + d, 1 - d)
                    dve.wait_ge(s_num, x + 2)
                    c = Chain(dve, s_cd, base + (x - 1) * 3)
                    c.done(dve.scalar_tensor_tensor(out=small[:, 0, :], in0=NUM[:, :, MV], scalar=-1.0,
                                                    in1=qcol[:, QEM, t, 4 * d:4 * d + 4], op0=ALU.mult, op1=ALU.max))
                    c.done(dve.tensor_tensor(small[:, 1, :], NUM[:, :, MV], small[:, 0, :], ALU.max))
                    c.done(dve.reciprocal(small[:, 2, :], small[:, 1, :]))
                    r = small[:, 2, :].rearrange("p (h o) -> p h o", o=1).to_broadcast([P, MH, MV])
                    dst = hsum[:, t - TC, :].rearrange("p (h n) -> p h n", h=MH)
                    if first:
                        dve.tensor_tensor(dst, NUM[:, :, 0:MV], r, ALU.mult).then_inc(s_h, 1)
                    else:
                        dve.tensor_tensor(other[:, :, :], NUM[:, :, 0:MV], r, ALU.mult).then_inc(s_h, 1)
                        dve.wait_ge(s_h, x + 1)
                        dve.tensor_tensor(dst, dst, other[:, :, :], ALU.add)
                    update(n, t, d)
                prepare(TC, 0)
                with dve.Fori(TC, TC + TX // 2) as i:
                    for d in range(2):
                        latent(i, d, True)
                with dve.Fori(TC + TX // 2, NT - 1) as i:
                    for d in range(2):
                        latent(i, d, False)
                latent(NT - 1, 0, False)
                latent(NT - 1, 1, False, False)

            @block.tensor
            def _(pe):
                pe.sem_inc(s_num, 2)
                pe.sem_inc(s_pt, 1)
                pe.sem_inc(s_h, 1)
                pe.sem_inc(s_kt, 1)
                pe.sem_inc(s_e, 1)
                pe.sem_inc(s_qw, 1)
                pe.wait_ge(s_cst, 2)
                pe.wait_ge(s_pad, 1)
                for g, bank in ((gi, 0), (gf, 3)):
                    for t in range(NT):
                        tr = pe.transpose(PS[0:ROWS, bank + t // 4, (t % 4) * P:(t % 4 + 1) * P], g[:, t, :], m.ident[:, :])
                tr.then_inc(s_gT, 1)
                pe.wait_ge(s_exd, 4)
                for q, r in enumerate((ra, rwi, rem, rws)):
                    for t in range(NT):
                        x = q * NT + t
                        tr = pe.transpose(PS[:, x // 8, (x % 8) * ROWS:(x % 8 + 1) * ROWS], r[:, t * P:(t + 1) * P], m.ident[0:ROWS, 0:ROWS])
                tr.then_inc(s_qc, 1)
                for c in range(4):
                    mm = pe.matmul(PS[:, 7, c * NT:(c + 1) * NT], selp[:, c, :], rdec[:, :], start=True, stop=True)
                mm.then_inc(s_dec, 1)
                pe.wait_ge(s_qcd, 1)

                def products(n, t, d):
                    pe.wait_ge(s_kw, n)
                    if not isinstance(n, int) or n > 1:
                        pe.wait_ge(s_c, n - 1)
                    for h in range(MH):
                        mm = pe.matmul(PS[:, 4, (h // 2) * 256:(h // 2) * 256 + MV + 1], kwt[d][:, h, :], m.vaug[:, t, h, :],
                                       start=(h % 2 == 0), stop=(h % 2 == 1), skip_group_check=True)
                    mm.then_inc(s_u, 1)
                for i in range(TC):
                    for d in range(2):
                        products(2 * i + d + 1, ORDER[d][i], d)

                def prepare(i, d):
                    t = i if d == 0 else i * -1 + (NT + 1)
                    n, x = 2 * i + d + 1, 2 * (i - TC) + d + 1
                    pe.wait_ge(s_kt, x)
                    pe.wait_ge(s_mkc, x)
                    for c in range(2):
                        tr = pe.transpose(PS[:, 3, c * P:(c + 1) * P], mkc[d][:, c * P:(c + 1) * P], m.ident[:, :])
                    tr.then_inc(s_ktp, 1)
                    pe.wait_ge(s_e, x)
                    pe.wait_ge(s_qw, x)
                    for h in range(MH):
                        pe.matmul(PS[:, 1, h * P:(h + 1) * P], sel[:, 4 * d + h, :], rm[:, bass.ds(t * P, P)],
                                  start=(h == 0), stop=False, skip_group_check=True)
                    pe.matmul(PS[:, 1, :].rearrange("p (h n) -> p h n", h=MH), identb[:, :],
                              maskb[:, d, :].rearrange("p (o n) -> p o n", o=1).to_broadcast([P, MH, P]),
                              start=False, stop=True, skip_group_check=True)
                    for h in range(MH):
                        mm = pe.matmul(PS[:, 2, h * P:(h + 1) * P], sel[:, 4 * d + h, :], rwi[:, bass.ds(t * P, P)], start=True, stop=True)
                    mm.then_inc(s_mb, 1)

                def latent(i, d, more=True):
                    t = i if d == 0 else i * -1 + (NT + 1)
                    n, x = 2 * i + d + 1, 2 * (i - TC) + d + 1
                    pe.wait_ge(s_kt, x + 1)
                    pe.wait_ge(s_qz, x)
                    pe.wait_ge(s_pt, x)
                    for h in range(MH):
                        mm = pe.matmul(PS[:, 0, h * P:(h + 1) * P], ktc[:, h // 2, :], qz[d][:, h, :], start=True, stop=True)
                    mm.then_inc(s_st, 1)
                    if more:
                        prepare(i + d, 1 - d)
                    products(n, t, d)
                    pe.wait_ge(s_qw, x + 1)
                    pe.wait_ge(s_pt, x + 1)
                    pe.wait_ge(s_h, x)
                    for h in range(MH):
                        pe.matmul(NUM[:, h, 0:MV + 1], qw[d][:, h, :], cst[d][:, h // 2, :], start=True, stop=False, skip_group_check=True)
                        mm = pe.matmul(NUM[:, h, 0:MV + 1], ptt[d][:, h, :], m.vaug[:, t, h, :], start=False, stop=True, skip_group_check=True)
                    mm.then_inc(s_num, 1)
                prepare(TC, 0)
                with pe.Fori(TC, NT - 1) as i:
                    for d in range(2):
                        latent(i, d)
                latent(NT - 1, 0)
                latent(NT - 1, 1, False)


def phase_attention(nc, a, m, PS):
    DQ = NOPE + ROPE
    NQ = SEQ // P
    HALF = SEQ // 2
    NST = 2 * NT
    S0, T0, O0 = 0, 3, 6
    with semaphores(nc, "attention") as sem:
        s_w = [sem("head_weights_in0"), sem("head_weights_in1")]
        s_tab, s_wo, s_wv, s_vh = sem("rope_tables_in"), sem("w_out_in"), sem("v_weights_in"), sem("head_v_ready")
        s_rot, s_kr = sem("rotated_weights_ready"), sem("shared_keys_and_ones_ready")
        s_krh, s_krl = sem("shared_keys_hi"), sem("shared_keys_lo")
        s_kp, s_qp, s_vp = sem("k_projected"), sem("q_projected"), sem("v_projected")
        s_kh, s_kl, s_v = sem("k_hi_kept"), sem("k_lo_kept"), sem("v_kept")
        s_qr, s_qh, s_ql, s_qc = sem("q_roped"), sem("q_hi_ready"), sem("q_lo_ready"), sem("rope_chain")
        s_s, s_mx, s_nt, s_nh, s_nl = sem("scores_done"), sem("max_ready"), sem("max_transposed"), sem("max_hi"), sem("max_lo")
        s_ov, s_ot = sem("values_kept"), sem("values_transposed")
        s_st, s_ex, s_pv, s_rc, s_o = sem("key_scores_done"), sem("exps_ready"), sem("pv_done"), sem("sum_inverted"), sem("attention_written")
        (m.w_out,), m.after_w_out = m.run(SB0 + 4608 + 4 * TX * MH * MV, [("w_out", [P, KD, D], F32)])
        base = m.W + 4 * TX * MH * MV
        items, end = m.run(base, [
            ("attn", [P, TX, HEADS * VH], F32), ("qTh0", [DQ + 1, SEQ], F32R), ("qTh1", [DQ + 1, SEQ], F32R),
            ("qTl0", [DQ + 1, SEQ], F32R), ("qTl1", [DQ + 1, SEQ], F32R), ("kTl1", [DQ + 1, KEYS], F32R),
            ("wqh0", [P, QL // P, P], F32), ("wqh1", [P, QL // P, P], F32),
            ("wkh0", [P, KVL // P, NOPE], F32), ("wkh1", [P, KVL // P, NOPE], F32),
            ("negmax", [P, NQ], F32), ("rinv", [P, 2, NQ // 2], F32), ("oT", [VH + 1, HALF], F32), ("cst", [P, SEQ], F32), ("qraw", [DQ, SEQ], F32), ("rtmp", [P, HALF], F32)])
        m.attn, qTh0, qTh1, qTl0, qTl1, kTl1, wq0, wq1, wk0, wk1, negmax, rinv, oT, cst, qraw, rtmp = items
        assert end <= m.R1
        (kTh0, kTh1, kTl0), end = m.run(m.R1, [
            ("kTh0", [DQ + 1, KEYS], F32R), ("kTh1", [DQ + 1, KEYS], F32R), ("kTl0", [DQ + 1, KEYS], F32R)])
        (probT, vall), at_end = m.run(end, [("probT", [P, NT, HALF], F32), ("vall", [P, NT, HEADS, VH + 1], F32)])
        assert at_end <= 229344
        wv = m.at("wv", [P, KVL // P, HEADS, VH], F32, end)
        assert end + 4 * KVL // P * HEADS * VH <= m.R1 + 32768
        (v0, v1), _ = m.run(m.after_w_out, [("v0", [P, NT, VH + 1], F32), ("v1", [P, NT, VH + 1], F32)])
        qTh, qTl, kTh, kTl, v, wqh, wkh = (qTh0, qTh1), (qTl0, qTl1), (kTh0, kTh1), (kTl0, kTl1), (v0, v1), (wq0, wq1), (wk0, wk1)
        uq = a["w_uq"].rearrange("l (k p) (h n) -> p (l k) h n", p=P, n=DQ)
        ukv = a["w_ukv"].rearrange("l (k p) (h n) -> p (l k) h n", p=P, n=NOPE + VH)
        CH = ((0, 512), (512, 512), (1024, 256))
        flat = PS[:, S0:S0 + 3, :].rearrange("p b n -> p (b n)")

        def heads(eng, body):
            body(0, 0, True)
            with eng.Fori(0, HEADS // 2 - 2) as i:
                for j in range(2):
                    body(2 * i + (j + 1), 1 - j, True)
            body(HEADS - 3, 1, True)
            body(HEADS - 2, 0, True)
            body(HEADS - 1, 1, False)

        with nc.Block() as block:
            @block.sync
            def _(sp):
                sp.dma_start(cst[NOPE:DQ, :], a["cs_tabT"]).then_inc(s_tab, 16)
                sp.dma_start(cst[96:128, :], a["sn_tabT"]).then_inc(s_tab, 16)

                def load(h, j):
                    sp.dma_start(wqh[j][:, :, 0:DQ], uq[:, :, h, :]).then_inc(s_w[j], 16)
                    sp.dma_start(wkh[j][:, :, :], ukv[:, :, h, 0:NOPE]).then_inc(s_w[j], 16)
                load(0, 0)
                for k in range(KVL // P):
                    sp.dma_start(wv[:, k, :, :], ukv[:, k, :, NOPE:]).then_inc(s_wv, 16)
                load(1, 1)
                sp.dma_start(m.w_out[:, :, :], a["w_out"].rearrange("l (k p) n -> p (l k) n", p=P)).then_inc(s_wo, 16)
                with sp.Fori(1, HEADS // 2) as i:
                    for j in range(2):
                        sp.wait_ge(s_qp, 2 * i + j - 1)
                        load(2 * i + j, j)
                sp.wait_ge(s_wo, 16)

            @block.scalar
            def _(act):
                act.preload_act_table_set("natural_log_exp_and_others")

                def k_hi(h, j):
                    act.wait_ge(s_kp, h + 1)
                    act.activation(kTh[j][0:NOPE, :], flat[0:NOPE, 0:KEYS], ACT.Copy).then_inc(s_kh, 1)

                def head_v(h, j):
                    act.activation(v[j].rearrange("p t (o n) -> p t o n", o=1), vall[:, :, bass.ds(h, 1), :], ACT.Copy).then_inc(s_vh, 1)

                def q_hi(h, j):
                    act.wait_ge(s_qr, h + 1)
                    act.activation(qTh[j][0:DQ, :], qraw[:, :], ACT.Copy).then_inc(s_qh, 1)

                def max_hi(h, j):
                    act.wait_ge(s_nt, h + 1)
                    act.activation(qTh[j][DQ:DQ + 1, :], flat[DQ:DQ + 1, 0:SEQ], ACT.Copy).then_inc(s_nh, 1)

                def exps(h, lo, hi):
                    for n in range(lo, hi):
                        act.wait_ge(s_st, h * NST + (n + 1))
                        act.activation(probT[:, n % NT, :], PS[:, T0 + n % 3, :], ACT.Exp).then_inc(s_ex, 1)
                for kh in kTh:
                    ins = act.activation(kh[NOPE:DQ, :], m.kT0[NOPE:DQ, :], ACT.Copy)
                ins.then_inc(s_krh, 1)
                k_hi(0, 0)
                for t in range(NT):
                    act.wait_ge(s_vp, t + 1)
                    act.activation(vall[:, t, :, 0:VH], PS[:, T0 + t % 3, :].rearrange("p (h n) -> p h n", h=HEADS), ACT.Copy).then_inc(s_v, 1)
                q_hi(0, 0)
                act.wait_ge(s_v, NT)
                act.wait_ge(s_kr, 1)
                head_v(0, 0)
                max_hi(0, 0)

                def body(h, j, more):
                    if more:
                        k_hi(h + 1, 1 - j)
                    exps(h, 0, NT)
                    if more:
                        q_hi(h + 1, 1 - j)
                        head_v(h + 1, 1 - j)
                    exps(h, NT, NST)
                    if more:
                        max_hi(h + 1, 1 - j)
                heads(act, body)

            @block.vector
            def _(dve):
                def swap(h, j):
                    dve.wait_ge(s_w[j], 16 * (h - j) + 32)
                    dve.tensor_copy(wqh[j][:, :, DQ:DQ + 16], wqh[j][:, :, DQ - 16:DQ])
                    dve.tensor_copy(wqh[j][:, :, DQ + 16:P], wqh[j][:, :, NOPE:NOPE + 16]).then_inc(s_rot, 1)

                def k_lo(h, j):
                    dve.wait_ge(s_kh, h + 1)
                    dve.tensor_tensor(kTl[j][0:NOPE, :], flat[0:NOPE, 0:KEYS], kTh[j][0:NOPE, :].bitcast(F32), ALU.subtract).then_inc(s_kl, 1)

                def q_rope(h):
                    dve.wait_ge(s_qp, h + 1)
                    for c in range(2):
                        cols = slice(512 * c, 512 * c + 512)
                        dve.tensor_scalar(qraw[0:NOPE, cols], PS[0:NOPE, S0 + c, :], SCALE, None, ALU.mult)
                        dve.tensor_tensor(qraw[NOPE:DQ, cols], PS[NOPE:DQ, S0 + c, :], cst[NOPE:DQ, cols], ALU.mult)
                        dve.tensor_tensor(rtmp[NOPE:DQ, :], PS[96:128, S0 + c, :], cst[96:128, cols], ALU.mult).then_inc(s_qc, 1)
                        dve.wait_ge(s_qc, 4 * h + (2 * c + 1))
                        ins = dve.tensor_tensor(qraw[NOPE:DQ, cols], qraw[NOPE:DQ, cols], rtmp[NOPE:DQ, :], ALU.add)
                        ins.then_inc(s_qc, 1)
                        dve.wait_ge(s_qc, 4 * h + (2 * c + 2))
                    dve.sem_inc(s_qr, 1)

                def q_lo(h, j):
                    dve.wait_ge(s_qh, h + 1)
                    dve.tensor_tensor(qTl[j][0:DQ, :], qraw[:, :], qTh[j][0:DQ, :].bitcast(F32), ALU.subtract).then_inc(s_ql, 1)

                def maxima(h, lo, hi):
                    for u in range(lo, hi):
                        dve.wait_ge(s_s, h * NQ + (u + 1))
                        dve.tensor_reduce(negmax[:, u:u + 1], flat[:, 0:KEYS], AX.X, ALU.max, negate=True).then_inc(s_mx, 1)

                def max_lo(h, j):
                    dve.wait_ge(s_nh, h + 1)
                    dve.tensor_tensor(qTl[j][DQ:DQ + 1, :], flat[DQ:DQ + 1, 0:SEQ], qTh[j][DQ:DQ + 1, :].bitcast(F32),
                                      ALU.subtract).then_inc(s_nl, 1)

                def values_out(h, half):
                    dve.wait_ge(s_pv, 2 * h + (half + 1))
                    dve.tensor_copy(oT[:, :], PS[0:VH + 1, O0, :]).then_inc(s_ov, 1)

                def output(h, half):
                    dve.wait_ge(s_ot, 2 * h + (half + 1))
                    o = PS[:, O0, 0:NQ // 2 * (VH + 1)].rearrange("p (t n) -> p t n", n=VH + 1)
                    dve.reciprocal(rinv[:, half, :].unsqueeze(2), o[:, :, VH:VH + 1]).then_inc(s_rc, 1)
                    dve.wait_ge(s_rc, 2 * h + (half + 1))
                    t = half * NQ // 2
                    dve.tensor_tensor(m.attn[:, t:t + NQ // 2, bass.ds(h * VH, VH)], o[:, :, 0:VH],
                                      rinv[:, half, :].unsqueeze(2).to_broadcast([P, NQ // 2, VH]), ALU.mult).then_inc(s_o, 1)
                for k in range(2):
                    dve.memset(kTh[k][DQ:DQ + 1, :].bitcast(F32), 1.0)
                    dve.memset(kTl[k][DQ:DQ + 1, :].bitcast(F32), 0.0)
                dve.wait_ge(s_krh, 1)
                for kl, kh in zip(kTl, kTh):
                    dve.tensor_tensor(kl[NOPE:DQ, :], m.kT0[NOPE:DQ, :], kh[NOPE:DQ, :].bitcast(F32), ALU.subtract).then_inc(s_krl, 1)
                dve.wait_ge(s_krl, 2)
                dve.memset(vall[:, :, :, VH:VH + 1], 1.0).then_inc(s_kr, 1)
                dve.sem_inc(s_o, 1)
                swap(0, 0)
                k_lo(0, 0)
                dve.wait_ge(s_tab, 32)
                q_rope(0)
                swap(1, 1)
                maxima(0, 0, NQ)
                q_lo(0, 0)
                max_lo(0, 0)

                def body(h, j, more):
                    if more:
                        k_lo(h + 1, 1 - j)
                    if not (isinstance(h, int) and h == 0):
                        output(h - 1, 1)
                    if more:
                        q_rope(h + 1)
                        if not (isinstance(h, int) and h + 2 == HEADS):
                            swap(h + 2, j)
                        maxima(h + 1, 0, 3)
                    values_out(h, 0)
                    if more:
                        maxima(h + 1, 3, 4)
                    output(h, 0)
                    if more:
                        maxima(h + 1, 4, NQ)
                        q_lo(h + 1, 1 - j)
                        max_lo(h + 1, 1 - j)
                    values_out(h, 1)
                heads(dve, body)
                output(HEADS - 1, 1)

            @block.tensor
            def _(pe):
                def project_k(h, j):
                    pe.wait_ge(s_rot, h + 1)
                    for c, (lo, w) in enumerate(CH):
                        for k in range(KVL // P):
                            mm = pe.matmul(PS[0:NOPE, S0 + c, 0:w], wkh[j][:, k, :], m.ckvT[:, k, lo:lo + w],
                                           start=(k == 0), stop=(k == KVL // P - 1))
                    mm.then_inc(s_kp, 1)

                def project_q(h, j):
                    pe.wait_ge(s_kl, h + 1)
                    for c in range(2):
                        for k in range(QL // P):
                            mm = pe.matmul(PS[:, S0 + c, :], wqh[j][:, k, :], m.cqT[:, k, 512 * c:512 * c + 512],
                                           start=(k == 0), stop=(k == QL // P - 1))
                    mm.then_inc(s_qp, 1)

                def project_v(t):
                    if t >= 3:
                        pe.wait_ge(s_v, t - 2)
                    for k in range(KVL // P):
                        mm = pe.matmul(PS[:, T0 + t % 3, :], m.ckvT[:, k, t * P:(t + 1) * P], wv[:, k, :, :],
                                       start=(k == 0), stop=(k == KVL // P - 1))
                    mm.then_inc(s_vp, 1)

                def scores(h, j, u):
                    if u == 0:
                        pe.wait_ge(s_qh, h + 1)
                    else:
                        pe.wait_ge(s_mx, h * NQ + u)
                    for c, (lo, w) in enumerate(CH):
                        mm = pe.matmul(PS[:, S0 + c, 0:w], qTh[j][0:DQ, u * P:(u + 1) * P], kTh[j][0:DQ, lo:lo + w], start=True, stop=True)
                    mm.then_inc(s_s, 1)

                def max_rows(h):
                    pe.wait_ge(s_mx, h * NQ + NQ)
                    for u in range(NQ):
                        tr = pe.matmul(flat[DQ:DQ + 1, u * P:(u + 1) * P], negmax[:, u:u + 1], m.ident[:, :], start=True, stop=True)
                    tr.then_inc(s_nt, 1)

                def key_scores(h, j, n):
                    t, q = n % NT, slice(n // NT * HALF, (n // NT + 1) * HALF)
                    if n >= 3:
                        pe.wait_ge(s_ex, h * NST + (n - 2))
                    for i, (k, x) in enumerate(((kTh, qTh), (kTl, qTh), (kTh, qTl))):
                        mm = pe.matmul(PS[:, T0 + n % 3, :], k[j][:, t * P:(t + 1) * P], x[j][:, q], start=(i == 0), stop=(i == 2))
                    mm.then_inc(s_st, 1)

                def weigh(h, j, half, t):
                    if t == 0:
                        pe.wait_ge(s_o, 2 * h + (half + 1))
                        pe.wait_ge(s_vh, h + 1)
                    pe.wait_ge(s_ex, h * NST + (NT * half + t + 1))
                    mm = pe.matmul(PS[0:VH + 1, O0, :], v[j][:, t, :], probT[:, t, :], start=(t == 0), stop=(t == NT - 1))
                    if t == NT - 1:
                        mm.then_inc(s_pv, 1)

                def output_rows(h, half):
                    pe.wait_ge(s_ov, 2 * h + (half + 1))
                    for q in range(NQ // 2):
                        tr = pe.transpose(PS[:, O0, q * (VH + 1):(q + 1) * (VH + 1)], oT[:, q * P:(q + 1) * P], m.ident[0:VH + 1, 0:VH + 1])
                    tr.then_inc(s_ot, 1)
                pe.wait_ge(s_kr, 1)
                project_k(0, 0)
                project_q(0, 0)
                pe.wait_ge(s_wv, 16 * KVL // P)
                for t in range(NT):
                    project_v(t)
                for u in range(NQ):
                    scores(0, 0, u)
                max_rows(0)
                pe.wait_ge(s_v, NT)

                def body(h, j, more):
                    pe.wait_ge(s_ql, h + 1)
                    pe.wait_ge(s_nl, h + 1)
                    if more:
                        project_k(h + 1, 1 - j)
                    if not (isinstance(h, int) and h == 0):
                        output_rows(h - 1, 1)
                    for n in range(NT // 2):
                        key_scores(h, j, n)
                    if more:
                        project_q(h + 1, 1 - j)
                    for n in range(NT // 2, NT):
                        key_scores(h, j, n)
                    todo = [(0, t) for t in range(NT)] + [(None, n) for n in range(NT, NST)] + [(1, t) for t in range(NT)]
                    before = {4: 0, 6: 1, 8: 2, 10: 3, 13: 4, 16: 5, 19: 6, 21: 7}
                    for n, (half, which) in enumerate(todo):
                        if more and n in before:
                            scores(h + 1, 1 - j, before[n])
                        if n == 13:
                            output_rows(h, 0)
                        if more and n == 25:
                            max_rows(h + 1)
                        if half is None:
                            key_scores(h, j, which)
                        else:
                            weigh(h, j, half, which)
                heads(pe, body)
                output_rows(HEADS - 1, 1)


def phase_output(nc, a, m, PS):
    with semaphores(nc, "output") as sem:
        s_bc, s_pad = sem("row_vectors_in"), sem("padding_rows_stored")
        s_bi, s_rw = sem("expert_biases_in"), sem("router_weights_in")
        s_x = [sem("x_in0"), sem("x_in1")]
        s_cd, s_ca = sem("out_chain_dve"), sem("out_chain_act")
        s_mv, s_mr = sem("mlstm_mean_square"), sem("mlstm_rstd_raw")
        s_at, s_cat = sem("attention_copied"), sem("mixed_tile_ready")
        s_tc, s_tca, s_tcd = sem("catT_in_psum"), sem("catT_lo_kept"), sem("catT_hi_kept")
        s_mm, s_x2 = sem("mixed_projected"), sem("residual_ready")
        s_ssq, s_xv, s_xr = sem("x2_square_sum"), sem("x2_variance"), sem("x2_rstd_raw")
        s_h2, s_th, s_tha, s_thd = sem("h2_ready"), sem("h2T_in_psum"), sem("h2T_lo_kept"), sem("h2T_hi_kept")
        s_lg, s_lgd = sem("logits_in_psum"), sem("logits_kept")
        s_sx, s_sh = [sem("x2_stored0"), sem("x2_stored1")], [sem("h2_stored0"), sem("h2_stored1")]
        s_z, s_ln = sem("zero_rows_set"), sem("x2_log_ready")

        items, end = m.run(m.after_w_out, [
            ("g1bc", [P, D], F32), ("s2bc", [P, D], F32), ("sh2bc", [P, D], F32), ("n2bc", [P, D], F32),
            ("rw", [P, KD, NE], F32)])
        w_out = m.w_out
        g1bc, s2bc, sh2bc, n2bc, rw = items
        assert end <= m.W
        items, end = m.run(m.W + 8 * TX * MH * MV, [
            ("cat0", [P, D], F32), ("cat1", [P, D], F32), ("catT0", [P, KD, P], F32), ("catT1", [P, KD, P], F32),
            ("ox0", [P, D], F32), ("ox1", [P, D], F32), ("x20", [P, D], F32), ("x21", [P, D], F32),
            ("h20", [P, D], F32), ("h21", [P, D], F32), ("h2T", [P, KD, P], F32), ("junk2", [P, D], F32),
            ("sq", [P, 512], F32), ("msv", [P, 4, 4], F32), ("xst", [P, 8], F32), ("sg", [P, 512], F32), ("msln", [P, 4], F32)])
        cat0, cat1, catT0, catT1, x0, x1, x20, x21, h20, h21, h2T, junk, sq, msv, xst, sg, msln = items
        cat, catT, xt, x2, h2 = (cat0, cat1), (catT0, catT1), (x0, x1), (x20, x21), (h20, h21)
        BC = (2 * FF + D) // TX
        (bias_f, m.bias3, m.logits, m.rbbc, bhi), end = m.run(end, [
            ("bias_f", [96, 2 * FF + D], F32), ("bias3", [96, 2 * FF + D], BF16), ("logits", [P, TX, NE], F32), ("rbbc", [P, NE], F32),
            ("bhi", [96, BC], BF16)])
        assert end <= 229344, end
        xsrc = a["x"].rearrange("b (t p) d -> (b t) p d", p=P)
        acc = a["acc"].rearrange("(t p) d -> t p d", p=P)
        h2d = a["h2"].rearrange("(t p) d -> t p d", p=P)

        def tiles(eng, body):
            body(0, 0, True, False)
            with eng.Fori(0, TX // 2 - 1) as i:
                for j in range(2):
                    body(2 * i + 1 + j, (1 + j) % 2, False, False)
            body(TX - 1, 1, False, True)

        with nc.Block() as block:
            @block.sync
            def _(sp):
                sp.dma_start(xt[0][:, :], xsrc[0]).then_inc(s_x[0], 16)
                for dst, row in ((g1bc, R_G1), (s2bc, R_SC2), (sh2bc, R_SH2)):
                    sp.dma_start(dst[:, :], a["mod"][0:1, row * P:row * P + D].to_broadcast([P, D])).then_inc(s_bc, 16)
                sp.dma_start(n2bc[:, :], a["norm2_g"].to_broadcast([P, D])).then_inc(s_bc, 16)
                sp.dma_start(m.rbbc[:, :], a["router_b"].to_broadcast([P, NE])).then_inc(s_bc, 16)
                sp.dma_start(rw[:, :, :], a["router_w"].rearrange("l (k p) n -> p (l k) n", p=P)).then_inc(s_rw, 16)
                sp.dma_start(xt[1][:, :], xsrc[1]).then_inc(s_x[1], 16)
                for g in range(3):
                    sp.dma_start(bias_f[32 * g:32 * g + 32, 0:2 * FF], a["b_gu"].rearrange("l e n -> (l e) n")).then_inc(s_bi, 16)
                    sp.dma_start(bias_f[32 * g:32 * g + 32, 2 * FF:], a["b_down"].rearrange("l e n -> (l e) n")).then_inc(s_bi, 16)
                sp.wait_ge(s_z, 1)
                sp.dma_start(acc[TX], junk[:, :]).then_inc(s_pad, 16)
                sp.dma_start(h2d[TX], junk[:, :]).then_inc(s_pad, 16)

                def tile(t, j, first, last):
                    sp.wait_ge(s_x2, t + 1)
                    sp.dma_start(acc[t], x2[j][:, :]).then_inc(s_sx[j], 16)
                    sp.wait_ge(s_h2, t + 1)
                    sp.dma_start(h2d[t], h2[j][:, :]).then_inc(s_sh[j], 16)
                tile(0, 0, True, False)
                with sp.Fori(0, TX // 2 - 1) as i:
                    for j in range(2):
                        t = 2 * i + 1 + j
                        sp.wait_ge(s_x2, t)
                        sp.dma_start(xt[j][:, :], xsrc[t + 1]).then_inc(s_x[j], 16)
                        tile(t, (1 + j) % 2, False, False)
                tile(TX - 1, 1, False, True)
                for j in range(2):
                    sp.wait_ge(s_sx[j], 16 * TX // 2)
                    sp.wait_ge(s_sh[j], 16 * TX // 2)

            @block.scalar
            def _(act):
                act.preload_act_table_set("natural_log_exp_and_others")

                def pre(t, j, first):
                    if not first:
                        act.wait_ge(s_tc, t)
                    act.activation(cat[j][:, 0:512], m.attn[:, t, :], ACT.Copy).then_inc(s_at, 1)
                    act.wait_ge(s_mv, t + 1)
                    act.activation(msln[:, :], msv[:, 0, :], ACT.Ln).then_inc(s_ca, 1)
                    act.wait_ge(s_ca, t + 1)
                    act.activation(msv[:, 1, :], msln[:, :], ACT.Exp, scale=-0.5).then_inc(s_mr, 1)

                def keep(t, j, first):
                    act.wait_ge(s_tc, t + 1)
                    act.activation(catT[j][:, 0:4, :], PS[:, 6, :].rearrange("p (k n) -> p k n", k=4), ACT.Copy).then_inc(s_tca, 1)

                def h2t(t):
                    act.wait_ge(s_th, t + 1)
                    act.activation(h2T[:, 0:4, :], PS[:, 4, :].rearrange("p (k n) -> p k n", k=4), ACT.Copy).then_inc(s_tha, 1)
                pre(0, 0, True)
                keep(0, 0, True)

                def tile(t, j, first, last):
                    if not last:
                        pre(t + 1, 1 - j, False)
                    if not first:
                        h2t(t - 1)
                    if not last:
                        keep(t + 1, 1 - j, False)
                    act.wait_ge(s_x2, t + 1)
                    act.activation(junk[:, :], x2[j][:, :], ACT.Square, accum_out=xst[:, 0:1]).then_inc(s_ssq, 1)
                    act.wait_ge(s_xv, t + 1)
                    act.activation(xst[:, 3:4], xst[:, 1:2], ACT.Ln).then_inc(s_ln, 1)
                    act.wait_ge(s_ln, t + 1)
                    act.activation(xst[:, 2:3], xst[:, 3:4], ACT.Exp, scale=-0.5).then_inc(s_xr, 1)
                act.wait_ge(s_pad, 32)
                tiles(act, tile)
                h2t(TX - 1)

            @block.vector
            def _(dve):
                dve.memset(junk[:, :], 0.0).then_inc(s_z, 1)
                base = 1
                A, B = 9, 13

                def newton(c, v, r, tmp):
                    c.done(dve.tensor_tensor(tmp, r, r, ALU.mult))
                    c.done(dve.tensor_tensor(tmp, tmp, v, ALU.mult))
                    c.done(dve.tensor_scalar(tmp, tmp, -0.5, 1.5, ALU.mult, ALU.add))
                    c.done(dve.tensor_tensor(r, r, tmp, ALU.mult))

                def pre(c, t, j, first):
                    h = m.hsum[:, t, :]
                    h3 = h.rearrange("p (h n) -> p h n", h=MH)
                    c.done(dve.tensor_tensor(sq[:, :], h, h, ALU.mult))
                    c.done(dve.tensor_reduce(msv[:, 2, :], sq[:, :].rearrange("p (h n) -> p h n", h=MH), AX.X, ALU.add))
                    dve.tensor_scalar(msv[:, 0, :], msv[:, 2, :], 1.0 / MV, EPS, ALU.mult, ALU.add).then_inc(s_mv, 1)
                    c.done(dve.tensor_scalar(sg[:, :], m.og[:, t, :], 1.0, None, ALU.add))
                    c.done(dve.reciprocal(sg[:, :], sg[:, :]))
                    dve.wait_ge(s_mr, t + 1)
                    newton(c, msv[:, 0, :], msv[:, 1, :], msv[:, 3, :])
                    r = msv[:, 1, :].rearrange("p (h o) -> p h o", o=1).to_broadcast([P, MH, MV])
                    c.done(dve.tensor_tensor(sq[:, :].rearrange("p (h n) -> p h n", h=MH), h3, r, ALU.mult))
                    if not first:
                        dve.wait_ge(s_tc, t)
                    dve.tensor_tensor(cat[j][:, 512:1024], sq[:, :], sg[:, :], ALU.mult).then_inc(s_cat, 1)

                def keep(t, j):
                    dve.wait_ge(s_tc, t + 1)
                    for k in range(4, KD):
                        ins = dve.tensor_scalar(catT[j][:, k, :], PS[:, 7, (k - 4) * P:(k - 3) * P], m.cols[:, R_MN + k - 4:R_MN + k - 3], None, ALU.mult)
                    ins.then_inc(s_tcd, 1)

                def h2t(t):
                    dve.wait_ge(s_th, t + 1)
                    dve.tensor_copy(h2T[:, 4:8, :], PS[:, 5, :].rearrange("p (k n) -> p k n", k=4)).then_inc(s_thd, 1)

                def logits(t):
                    dve.wait_ge(s_lg, t + 1)
                    dve.tensor_tensor(m.logits[:, t, :], PS[:, 4, 0:NE], m.rbbc[:, :], ALU.add).then_inc(s_lgd, 1)

                def residual(c, t, j, first):
                    dve.wait_ge(s_mm, t + 1)
                    dve.wait_ge(s_x[j], 8 * (t - j) + 16)
                    if not first:
                        dve.wait_ge(s_sx[j], 8 * (t - j))
                        dve.wait_ge(s_sh[j], 8 * (t - j))
                    ps = PS[:, 2 * j:2 * j + 2, :].rearrange("p b n -> p (b n)")
                    c.done(dve.tensor_tensor(x2[j][:, :], ps, g1bc[:, :], ALU.mult))
                    dve.tensor_tensor(x2[j][:, :], x2[j][:, :], xt[j][:, :], ALU.add).then_inc(s_x2, 1)
                    dve.wait_ge(s_ssq, t + 1)
                    dve.tensor_scalar(xst[:, 1:2], xst[:, 0:1], 1.0 / D, EPS, ALU.mult, ALU.add).then_inc(s_xv, 1)
                    dve.wait_ge(s_xr, t + 1)
                    newton(c, xst[:, 1:2], xst[:, 2:3], xst[:, 4:5])
                    c.done(dve.scalar_tensor_tensor(out=h2[j][:, :], in0=x2[j][:, :], scalar=xst[:, 2:3], in1=s2bc[:, :], op0=ALU.mult, op1=ALU.mult))
                    dve.tensor_tensor(h2[j][:, :], h2[j][:, :], sh2bc[:, :], ALU.add).then_inc(s_h2, 1)

                def biases(c, t):
                    cols = bass.ds(t * BC, BC)
                    c.done(dve.tensor_scalar(bhi[:, :], bias_f[:, cols], 1.0, None, ALU.mult))
                    c.done(dve.tensor_scalar(m.bias3[0:32, cols], bhi[0:32, :], 1.0, None, ALU.mult))
                    c.done(dve.tensor_tensor(bias_f[:, cols], bias_f[:, cols], bhi[:, :], ALU.subtract))
                    c.done(dve.tensor_scalar(bhi[:, :], bias_f[:, cols], 1.0, None, ALU.mult))
                    c.done(dve.tensor_scalar(m.bias3[32:64, cols], bhi[32:64, :], 1.0, None, ALU.mult))
                    c.done(dve.tensor_tensor(bias_f[:, cols], bias_f[:, cols], bhi[:, :], ALU.subtract))
                    c.done(dve.tensor_scalar(m.bias3[64:96, cols], bias_f[64:96, cols], 1.0, None, ALU.mult))
                pre(Chain(dve, s_cd), 0, 0, True)
                dve.wait_ge(s_bc, 80)
                Chain(dve, s_cd, A).done(dve.scalar_tensor_tensor(out=s2bc[:, :], in0=s2bc[:, :], scalar=1.0, in1=n2bc[:, :], op0=ALU.add, op1=ALU.mult))
                keep(0, 0)
                dve.wait_ge(s_bi, 96)

                def tile(t, j, first, last):
                    c = Chain(dve, s_cd, base + A + t * (A + B))
                    if not last:
                        pre(c, t + 1, 1 - j, False)
                    if not first:
                        h2t(t - 1)
                    if not last:
                        keep(t + 1, 1 - j)
                    residual(c, t, j, first)
                    if not first:
                        logits(t - 1)
                    biases(c, t)
                    assert c.n == (B if last else A + B), c.n
                tiles(dve, tile)
                h2t(TX - 1)
                logits(TX - 1)

            @block.tensor
            def _(pe):
                def cat_transposes(t, j, first):
                    pe.wait_ge(s_at, t + 1)
                    pe.wait_ge(s_cat, t + 1)
                    if not first:
                        pe.wait_ge(s_tcd, t)
                        pe.wait_ge(s_tca, t)
                    for k in range(KD):
                        tr = pe.transpose(PS[:, 6 + k // 4, (k % 4) * P:(k % 4 + 1) * P], cat[j][:, k * P:(k + 1) * P], m.ident[:, :])
                    tr.then_inc(s_tc, 1)

                def project(t, j, n):
                    for k in range(KD):
                        mm = pe.matmul(PS[:, 2 * j + n, :], catT[j][:, k, :], w_out[:, k, 512 * n:512 * n + 512], start=(k == 0), stop=(k == KD - 1))
                    return mm

                def h2_transposes(t, j):
                    pe.wait_ge(s_h2, t + 1)
                    pe.wait_ge(s_lgd, t + 1)
                    for k in range(KD):
                        tr = pe.transpose(PS[:, 4 + k // 4, (k % 4) * P:(k % 4 + 1) * P], h2[j][:, k * P:(k + 1) * P], m.ident[:, :])
                    tr.then_inc(s_th, 1)

                def logits(t):
                    pe.wait_ge(s_tha, t + 1)
                    pe.wait_ge(s_thd, t + 1)
                    for k in range(KD):
                        mm = pe.matmul(PS[:, 4, 0:NE], h2T[:, k, :], rw[:, k, :], start=(k == 0), stop=(k == KD - 1))
                    mm.then_inc(s_lg, 1)
                pe.sem_inc(s_lgd, 1)
                cat_transposes(0, 0, True)
                pe.wait_ge(s_rw, 16)

                def tile(t, j, first, last):
                    pe.wait_ge(s_tca, t + 1)
                    pe.wait_ge(s_tcd, t + 1)
                    if not first:
                        pe.wait_ge(s_x2, t)
                    project(t, j, 0)
                    project(t, j, 1).then_inc(s_mm, 1)
                    if not first:
                        h2_transposes(t - 1, 1 - j)
                    if not last:
                        cat_transposes(t + 1, 1 - j, False)
                    if not first:
                        logits(t - 1)
                tiles(pe, tile)
                h2_transposes(TX - 1, 1)
                logits(TX - 1)


NW = 12
NBLK = 64
GRID_W = 256


def expert_weights(a, m):
    w, end = m.run(SB0 + 4608, [(f"w{c}", [P, 2048], F32) for c in range(NW)])
    wv = [t.rearrange("p (k g n) -> p k g n", k=2, g=2) for t in w]
    gu_src = a["w_gu"].rearrange("l e (k p) (g j n) -> (l e) j p k g n", p=P, g=2, j=2)
    dn_src = a["w_down"].rearrange("l e (k p) (g n) -> (l e) p k g n", p=P, g=2)

    def load(sp, e, c, signal):
        for g in range(2):
            if c < 8:
                src = gu_src[e, c // 4][:, 2 * (c % 4):2 * (c % 4) + 2, g, :]
            else:
                src = dn_src[e][:, 2 * (c - 8):2 * (c - 8) + 2, g, :]
            sp.dma_start(wv[c][:, :, g, :], src).then_inc(signal, 16)
    return w, end, load


def phase_route(nc, a, m, PS):
    TK = TX * TOPK
    with semaphores(nc, "route") as sem:
        s_grid, s_cd, s_w0 = sem("index_constants_in"), sem("route_chain_dve"), sem("first_expert_in")
        s_top, s_exp = sem("top_logits_ready"), sem("gate_exps_ready")
        s_mask, s_cum = sem("mask_ready"), sem("ranks_in_psum")
        s_pair, s_tab = sem("pair_codes_ready"), sem("tables_in_psum")
        m.expert_w, after_w, m.load_weights = expert_weights(a, m)
        items, end = m.run(after_w, [
            ("grid", [P, GRID_W], F32), ("ones", [P, P], F32), ("upper", [P, P], F32),
            ("mx", [P, TX, 8], F32), ("ix", [P, TX, 8], U32), ("gt", [P, TX, TOPK], F32), ("gsum", [P, TX], F32),
            ("ixf", [P, TX, TOPK], F32), ("oh", [P, TK, NE], F32), ("ohc", [P, TK, NE], F32),
            ("mask", [P, TX, NE], F32), ("rank", [P, TX, NE], F32), ("tot", [P, TX + 1, NE], F32),
            ("nb", [P, NE], F32), ("b1", [P, NE], F32), ("b0", [P, NE], F32), ("code", [P, TK], F32),
            ("codei", [P, TK], I32), ("coli", [P, TK], I32), ("lanei", [P, TK], I32),
            ("colf", [P, TK], F32), ("lanef", [P, TK], F32),
            ("rowsel", [P, TK, P], F32), ("colsel", [P, TK, NBLK], F32), ("pairs", [P, TK, 2, NBLK], F32),
            ("cmp", [P, NBLK, NE], F32), ("blk", [P, NBLK], F32), ("tokf", [P, NBLK], F32), ("empty", [P, NBLK], F32),
            ("zeros", [P, NE], F32), ("used", [P, NE], F32)])
        (grid, ones, upper, mx, ix, gt, gsum, ixf, oh, ohc, mask, rank, tot, nb, b1, b0, code, codei, coli, lanei,
         colf, lanef, rowsel, colsel, pairs, cmp, blk, tokf, empty, zeros, used) = items
        assert end <= 198176
        (m.tokens, m.gates, m.table, m.esel), m.free = m.run(205472, [
            ("tokens", [P, NBLK], I32), ("gates", [P, NBLK], F32), ("table", [P, NBLK + NE + 1], I32), ("esel", [96, NBLK], BF16)])
        iota = grid[:, 0:P]
        tok1, pmod, pad1, lane = grid[:, P:P + TX], grid[:, 136:137], grid[:, 137:138], grid[:, 138:139]

        with nc.Block() as block:
            @block.sync
            def _(sp):
                sp.dma_start(grid[:, :], a["grid"]).then_inc(s_grid, 16)
                for c in range(NW):
                    m.load_weights(sp, 0, c, s_w0)
                sp.wait_ge(s_grid, 16)
                sp.wait_ge(s_w0, NW * 32)

            @block.scalar
            def _(act):
                act.wait_ge(s_top, 1)
                act.activation(gt[:, :, :], gt[:, :, :], ACT.Exp).then_inc(s_exp, 1)

            @block.tensor
            def _(pe):
                pe.wait_ge(s_mask, 1)
                pe.matmul(PS[:, 0, 0:TX * NE], upper[:, :], mask[:, :, :], start=True, stop=True)
                pe.matmul(PS[:, 1, 0:TX * NE], ones[:, :], mask[:, :, :], start=True, stop=True).then_inc(s_cum, 1)
                pe.wait_ge(s_pair, 1)
                for j in range(TK):
                    mm = pe.matmul(PS[:, 2, 0:2 * NBLK], rowsel[:, j, :], pairs[:, j, :, :], start=(j == 0), stop=(j == TK - 1))
                mm.then_inc(s_tab, 1)

            @block.vector
            def _(dve):
                chain = Chain(dve, s_cd)

                def bc(ap, shape):
                    return ap.to_broadcast(shape)
                for t in range(TX):
                    ins = dve.max(out=mx[:, t, :], in_=m.logits[:, t, :])
                chain.done(ins)
                for t in range(TX):
                    ins = dve.max_index(out=ix[:, t, :], in_max=mx[:, t, :], in_values=m.logits[:, t, :])
                chain.done(ins)
                dve.tensor_tensor(gt[:, :, :], mx[:, :, 0:TOPK], bc(mx[:, :, 0:1], [P, TX, TOPK]), ALU.subtract).then_inc(s_top, 1)
                chain.done(dve.tensor_copy(ixf[:, :, :], ix[:, :, 0:TOPK]))
                dve.wait_ge(s_grid, 16)
                dve.memset(ones[:, :], 1.0)
                dve.tensor_scalar(upper[:, :], iota, lane, None, ALU.is_gt)
                chain.done(dve.tensor_tensor(oh[:, :, :], bc(grid[:, 0:NE].unsqueeze(1), [P, TK, NE]),
                                             bc(ixf.rearrange("p t k -> p (t k)").unsqueeze(2), [P, TK, NE]), ALU.is_equal))
                dve.tensor_reduce(mask[:, :, :], oh.rearrange("p (t k) e -> p t e k", k=TOPK), AX.X, ALU.add).then_inc(s_mask, 1)
                dve.wait_ge(s_exp, 1)
                chain.done(dve.tensor_reduce(gsum[:, :], gt[:, :, :], AX.X, ALU.add))
                chain.done(dve.reciprocal(gsum[:, :], gsum[:, :]))
                chain.done(dve.tensor_tensor(gt[:, :, :], gt[:, :, :], bc(gsum[:, :].unsqueeze(2), [P, TX, TOPK]), ALU.mult))
                dve.wait_ge(s_cum, 1)
                dve.memset(zeros[:, :], 0.0)
                chain.done(dve.memset(tot[:, 0, :], 0.0))
                for t in range(TX):
                    chain.done(dve.tensor_tensor(tot[:, t + 1, :], tot[:, t, :], PS[:, 1, t * NE:(t + 1) * NE], ALU.add))
                chain.done(dve.memset(nb[:, :], 1.0))
                for j in range(1, SEQ // P):
                    chain.done(dve.scalar_tensor_tensor(out=nb[:, :], in0=tot[:, TX, :], scalar=float(P * j), in1=nb[:, :],
                                                        op0=ALU.is_gt, op1=ALU.add))
                chain.done(dve.tensor_tensor_scan(b1[:, :], nb[:, :], zeros[:, :], 0.0, ALU.add, ALU.add))
                chain.done(dve.tensor_tensor(b0[:, :], b1[:, :], nb[:, :], ALU.subtract))
                chain.done(dve.tensor_tensor(rank[:, :, :], PS[:, 0, 0:TX * NE].rearrange("p (t e) -> p t e", e=NE),
                                             tot[:, 0:TX, :], ALU.add))
                for t in range(TX):
                    ins = dve.scalar_tensor_tensor(out=rank[:, t, :], in0=b0[:, :], scalar=float(P), in1=rank[:, t, :],
                                                   op0=ALU.mult, op1=ALU.add)
                chain.done(ins)
                for t in range(TX):
                    ins = dve.tensor_tensor(ohc[:, TOPK * t:TOPK * t + TOPK, :], oh[:, TOPK * t:TOPK * t + TOPK, :],
                                            bc(rank[:, t:t + 1, :], [P, TOPK, NE]), ALU.mult)
                chain.done(ins)
                chain.done(dve.tensor_reduce(code[:, :], ohc[:, :, :], AX.X, ALU.add))
                chain.done(dve.tensor_copy(codei[:, :], code[:, :]))
                dve.tensor_scalar(coli[:, :], codei[:, :], 7, None, ALU.arith_shift_right)
                chain.done(dve.tensor_scalar(lanei[:, :], codei[:, :], P - 1, None, ALU.bitwise_and))
                dve.tensor_copy(colf[:, :], coli[:, :])
                chain.done(dve.tensor_copy(lanef[:, :], lanei[:, :]))
                dve.tensor_tensor(rowsel[:, :, :], bc(iota.unsqueeze(1), [P, TK, P]), bc(lanef[:, :].unsqueeze(2), [P, TK, P]), ALU.is_equal)
                chain.done(dve.tensor_tensor(colsel[:, :, :], bc(grid[:, 0:NBLK].unsqueeze(1), [P, TK, NBLK]),
                                             bc(colf[:, :].unsqueeze(2), [P, TK, NBLK]), ALU.is_equal))
                for t in range(TX):
                    dve.tensor_scalar(pairs[:, TOPK * t:TOPK * t + TOPK, 0, :], colsel[:, TOPK * t:TOPK * t + TOPK, :],
                                      tok1[:, t:t + 1], None, ALU.mult)
                chain.done(dve.tensor_tensor(pairs[:, :, 1, :], colsel[:, :, :],
                                             bc(gt.rearrange("p t k -> p (t k)").unsqueeze(2), [P, TK, NBLK]), ALU.mult))
                dve.sem_inc(s_pair, 1)
                chain.done(dve.tensor_tensor(cmp[:, :, :], bc(grid[:, 0:NBLK].unsqueeze(2), [P, NBLK, NE]),
                                             bc(b1[:, :].unsqueeze(1), [P, NBLK, NE]), ALU.is_ge))
                chain.done(dve.tensor_reduce(blk[:, :], cmp[:, :, :], AX.X, ALU.add))
                chain.done(dve.tensor_scalar(blk[:, :], blk[:, :], float(NE - 1), None, ALU.min))
                chain.done(dve.tensor_scalar(used[:, :], b0[:, :], float(NW), float(-NW), ALU.mult, ALU.add))
                chain.done(dve.tensor_scalar(used[:, :], used[:, :], 0.0, None, ALU.max))
                dve.tensor_copy(m.table[:, 0:NBLK], blk[:, :])
                dve.tensor_copy(m.table[:, NBLK:NBLK + NE], used[:, :])
                dve.tensor_copy(m.table[:, NBLK + NE:NBLK + NE + 1], b1[:, NE - 1:NE])
                dve.tensor_scalar(m.esel[:, :], blk[0:96, :], pmod[0:96, :], None, ALU.is_equal)
                dve.wait_ge(s_tab, 1)
                dve.tensor_copy(m.gates[:, :], PS[:, 2, NBLK:2 * NBLK])
                chain.done(dve.tensor_scalar(empty[:, :], PS[:, 2, 0:NBLK], 0.0, None, ALU.is_equal))
                chain.done(dve.scalar_tensor_tensor(out=tokf[:, :], in0=empty[:, :], scalar=pad1, in1=PS[:, 2, 0:NBLK],
                                                    op0=ALU.mult, op1=ALU.add))
                chain.done(dve.tensor_scalar(m.tokens[:, :], tokf[:, :], -1.0, None, ALU.add))


def phase_experts(nc, a, m, PS):
    H = FF // 2
    SLOTS = 4
    ALPHA = 1.702
    G0, DN, TR = 0, 4, 6
    nc.clear_and_free_semaphores(RELEASED)
    nc.all_engine_barrier()
    RELEASED.clear()
    with semaphores(nc, "experts") as sem:
        s_w = [sem(f"weights_in{c}") for c in range(NW)]
        s_hi, s_lo, s_used, s_gb = sem("chunk_hi_ready"), sem("chunk_lo_ready"), sem("chunks_used"), sem("g2_rows_in")
        s_xg, s_sc = sem("rows_gathered"), sem("rows_added")
        s_step, s_yf, s_pc, s_cd = sem("indirect_dma_may_start"), sem("y_free"), sem("index_copied"), sem("expert_chain_dve")
        s_sel, s_g, s_sg = sem("selector_ready"), sem("gate_clamped"), sem("silu_ready")
        s_h, s_tp, s_eh, s_el = sem("hidden_ready"), sem("transposed"), sem("transpose_hi_kept"), sem("transpose_lo_kept")
        s_bias, s_y = sem("selector_used"), sem("y_ready")
        w = m.expert_w
        items, end = m.run(SB0 + 4608 + NW * 8192, [(f"wh{c}", [P, 2048], F32R) for c in range(SLOTS)] + [(f"wl{c}", [P, 2048], F32R) for c in range(SLOTS)]
                           + [("xTh", [P, KD, P], F32R), ("xTl", [P, KD, P], F32R), ("hTh", [P, FF // P, P], F32R),
                              ("idxg", [P, 1], I32), ("idxs", [P, 1], I32), ("gcol", [P, 1], F32), ("sel", [96, P], BF16)])
        wh, wl = items[:SLOTS], items[SLOTS:2 * SLOTS]
        xTh, xTl, hTh, idxg, idxs, gcol, sel = items[2 * SLOTS:]
        assert end <= 198176
        (hTl, xg, hid, gc, sgm, g2bc), end = m.run(m.free, [
            ("hTl", [P, FF // P, P], F32R), ("xg", [P, D], F32), ("hid", [P, FF], F32), ("gc", [P, H], F32), ("sgm", [P, H], F32),
            ("g2bc", [P, D], F32)])
        assert end <= 229344
        y = hid
        xT, hT = (xTh, xTl), (hTh, hTl)
        whv, wlv = ([s.rearrange("p (k g n) -> p k g n", k=2, g=2) for s in ws] for ws in (wh, wl))
        T_B, T_N = NBLK, NBLK + NE

        def count(eng):
            return eng.value_load(m.table[0:1, T_N:T_N + 1], min_val=NE, max_val=NBLK - 1)

        def expert(eng, i):
            return eng.value_load(m.table[0:1, bass.ds(i, 1)], min_val=0, max_val=NE - 1)

        def bank4(half):
            return PS[:, TR + half, :].rearrange("p (q n) -> p q n", q=4)

        with nc.Block() as block:
            @block.sync
            def _(sp):
                sp.dma_start(g2bc[:, :], a["mod"][0:1, R_G2 * P:R_G2 * P + D].to_broadcast([P, D])).then_inc(s_gb, 16)
                for c in range(NW):
                    sp.sem_inc(s_w[c], 32)
                with sp.Fori(1, NE) as e:
                    used = sp.value_load(m.table[0:1, bass.ds(e + T_B, 1)], min_val=0, max_val=NW * (NBLK - 2))
                    for c in range(NW):
                        sp.wait_ge(s_lo, used + (c + 1))
                        m.load_weights(sp, e, c, s_w[c])
                sp.wait_ge(s_gb, 16)

            @block.gpsimd
            def _(pool):
                n = count(pool)

                def gather():
                    pool.indirect_dma_start(out=xg[:, :], out_offset=None, in_=a["h2"],
                                            in_offset=bass.IndirectOffsetOnAxis(ap=idxg[:, 0:1], axis=0)).then_inc(s_xg, 16)
                pool.sem_inc(s_yf, 1)
                pool.tensor_copy(idxg[:, :], m.tokens[:, 0:1]).then_inc(s_pc, 1)
                pool.wait_ge(s_pc, 1)
                gather()
                with pool.Fori(0, n) as i:
                    pool.wait_ge(s_tp, 4 * i + 2)
                    pool.tensor_copy(idxg[:, :], m.tokens[:, bass.ds(i + 1, 1)]).then_inc(s_pc, 1)
                    pool.tensor_copy(idxs[:, :], m.tokens[:, bass.ds(i, 1)]).then_inc(s_pc, 1)
                    pool.wait_ge(s_pc, 2 * i + 3)
                    pool.sem_inc(s_step, 1)
                    gather()
                    pool.wait_ge(s_y, i + 2)
                    pool.sem_inc(s_step, 1)
                    pool.indirect_dma_start(out=a["acc"], out_offset=bass.IndirectOffsetOnAxis(ap=idxs[:, 0:1], axis=0),
                                            in_=y[:, :], in_offset=None, compute_op=ALU.add).then_inc(s_sc, 16)
                    pool.wait_ge(s_sc, 16 * i + 16)
                    pool.sem_inc(s_yf, 1)
                pool.wait_ge(s_xg, n * 16 + 16)

            @block.tensor
            def _(pe):
                n = count(pe)

                def transposes(src, half):
                    for q in range(4):
                        k = 4 * half + q
                        ins = pe.transpose(PS[:, TR + half, q * P:(q + 1) * P], src[:, k * P:(k + 1) * P], m.ident[:, :])
                    ins.then_inc(s_tp, 1)

                def product(bank, xs, k, slot, kk, last):
                    for op, ws in ((xs[0], whv), (xs[0], wlv), (xs[1], whv)):
                        for g in range(2):
                            mm = pe.matmul(PS[:, bank + g, :], op[:, k, :], ws[slot][:, kk, g, :], start=False,
                                           stop=(last and op is xs[1]))
                    return mm
                pe.wait_ge(s_xg, 16)
                transposes(xg, 0)
                transposes(xg, 1)
                with pe.Fori(0, n) as i:
                    pe.wait_ge(s_sel, i + 1)

                    def bias(bank, col):
                        return pe.matmul(PS[:, bank, :], sel[:, :], m.bias3[:, col:col + 512], start=True, stop=False)

                    def step(c, kk):
                        if kk == 0:
                            pe.wait_ge(s_lo, i * NW + (c + 1))
                        if c < 8:
                            mm = product(G0 + 2 * (c // 4), xT, 2 * (c % 4) + kk, c % SLOTS, kk, c % 4 == 3 and kk == 1)
                        else:
                            mm = product(DN, hT, 2 * (c - 8) + kk, c % SLOTS, kk, c == NW - 1 and kk == 1)
                        if kk == 1:
                            mm.then_inc(s_used, 1)

                    def chunk(c):
                        step(c, 0)
                        step(c, 1)
                    bias(G0, 0)
                    bias(G0 + 1, FF)
                    pe.wait_ge(s_el, 4 * i + 1)
                    step(0, 0)
                    step(0, 1)
                    step(1, 0)
                    step(1, 1)
                    pe.wait_ge(s_el, 4 * i + 2)
                    step(2, 0)
                    step(2, 1)
                    step(3, 0)
                    step(3, 1)
                    bias(G0 + 2, H)
                    bias(G0 + 3, FF + H)
                    step(4, 0)
                    step(4, 1)
                    step(5, 0)
                    step(5, 1)
                    step(6, 0)
                    step(6, 1)
                    pe.wait_ge(s_h, 2 * i + 1)
                    transposes(hid, 0)
                    step(7, 0)
                    step(7, 1)
                    pe.wait_ge(s_y, i + 1)
                    bias(DN, 2 * FF)
                    bias(DN + 1, 2 * FF + 512).then_inc(s_bias, 1)
                    pe.wait_ge(s_el, 4 * i + 3)
                    step(8, 0)
                    step(8, 1)
                    pe.wait_ge(s_h, 2 * i + 2)
                    transposes(hid, 1)
                    step(9, 0)
                    step(9, 1)
                    pe.wait_ge(s_xg, 16 * i + 32)
                    transposes(xg, 0)
                    pe.wait_ge(s_el, 4 * i + 4)
                    step(10, 0)
                    step(10, 1)
                    step(11, 0)
                    transposes(xg, 1)
                    step(11, 1)

            @block.scalar
            def _(act):
                n = count(act)
                act.preload_act_table_set("silu_and_others")

                def keep(dst, half, which, scale=1.0):
                    act.wait_ge(s_tp, which)
                    act.activation(dst[0][:, 4 * half:4 * half + 4, :], bank4(half), ACT.Copy, scale=scale).then_inc(s_eh, 1)

                def split(c, e, used):
                    act.wait_ge(s_w[c], e * 32 + 32)
                    if used is not None:
                        act.wait_ge(s_used, used)
                    act.activation(wh[c % SLOTS][:, :], w[c][:, :], ACT.Copy).then_inc(s_hi, 1)
                keep(xT, 0, 1)
                keep(xT, 1, 2)
                for c in range(SLOTS):
                    split(c, 0, None)
                with act.Fori(0, n) as i:
                    e = expert(act, i)
                    e1 = expert(act, i + 1)

                    def this(*cs):
                        for c in cs:
                            split(c, e, i * NW + (c + 1 - SLOTS))

                    def following(c):
                        split(c, e1, i * NW + (c + 1 + NW - SLOTS))

                    def silu(j):
                        act.wait_ge(s_g, 2 * i + (j + 1))
                        act.activation(sgm[:, :], gc[:, :], ACT.Silu).then_inc(s_sg, 1)
                    this(4)
                    this(5)
                    this(6)
                    this(7)
                    silu(0)
                    this(8)
                    this(9)
                    keep(hT, 0, 4 * i + 3, 1.0 / ALPHA)
                    this(10)
                    silu(1)
                    this(11)
                    keep(hT, 1, 4 * i + 4, 1.0 / ALPHA)
                    following(0)
                    keep(xT, 0, 4 * i + 5)
                    following(1)
                    following(2)
                    keep(xT, 1, 4 * i + 6)
                    following(3)

            @block.vector
            def _(dve):
                n = count(dve)

                def keep(dst, half, which, scale=1.0):
                    dve.wait_ge(s_eh, which)
                    dve.scalar_tensor_tensor(out=dst[1][:, 4 * half:4 * half + 4, :], in0=bank4(half), scalar=scale,
                                             in1=dst[0][:, 4 * half:4 * half + 4, :].bitcast(F32), op0=ALU.mult,
                                             op1=ALU.subtract).then_inc(s_el, 1)

                def split(c, done):
                    dve.wait_ge(s_hi, done)
                    dve.tensor_tensor(wl[c % SLOTS][:, :], w[c % NW][:, :], wh[c % SLOTS][:, :].bitcast(F32), ALU.subtract).then_inc(s_lo, 1)
                dve.sem_inc(s_y, 1)
                dve.tensor_copy(sel[:, :], m.esel[:, 0:1].to_broadcast([96, P])).then_inc(s_sel, 1)
                keep(xT, 0, 1)
                keep(xT, 1, 2)
                for c in range(SLOTS):
                    split(c, c + 1)
                dve.wait_ge(s_gb, 16)
                with dve.Fori(0, n) as i:
                    chain = Chain(dve, s_cd, 3 * i)

                    def this(*cs):
                        for c in cs:
                            split(c, i * NW + (c + 1))

                    def hidden(j):
                        dve.wait_ge(s_used, i * NW + (4 * j + 4))
                        dve.tensor_scalar(gc[:, :], PS[:, G0 + 2 * j, :], 7.0, ALPHA, ALU.min, ALU.mult).then_inc(s_g, 1)
                        hj = hid[:, j * H:(j + 1) * H]
                        if j == 0:
                            dve.wait_ge(s_yf, i + 1)
                        chain.done(dve.tensor_scalar(hj, PS[:, G0 + 2 * j + 1, :], 7.0, -7.0, ALU.min, ALU.max))
                        dve.wait_ge(s_sg, 2 * i + (j + 1))
                        dve.scalar_tensor_tensor(out=hj, in0=hj, scalar=1.0, in1=sgm[:, :], op0=ALU.add, op1=ALU.mult).then_inc(s_h, 1)
                    this(4)
                    this(5)
                    this(6)
                    hidden(0)
                    this(7)
                    this(8)
                    this(9)
                    keep(hT, 0, 4 * i + 3, 1.0 / ALPHA)
                    hidden(1)
                    dve.wait_ge(s_bias, i + 1)
                    dve.tensor_copy(sel[:, :], m.esel[:, bass.ds(i + 1, 1)].to_broadcast([96, P])).then_inc(s_sel, 1)
                    chain.done(dve.tensor_copy(gcol[:, :], m.gates[:, bass.ds(i, 1)]))
                    this(10)
                    keep(hT, 1, 4 * i + 4, 1.0 / ALPHA)
                    this(11)
                    this(12)
                    keep(xT, 0, 4 * i + 5)
                    this(13)
                    keep(xT, 1, 4 * i + 6)
                    dve.wait_ge(s_used, i * NW + NW)
                    dve.scalar_tensor_tensor(out=y.rearrange("p (g n) -> p g n", g=2), in0=PS[:, DN:DN + 2, :], scalar=gcol[:, :],
                                             in1=g2bc.rearrange("p (g n) -> p g n", g=2), op0=ALU.mult, op1=ALU.mult).then_inc(s_y, 1)
                    this(14)
                    this(15)


def phase_final(nc, a, m, PS):
    with semaphores(nc, "final") as sem:
        s_in, s_g, s_out = [sem(f"rows_in{g}") for g in range(4)], sem("final_gain_in"), [sem(f"out_stored{g}") for g in range(4)]
        s_ss, s_v, s_r, s_cd, s_o = sem("square_sum"), sem("variance"), sem("rstd_raw"), sem("final_chain"), sem("out_ready")
        s_ln = sem("log_ready")
        items, end = m.run(SB0 + 4608, [
            ("rows", [P, TX, D], F32), ("outs", [P, TX, D], F32), ("fgain", [P, D], F32), ("sqj", [P, D], F32),
            ("ss", [P, TX], F32), ("var", [P, TX], F32), ("rs", [P, TX], F32), ("rt", [P, TX], F32), ("lg", [P, TX], F32)])
        rows, outs, fgain, sqj, ss, var, rs, rt, lg = items
        NG = 4
        W = TX // NG
        src = a["acc"][0:SEQ, :].rearrange("(g t p) d -> g p t d", p=P, t=W)
        dst = a["out"].rearrange("b (g t p) d -> (b g) p t d", p=P, t=W)
        with nc.Block() as block:
            @block.sync
            def _(sp):
                for g in range(NG):
                    sp.dma_start(rows[:, W * g:W * g + W, :], src[g]).then_inc(s_in[g], 16)
                sp.dma_start(fgain[:, :], a["final_norm_g"].unsqueeze(0).to_broadcast([P, D])).then_inc(s_g, 16)
                for g in range(NG):
                    sp.wait_ge(s_o, W * (g + 1))
                    sp.dma_start(dst[g], outs[:, W * g:W * g + W, :]).then_inc(s_out[g], 16)
                for g in range(NG):
                    sp.wait_ge(s_out[g], 16)

            @block.scalar
            def _(act):
                act.preload_act_table_set("natural_log_exp_and_others")

                def squares(g):
                    act.wait_ge(s_in[g], 16)
                    for t in range(W * g, W * g + W):
                        act.activation(sqj[:, :], rows[:, t, :], ACT.Square, accum_out=ss[:, t:t + 1]).then_inc(s_ss, 1)
                        act.wait_ge(s_ss, t + 1)

                def rstd(g):
                    cols = slice(W * g, W * g + W)
                    act.wait_ge(s_v, g + 1)
                    act.activation(lg[:, cols], var[:, cols], ACT.Ln).then_inc(s_ln, 1)
                    act.wait_ge(s_ln, g + 1)
                    act.activation(rs[:, cols], lg[:, cols], ACT.Exp, scale=-0.5).then_inc(s_r, 1)
                for g in range(NG):
                    squares(g)
                    rstd(g)

            @block.vector
            def _(dve):
                chain = Chain(dve, s_cd)
                for g in range(NG):
                    cols = slice(W * g, W * g + W)
                    dve.wait_ge(s_ss, W * (g + 1))
                    dve.tensor_scalar(var[:, cols], ss[:, cols], 1.0 / D, EPS, ALU.mult, ALU.add).then_inc(s_v, 1)
                    dve.wait_ge(s_r, g + 1)
                    chain.done(dve.tensor_tensor(rt[:, cols], rs[:, cols], rs[:, cols], ALU.mult))
                    chain.done(dve.tensor_tensor(rt[:, cols], rt[:, cols], var[:, cols], ALU.mult))
                    chain.done(dve.tensor_scalar(rt[:, cols], rt[:, cols], -0.5, 1.5, ALU.mult, ALU.add))
                    chain.done(dve.tensor_tensor(rs[:, cols], rs[:, cols], rt[:, cols], ALU.mult))
                    if g == 0:
                        dve.wait_ge(s_g, 16)
                    for t in range(W * g, W * g + W):
                        dve.scalar_tensor_tensor(out=outs[:, t, :], in0=rows[:, t, :], scalar=rs[:, t:t + 1], in1=fgain[:, :],
                                                 op0=ALU.mult, op1=ALU.mult).then_inc(s_o, 1)


SB0 = 16512


def build_program(nc, a):
    m = Memory(nc)
    RELEASED.clear()
    a["mod"] = nc.dram_tensor("mod_dram", (2, 6 * D), F32).ap()
    a["acc"] = nc.dram_tensor("acc_dram", (SEQ + P, D), F32).ap()
    a["h2"] = nc.dram_tensor("h2_dram", (SEQ + P, D), F32).ap()
    (m.ident, m.cols, m.s1x, m.s1c, m.s2, m.eps, m.bgates, m.cs_tab, m.sn_tab), end = m.run(SB0, [
        ("ident", [P, P], F32), ("cols", [P, N_COLS], F32), ("s1x", [P, KD], F32), ("s1c", [P, KD], F32),
        ("s2", [P, KD], F32), ("eps", [P, 1], F32), ("bgates", [P, 16], F32),
        ("cs_tab", [P, NT, ROPE], F32), ("sn_tab", [P, NT, ROPE], F32)])
    (m.og, m.vaug, m.mk, m.mqT, m.cqT, m.ckvT, m.g16), end = m.run(SB0 + 4608, [
        ("og", [P, TX, MH * MV], F32), ("vaug", [P, NT, MH, MV + 1], F32), ("mk", [P, NT, MH * MQK], F32),
        ("mqT", [P, 2, SEQ], F32), ("cqT", [P, QL // P, SEQ], F32), ("ckvT", [P, KVL // P, KEYS], F32),
        ("g16", [P, NT, 4 * MH], F32)])
    m.W = end
    (m.w_in,), m.R1 = m.run(end, [("w_in", [P, KD, IN_W], F32)])
    m.kT0 = m.at("kT0", [NOPE + ROPE, KEYS], F32, m.R1 + 32768)
    with nc.psum_tensor("PS", [P, 8, 512], F32) as PS:
        for phase in PHASES:
            phase(nc, a, m, PS)
PHASES = [phase_modulation, phase_projection, phase_mlstm, phase_attention, phase_output, phase_route, phase_experts, phase_final]


def rope_tables():
    t = np.arange(SEQ)
    row, col = (t // 64).astype(np.float32), (t % 64).astype(np.float32)
    pairs = ROPE // 4
    inv = (np.float32(10000.0) ** (-np.arange(pairs, dtype=np.float32) / np.float32(pairs))).astype(np.float32)
    ang = np.concatenate([row[:, None] * inv, col[:, None] * inv], axis=-1)
    cos, sin = np.cos(ang).astype(np.float32), np.sin(ang).astype(np.float32)
    cs = np.concatenate([np.ones((CTX, ROPE), np.float32), np.concatenate([cos, cos], 1)])
    sn = np.concatenate([np.zeros((CTX, ROPE), np.float32), np.concatenate([-sin, sin], 1)])
    csT = np.ascontiguousarray(np.concatenate([cos, cos], 1).T * np.float32(SCALE))
    snT = np.ascontiguousarray(np.concatenate([-sin, sin], 1).T * np.float32(SCALE))
    return cs, sn, csT, snT


def index_constants():
    grid = np.zeros((P, GRID_W), np.float32)
    lane = np.arange(P, dtype=np.float32)
    grid[:, 0:P] = lane[None, :]
    grid[:, P:P + TX] = 1 + lane[:, None] + P * np.arange(TX, dtype=np.float32)[None, :]
    grid[:, P + TX], grid[:, P + TX + 1], grid[:, P + TX + 2] = lane % NE, SEQ + 1 + lane, lane
    return grid


_INS = ["x", "c", "ctx", "c_ctx", "w_mod", "b_mod", "norm1_g", "w_in", "b_gates", "q_norm_g", "w_uq", "kv_norm_g",
        "w_ukv", "m_norm_g", "w_out", "norm2_g", "router_w", "router_b", "w_gu", "b_gu", "w_down", "b_down",
        "final_norm_g"]


def kernel(**inputs):
    import numpy as _np
    import concourse.bacc as _bacc
    from concourse import mybir as _mybir
    from concourse.bass_utils import run_bass_kernel_spmd as _run

    nc = _bacc.Bacc("TRN2", target_bir_lowering=False, num_devices=1)
    arrays, aps = {}, {}
    given = {n: _np.ascontiguousarray(inputs[n]) for n in _INS}
    given.update(zip(("cs_tab", "sn_tab", "cs_tabT", "sn_tabT"), rope_tables()))
    given["grid"] = index_constants()
    for name, v in given.items():
        arrays[f"in_{name}_dram"] = v
        aps[name] = nc.dram_tensor(f"in_{name}_dram", v.shape, _mybir.dt.from_np(v.dtype), kind="ExternalInput").ap()
    aps["out"] = nc.dram_tensor("out_0_dram", (1, SEQ, D), F32, kind="ExternalOutput").ap()
    build_program(nc, aps)
    r = _run(nc, [arrays], core_ids=[0])
    return r.results[0]["out_0_dram"]
```
